# Optimizing a Trainium2 kernel written in Bass

```python
import math
import jax, jax.numpy as jnp
from jax import lax
import numpy as np

D_MODEL = 1024
BATCH = 1
SEQ = 256
DEPTH = 1

GLA_HEADS = 4
GLA_DK = 64
GLA_DV = 128
GLA_LOWRANK = 16
GLA_TAU = 16.0
GLA_CHUNK = 64
MOBA_HEADS = 8
MOBA_DH = 64
MOBA_BLOCK = 256
MOBA_TOPK = 3
MOBA_QCHUNK = 128
REL_BUCKETS = 32
REL_MAX_DIST = 128
MEM_LEN = 256
MEM_HEADS = 4
MEM_DH = 128
N_GROUPS = 4
EXPERTS_PER_GROUP = 8
N_EXPERTS = N_GROUPS * EXPERTS_PER_GROUP
TOPK_IN_GROUP = 2
D_EXPERT = 512
MOE_BLOCK = 128
EPS = 1e-6

GLA_QK = GLA_HEADS * GLA_DK
GLA_V = GLA_HEADS * GLA_DV
MOBA_W = MOBA_HEADS * MOBA_DH
MEM_W = MEM_HEADS * MEM_DH
IN_SPLITS = (GLA_QK, GLA_QK, GLA_V, GLA_V, GLA_LOWRANK, MOBA_W, MOBA_W, MOBA_W, D_MODEL, D_MODEL)
D_IN = sum(IN_SPLITS)
SPLIT_POINTS = tuple(sum(IN_SPLITS[:i + 1]) for i in range(len(IN_SPLITS) - 1))


def rmsnorm(x, g):
    xf = x.astype(jnp.float32)
    y = xf * lax.rsqrt(jnp.mean(xf * xf, axis=-1, keepdims=True) + EPS)
    return (y * g.astype(jnp.float32)).astype(x.dtype)

def gla_chunked(q, k, v, log_a):
    B, S = q.shape[0], q.shape[1]
    C = GLA_CHUNK
    N = S // C

    def chunks(t):
        return t.astype(jnp.float32).reshape(B, N, C, GLA_HEADS, t.shape[-1]).transpose(0, 3, 1, 2, 4)

    q, k, v, log_a = chunks(q) * (GLA_DK ** -0.5), chunks(k), chunks(v), chunks(log_a)
    b = jnp.cumsum(log_a, axis=3)
    b_last = b[:, :, :, C - 1:]
    b_mid = b[:, :, :, C // 2 - 1:C // 2]
    att = jnp.einsum('bhncd,bhnsd->bhncs', q * jnp.exp(b - b_mid), k * jnp.exp(b_mid - b))
    causal = jnp.tril(jnp.ones((C, C), dtype=bool))
    att = jnp.where(causal, att, 0.0)
    o_intra = jnp.einsum('bhncs,bhnsv->bhncv', att, v)
    kv = jnp.einsum('bhncd,bhncv->bhndv', k * jnp.exp(b_last - b), v)
    decay = jnp.exp(b_last[:, :, :, 0])

    def step(state, inp):
        dec, kv_c = inp
        return dec[..., None] * state + kv_c, state

    init = jnp.zeros((B, GLA_HEADS, GLA_DK, GLA_DV), jnp.float32)
    _, states = lax.scan(step, init, (jnp.moveaxis(decay, 2, 0), jnp.moveaxis(kv, 2, 0)))
    states = jnp.moveaxis(states, 0, 2)
    o_inter = jnp.einsum('bhncd,bhndv->bhncv', q * jnp.exp(b), states)
    o = o_intra + o_inter
    return o.transpose(0, 2, 3, 1, 4).reshape(B, S, GLA_HEADS, GLA_DV)

def t5_bucket(dist):
    n = jnp.maximum(dist, 0)
    max_exact = REL_BUCKETS // 2
    nf = jnp.maximum(n, 1).astype(jnp.float32)
    large = max_exact + (jnp.log(nf / max_exact) / math.log(REL_MAX_DIST / max_exact)
                         * (REL_BUCKETS - max_exact)).astype(jnp.int32)
    large = jnp.minimum(large, REL_BUCKETS - 1)
    return jnp.where(n < max_exact, n, large)

def moba_attention(q, k, v, rel_bias):
    B, S = q.shape[0], q.shape[1]
    H, BS, QC = MOBA_HEADS, MOBA_BLOCK, MOBA_QCHUNK
    Sp = -(-S // BS) * BS
    NB = Sp // BS
    NC = Sp // QC
    K = min(MOBA_TOPK, NB)

    def heads(t):
        t = t.reshape(B, S, H, MOBA_DH).transpose(0, 2, 1, 3)
        return jnp.pad(t, ((0, 0), (0, 0), (0, Sp - S), (0, 0)))

    q = heads(q) * (MOBA_DH ** -0.5)
    kb = heads(k).reshape(B, H, NB, BS, MOBA_DH)
    vb = heads(v).reshape(B, H, NB, BS, MOBA_DH)
    k_mean = jnp.mean(kb.astype(jnp.float32), axis=3)
    gate = jnp.einsum('bhsd,bhnd->bhsn', q.astype(jnp.float32), k_mean)
    q_blk = jnp.arange(Sp) // BS
    fully_past = jnp.arange(NB)[None, :] < q_blk[:, None]
    gate = jnp.where(fully_past, gate, -jnp.inf)
    _, sel = lax.top_k(gate, K)
    sel_valid = sel < q_blk[:, None]

    def to_chunks(t):
        return jnp.moveaxis(t.reshape(B, H, NC, QC, t.shape[-1]), 2, 0)

    bias_hb = rel_bias.T.astype(jnp.float32)
    b_idx = jnp.arange(B)[:, None, None, None]
    h_idx = jnp.arange(H)[None, :, None, None]
    offs = jnp.arange(BS)

    def one_chunk(args):
        c, qc, selc, validc = args
        q_pos = c * QC + jnp.arange(QC)
        own = (c * QC) // BS
        k_own = lax.dynamic_index_in_dim(kb, own, axis=2, keepdims=False)
        v_own = lax.dynamic_index_in_dim(vb, own, axis=2, keepdims=False)
        d_own = q_pos[:, None] - (own * BS + offs)[None, :]
        s_own = jnp.einsum('bhqd,bhkd->bhqk', qc, k_own).astype(jnp.float32) + bias_hb[:, t5_bucket(d_own)]
        s_own = jnp.where(d_own >= 0, s_own, -jnp.inf)
        k_sel = kb[b_idx, h_idx, selc]
        v_sel = vb[b_idx, h_idx, selc]
        d_sel = q_pos[:, None, None] - (selc[..., None] * BS + offs)
        s_sel = (jnp.einsum('bhqd,bhqjkd->bhqjk', qc, k_sel).astype(jnp.float32)
                 + bias_hb[h_idx[..., None], t5_bucket(d_sel)])
        s_sel = jnp.where(validc[..., None], s_sel, -jnp.inf)
        logits = jnp.concatenate([s_own, s_sel.reshape(B, H, QC, K * BS)], axis=-1)
        p = jax.nn.softmax(logits, axis=-1)
        p_own = p[..., :BS].astype(v_own.dtype)
        p_sel = p[..., BS:].reshape(B, H, QC, K, BS).astype(v_sel.dtype)
        return (jnp.einsum('bhqk,bhkd->bhqd', p_own, v_own)
                + jnp.einsum('bhqjk,bhqjkd->bhqd', p_sel, v_sel))

    out = lax.map(one_chunk, (jnp.arange(NC), to_chunks(q), to_chunks(sel), to_chunks(sel_valid)))
    out = out.transpose(1, 0, 3, 2, 4).reshape(B, Sp, H * MOBA_DH)
    return out[:, :S]

def mixer(h, rel_bias, w_in, w_alpha_up, b_alpha, g_gla_head, w_proj_gla, w_proj_moba, w_out):
    B, S, _ = h.shape
    proj = h @ w_in
    q_g, k_g, v_g, r_g, a_lr, q_m, k_m, v_m, z_g, z_m = jnp.split(proj, SPLIT_POINTS, axis=-1)
    log_a = jax.nn.log_sigmoid((a_lr @ w_alpha_up + b_alpha).astype(jnp.float32)) / GLA_TAU
    o_g = gla_chunked(q_g.reshape(B, S, GLA_HEADS, GLA_DK), k_g.reshape(B, S, GLA_HEADS, GLA_DK),
                      v_g.reshape(B, S, GLA_HEADS, GLA_DV), log_a.reshape(B, S, GLA_HEADS, GLA_DK))
    o_g = rmsnorm(o_g, g_gla_head).reshape(B, S, GLA_V).astype(h.dtype) * jax.nn.silu(r_g)
    o_m = moba_attention(q_m, k_m, v_m, rel_bias)
    merged = jax.nn.sigmoid(z_g) * (o_g @ w_proj_gla) + jax.nn.sigmoid(z_m) * (o_m @ w_proj_moba)
    return merged @ w_out

def memory_attention(h, mem_n, w_cq, w_ckv, w_co):
    B, S, _ = h.shape
    M = mem_n.shape[1]
    q = (h @ w_cq).reshape(B, S, MEM_HEADS, MEM_DH)
    k, v = jnp.split((mem_n @ w_ckv).reshape(B, M, 2, MEM_HEADS, MEM_DH), 2, axis=2)
    k, v = k[:, :, 0], v[:, :, 0]
    s = jnp.einsum('bqhd,bkhd->bhqk', q, k).astype(jnp.float32) * (MEM_DH ** -0.5)
    p = jax.nn.softmax(s, axis=-1).astype(v.dtype)
    o = jnp.einsum('bhqk,bkhd->bqhd', p, v).reshape(B, S, MEM_W)
    return o @ w_co

def hier_moe(h, w_rg, b_rg, w_re, b_re, w_gate, w_up, w_down):
    B, S, D = h.shape
    T = B * S
    xt = h.reshape(T, D)
    g_prob = jax.nn.softmax((xt @ w_rg).astype(jnp.float32) + b_rg, axis=-1)
    p_grp, grp = lax.top_k(g_prob, 1)
    e_logits = ((xt @ w_re).astype(jnp.float32) + b_re).reshape(T, N_GROUPS, EXPERTS_PER_GROUP)
    e_in = jnp.take_along_axis(e_logits, grp[:, :, None], axis=1)[:, 0]
    top_p, top_i = lax.top_k(jax.nn.softmax(e_in, axis=-1), TOPK_IN_GROUP)
    weights = p_grp * top_p / jnp.sum(top_p, axis=-1, keepdims=True)
    expert = grp * EXPERTS_PER_GROUP + top_i
    A = T * TOPK_IN_GROUP
    flat_e = expert.reshape(A)
    flat_t = jnp.repeat(jnp.arange(T, dtype=jnp.int32), TOPK_IN_GROUP)
    flat_w = weights.reshape(A)
    order = jnp.argsort(flat_e)
    se = flat_e[order]
    counts = jnp.zeros((N_EXPERTS,), jnp.int32).at[flat_e].add(1)
    padded = (counts + MOE_BLOCK - 1) // MOE_BLOCK * MOE_BLOCK
    start = jnp.cumsum(counts) - counts
    pend = jnp.cumsum(padded)
    pstart = pend - padded
    dest = pstart[se] + (jnp.arange(A) - start[se])
    cap = (A + N_EXPERTS * (MOE_BLOCK - 1) + MOE_BLOCK - 1) // MOE_BLOCK * MOE_BLOCK
    n_blk = cap // MOE_BLOCK
    buf_t = jnp.zeros((cap,), jnp.int32).at[dest].set(flat_t[order])
    buf_w = jnp.zeros((cap,), jnp.float32).at[dest].set(flat_w[order])
    blk_e = jnp.minimum(jnp.searchsorted(pend, jnp.arange(n_blk) * MOE_BLOCK, side='right'), N_EXPERTS - 1)

    def run_block(args):
        e, tok, w = args
        xb = xt[tok]
        hid = jax.nn.silu(xb @ w_gate[e]) * (xb @ w_up[e])
        return (hid @ w_down[e]) * w[:, None].astype(xb.dtype)

    yb = lax.map(run_block, (blk_e, buf_t.reshape(n_blk, MOE_BLOCK), buf_w.reshape(n_blk, MOE_BLOCK)))
    out = jnp.zeros((T, D), h.dtype).at[buf_t].add(yb.reshape(cap, D).astype(h.dtype))
    return out.reshape(B, S, D)

def first_inputs(seed: int = 0) -> dict:
    key = jax.random.key(seed)
    ks = jax.random.split(key, 26)
    f32 = jnp.float32
    L = DEPTH

    def nrm(k, shape, scale):
        return jax.random.normal(k, shape, f32) * scale

    def gain(k, shape):
        return 1.0 + 0.02 * jax.random.normal(k, shape, f32)

    return {
        'x': nrm(ks[0], (BATCH, SEQ, D_MODEL), 1.0),
        'mem': nrm(ks[1], (BATCH, MEM_LEN, D_MODEL), 1.0),
        'g_mem': gain(ks[2], (D_MODEL,)),
        'rel_bias': nrm(ks[3], (REL_BUCKETS, MOBA_HEADS), 0.5),
        'g_mix': gain(ks[4], (L, D_MODEL)),
        'w_in': nrm(ks[5], (L, D_MODEL, D_IN), D_MODEL ** -0.5),
        'w_alpha_up': nrm(ks[6], (L, GLA_LOWRANK, GLA_QK), GLA_LOWRANK ** -0.5),
        'b_alpha': nrm(ks[7], (L, GLA_QK), 0.1),
        'g_gla_head': gain(ks[8], (L, GLA_HEADS, GLA_DV)),
        'w_proj_gla': nrm(ks[9], (L, GLA_V, D_MODEL), GLA_V ** -0.5),
        'w_proj_moba': nrm(ks[10], (L, MOBA_W, D_MODEL), MOBA_W ** -0.5),
        'w_out': nrm(ks[11], (L, D_MODEL, D_MODEL), D_MODEL ** -0.5),
        'g_cross': gain(ks[12], (L, D_MODEL)),
        'w_cq': nrm(ks[13], (L, D_MODEL, MEM_W), D_MODEL ** -0.5),
        'w_ckv': nrm(ks[14], (L, D_MODEL, 2 * MEM_W), D_MODEL ** -0.5),
        'w_co': nrm(ks[15], (L, MEM_W, D_MODEL), MEM_W ** -0.5),
        'g_moe': gain(ks[16], (L, D_MODEL)),
        'w_router_group': nrm(ks[17], (L, D_MODEL, N_GROUPS), D_MODEL ** -0.5),
        'b_router_group': nrm(ks[18], (L, N_GROUPS), 0.01),
        'w_router_expert': nrm(ks[19], (L, D_MODEL, N_EXPERTS), D_MODEL ** -0.5),
        'b_router_expert': nrm(ks[20], (L, N_EXPERTS), 0.01),
        'w_exp_gate': nrm(ks[21], (L, N_EXPERTS, D_MODEL, D_EXPERT), D_MODEL ** -0.5),
        'w_exp_up': nrm(ks[22], (L, N_EXPERTS, D_MODEL, D_EXPERT), D_MODEL ** -0.5),
        'w_exp_down': nrm(ks[23], (L, N_EXPERTS, D_EXPERT, D_MODEL), D_EXPERT ** -0.5),
        'g_final': gain(ks[24], (D_MODEL,)),
    }

def first_block(x, mem, g_mem, rel_bias, g_mix, w_in, w_alpha_up, b_alpha, g_gla_head, w_proj_gla,
              w_proj_moba, w_out, g_cross, w_cq, w_ckv, w_co, g_moe, w_router_group, b_router_group,
              w_router_expert, b_router_expert, w_exp_gate, w_exp_up, w_exp_down, g_final):
    mem_n = rmsnorm(mem, g_mem)
    for l in range(DEPTH):
        x = x + mixer(rmsnorm(x, g_mix[l]), rel_bias, w_in[l], w_alpha_up[l], b_alpha[l], g_gla_head[l],
                      w_proj_gla[l], w_proj_moba[l], w_out[l])
        x = x + memory_attention(rmsnorm(x, g_cross[l]), mem_n, w_cq[l], w_ckv[l], w_co[l])
        x = x + hier_moe(rmsnorm(x, g_moe[l]), w_router_group[l], b_router_group[l], w_router_expert[l],
                         b_router_expert[l], w_exp_gate[l], w_exp_up[l], w_exp_down[l])
    return rmsnorm(x, g_final)


DEPTH_2 = 2

DIFF_HEADS = 4
DIFF_HEAD_DIM = 64
DIFF_WIDTH = DIFF_HEADS * 2 * DIFF_HEAD_DIM
SB_HEADS = 8
SB_HEAD_DIM = 64
SB_WIDTH = SB_HEADS * SB_HEAD_DIM
IN_COLS = 3 * DIFF_WIDTH + 3 * SB_WIDTH + 2 * D_MODEL
FFN_HIDDEN = -(-(8 * D_MODEL) // (3 * 256)) * 256
Q_BLOCK = 128
ROPE_THETA = 10000.0
NORM_EPS = 1e-6


def rms_norm(x, g):
    xf = x.astype(jnp.float32)
    y = xf * lax.rsqrt(jnp.mean(xf * xf, axis=-1, keepdims=True) + NORM_EPS)
    return (y * g.astype(jnp.float32)).astype(x.dtype)

def rope_tables(seq, dim):
    pos = jnp.arange(seq, dtype=jnp.float32)
    inv = ROPE_THETA ** (-jnp.arange(0, dim, 2, dtype=jnp.float32) / dim)
    ang = pos[:, None] * inv[None, :]
    return jnp.cos(ang), jnp.sin(ang)

def apply_rope(t, cos, sin):
    c = cos[None, :, None, :].astype(t.dtype)
    s = sin[None, :, None, :].astype(t.dtype)
    t1, t2 = jnp.split(t, 2, axis=-1)
    return jnp.concatenate([t1 * c - t2 * s, t2 * c + t1 * s], axis=-1)

def to_blocks(t):
    b, h, s, d = t.shape
    return t.reshape(b, h, s // Q_BLOCK, Q_BLOCK, d).transpose(2, 0, 1, 3, 4)

def from_blocks(o):
    nb, b, h, q, dv = o.shape
    return o.transpose(1, 0, 3, 2, 4).reshape(b, nb * q, h, dv)

def diff_attention(q1, q2, k1, k2, v, lam):
    s_len = k1.shape[2]
    kpos = jnp.arange(s_len)
    qpos_blocks = kpos.reshape(-1, Q_BLOCK)
    scale = DIFF_HEAD_DIM ** -0.5

    def block(args):
        qb1, qb2, qpos = args
        mask = kpos[None, :] <= qpos[:, None]

        def probs(qb, k):
            sc = jnp.einsum('bhqd,bhkd->bhqk', qb, k).astype(jnp.float32) * scale
            sc = jnp.where(mask, sc, -jnp.inf)
            return jax.nn.softmax(sc, axis=-1)

        w = probs(qb1, k1) - lam * probs(qb2, k2)
        return jnp.einsum('bhqk,bhkd->bhqd', w.astype(v.dtype), v)

    o = lax.map(block, (to_blocks(q1), to_blocks(q2), qpos_blocks))
    return from_blocks(o)

def stick_breaking_attention(q, k, v):
    s_len = k.shape[2]
    kpos = jnp.arange(s_len)
    qpos_blocks = kpos.reshape(-1, Q_BLOCK)
    scale = SB_HEAD_DIM ** -0.5

    def block(args):
        qb, qpos = args
        mask = kpos[None, :] < qpos[:, None]
        z = jnp.einsum('bhqd,bhkd->bhqk', qb, k).astype(jnp.float32) * scale
        log_beta = jax.nn.log_sigmoid(z)
        log_rem = jnp.where(mask, jax.nn.log_sigmoid(-z), 0.0)
        key_axis = log_rem.ndim - 1
        after = lax.cumsum(log_rem, axis=key_axis, reverse=True) - log_rem
        a = jnp.where(mask, jnp.exp(log_beta + after), 0.0)
        return jnp.einsum('bhqk,bhkd->bhqd', a.astype(v.dtype), v)

    o = lax.map(block, (to_blocks(q), qpos_blocks))
    return from_blocks(o)

def hybrid_layer(x, cos, sin, layer, g_attn, w_in, b_gate, lam_p, subln, w_o_diff, w_o_sb,
                 w_out, g_ffn, w_ffn_in, w_ffn_out):
    b, s, _ = x.shape
    h = rms_norm(x, g_attn)
    proj = h @ w_in
    offs = np.cumsum([DIFF_WIDTH, DIFF_WIDTH, DIFF_WIDTH, SB_WIDTH, SB_WIDTH, SB_WIDTH]).tolist()
    dq, dk, dv, sq, sk, sv, gates = jnp.split(proj, offs, axis=-1)

    dq = apply_rope(dq.reshape(b, s, 2 * DIFF_HEADS, DIFF_HEAD_DIM), cos, sin)
    dk = apply_rope(dk.reshape(b, s, 2 * DIFF_HEADS, DIFF_HEAD_DIM), cos, sin)
    dq = dq.reshape(b, s, DIFF_HEADS, 2, DIFF_HEAD_DIM).transpose(3, 0, 2, 1, 4)
    dk = dk.reshape(b, s, DIFF_HEADS, 2, DIFF_HEAD_DIM).transpose(3, 0, 2, 1, 4)
    dv = dv.reshape(b, s, DIFF_HEADS, 2 * DIFF_HEAD_DIM).transpose(0, 2, 1, 3)
    lam_init = 0.8 - 0.6 * math.exp(-0.3 * layer)
    lp = lam_p.astype(jnp.float32)
    lam = jnp.exp(jnp.sum(lp[0] * lp[1])) - jnp.exp(jnp.sum(lp[2] * lp[3])) + lam_init
    o_diff = diff_attention(dq[0], dq[1], dk[0], dk[1], dv, lam)
    o_diff = (rms_norm(o_diff, subln) * (1.0 - lam_init)).reshape(b, s, DIFF_WIDTH)

    sq = sq.reshape(b, s, SB_HEADS, SB_HEAD_DIM).transpose(0, 2, 1, 3)
    sk = sk.reshape(b, s, SB_HEADS, SB_HEAD_DIM).transpose(0, 2, 1, 3)
    sv = sv.reshape(b, s, SB_HEADS, SB_HEAD_DIM).transpose(0, 2, 1, 3)
    o_sb = stick_breaking_attention(sq, sk, sv).reshape(b, s, SB_WIDTH)

    g_diff, g_sb = jnp.split(jax.nn.sigmoid(gates + b_gate), 2, axis=-1)
    merged = g_diff * (o_diff @ w_o_diff) + g_sb * (o_sb @ w_o_sb)
    x = x + merged @ w_out

    h2 = rms_norm(x, g_ffn)
    gate, up = jnp.split(h2 @ w_ffn_in, 2, axis=-1)
    return x + (jax.nn.silu(gate) * up) @ w_ffn_out

def second_inputs(seed: int = 0) -> dict:
    key = jax.random.key(seed)
    ks = jax.random.split(key, 14)
    f32 = jnp.float32
    nrm = lambda k, shape, scale: jax.random.normal(k, shape, f32) * scale
    return {
        "x": nrm(ks[0], (BATCH, SEQ, D_MODEL), 1.0),
        "norm_attn": 1.0 + nrm(ks[1], (DEPTH_2, D_MODEL), 0.02),
        "w_in": nrm(ks[2], (DEPTH_2, D_MODEL, IN_COLS), D_MODEL ** -0.5),
        "b_gate": nrm(ks[3], (DEPTH_2, 2 * D_MODEL), 0.02),
        "diff_lambda": nrm(ks[4], (DEPTH_2, 4, DIFF_HEAD_DIM), 0.1),
        "diff_subln": 1.0 + nrm(ks[5], (DEPTH_2, 2 * DIFF_HEAD_DIM), 0.02),
        "w_o_diff": nrm(ks[6], (DEPTH_2, DIFF_WIDTH, D_MODEL), DIFF_WIDTH ** -0.5),
        "w_o_sb": nrm(ks[7], (DEPTH_2, SB_WIDTH, D_MODEL), SB_WIDTH ** -0.5),
        "w_out": nrm(ks[8], (DEPTH_2, D_MODEL, D_MODEL), D_MODEL ** -0.5),
        "norm_ffn": 1.0 + nrm(ks[9], (DEPTH_2, D_MODEL), 0.02),
        "w_ffn_in": nrm(ks[10], (DEPTH_2, D_MODEL, 2 * FFN_HIDDEN), D_MODEL ** -0.5),
        "w_ffn_out": nrm(ks[11], (DEPTH_2, FFN_HIDDEN, D_MODEL), FFN_HIDDEN ** -0.5),
        "norm_final": 1.0 + nrm(ks[12], (D_MODEL,), 0.02),
    }

def second_block(x, norm_attn, w_in, b_gate, diff_lambda, diff_subln, w_o_diff, w_o_sb, w_out,
              norm_ffn, w_ffn_in, w_ffn_out, norm_final):
    cos, sin = rope_tables(x.shape[1], DIFF_HEAD_DIM)
    for layer in range(DEPTH_2):
        x = hybrid_layer(x, cos, sin, layer, norm_attn[layer], w_in[layer], b_gate[layer],
                         diff_lambda[layer], diff_subln[layer], w_o_diff[layer], w_o_sb[layer],
                         w_out[layer], norm_ffn[layer], w_ffn_in[layer], w_ffn_out[layer])
    return rms_norm(x, norm_final)


def setup_inputs(seed=0):
    out = dict(first_inputs(seed))
    for name, value in second_inputs(seed + 1).items():
        if name != "x":
            out[name + "_2"] = value
    return out


def reference(
    x, mem, g_mem, rel_bias, g_mix, w_in, w_alpha_up, b_alpha, g_gla_head, w_proj_gla,
    w_proj_moba, w_out, g_cross, w_cq, w_ckv, w_co, g_moe, w_router_group, b_router_group,
    w_router_expert, b_router_expert, w_exp_gate, w_exp_up, w_exp_down, g_final, norm_attn_2,
    w_in_2, b_gate_2, diff_lambda_2, diff_subln_2, w_o_diff_2, w_o_sb_2, w_out_2, norm_ffn_2,
    w_ffn_in_2, w_ffn_out_2, norm_final_2,
):
    x = first_block(
        x, mem, g_mem, rel_bias, g_mix, w_in, w_alpha_up, b_alpha, g_gla_head, w_proj_gla,
        w_proj_moba, w_out, g_cross, w_cq, w_ckv, w_co, g_moe, w_router_group, b_router_group,
        w_router_expert, b_router_expert, w_exp_gate, w_exp_up, w_exp_down, g_final,
    )
    return second_block(
        x, norm_attn_2, w_in_2, b_gate_2, diff_lambda_2, diff_subln_2, w_o_diff_2, w_o_sb_2,
        w_out_2, norm_ffn_2, w_ffn_in_2, w_ffn_out_2, norm_final_2,
    )


_drawn_inputs = setup_inputs


def setup_inputs(seed=0):
    import zlib

    import numpy as np

    out = dict(_drawn_inputs(seed))
    spreads = {}
    factors = {'g_mem': 4.167,
     'g_cross': 3.888,
     'b_gate_2': 8.0,
     'diff_subln_2': 4.814,
     'norm_ffn_2': 3.074,
     'norm_final_2': 8.043,
     'g_moe': 3.242,
     'b_router_group': 8.0,
     'b_router_expert': 3.523}
    for name, (base, spread) in spreads.items():
        noise = np.random.default_rng([zlib.crc32(name.encode()), seed]).standard_normal(out[name].shape)
        drawn = base * np.exp(spread * noise) if base else spread * noise
        out[name] = __import__('jax').numpy.asarray(drawn.astype(out[name].dtype))
    for name, factor in factors.items():
        out[name] = (out[name] * factor).astype(out[name].dtype)
    return out
```

```python
import math
from contextlib import ExitStack

import concourse.bass as bass
import numpy as np
from concourse import mybir

F32 = mybir.dt.float32
I32 = mybir.dt.int32
U32 = mybir.dt.uint32
ALU = mybir.AluOpType
ACT = mybir.ActivationFunctionType
AX = mybir.AxisListType.X

P = 128
T = 256
TB = T // P
D = 1024
KT = D // P
EPS = 1e-6
BIG = 1.0e30
HALF = 512

NE = 32
PAIRS = NE // 2
SLOTS = 64
OVER_PASSES = T // SLOTS - 1
KEYS = NE + 2

FFN = 2816
FT = FFN // P
RING = 6
LAYERS = 2

CA = dict(ident=(0, 128), later=(128, 128), earlier=(256, 128), ones=(384, 128), m64=(512, 64), iota=(576, 128),
          i100=(704, 8))
CA_W = 712
CB = dict(rope=(0, 128), cos=(128, 256), sin=(384, 256), causal=(640, 384), strict=(1024, 384))
CB_W = 1408
CC = dict(rev=(0, 128), buckets=(128, 384))
CC_W = 512

ROWS = {}
_n = 0
for _name, _k in (("g_mem", 8), ("g_mix", 8), ("g_cross", 8), ("g_moe", 8), ("g_final", 8), ("g_gla_head", 4),
                  ("b_alpha", 2), ("norm_attn_2", 16), ("norm_ffn_2", 16), ("b_gate_2", 32), ("diff_subln_2", 2),
                  ("norm_final_2", 8)):
    ROWS[_name] = (_n, _k)
    _n += _k
NROWS = _n


def constants():
    i = np.arange(P)
    c = np.zeros((P, CA_W + CB_W + CC_W), np.float32)

    def put(base, table, name, value):
        at, n = table[name]
        c[:value.shape[0], base + at:base + at + n] = value

    put(0, CA, "ident", np.eye(P))
    put(0, CA, "later", (i[:, None] < i[None, :]).astype(np.float32))
    put(0, CA, "earlier", (i[:, None] > i[None, :]).astype(np.float32))
    put(0, CA, "ones", np.ones((P, P)))
    put(0, CA, "m64", ((i % 64)[:, None] <= np.arange(64)[None, :]).astype(np.float32))
    put(0, CA, "iota", np.tile(np.arange(P) % SLOTS, (P, 1)))
    put(0, CA, "i100", np.tile(np.arange(8) + 100, (P, 1)))
    rope = np.zeros((P, P))
    for h in range(0, P, 64):
        for d in range(32):
            rope[h + 32 + d, h + d] = -1.0
            rope[h + d, h + 32 + d] = 1.0
    inv = np.float32(10000.0) ** (-np.arange(0, 64, 2, dtype=np.float32) / np.float32(64))
    ang = np.arange(T, dtype=np.float32)[None, :] * inv[i % 32][:, None]
    put(CA_W, CB, "rope", rope)
    put(CA_W, CB, "cos", np.cos(ang))
    put(CA_W, CB, "sin", np.sin(ang))
    q = np.arange(P)[:, None]
    diag = np.where(i[None, :] <= q, 0.0, -BIG)
    put(CA_W, CB, "causal", np.concatenate([diag, np.zeros((P, P)), diag], 1))
    strict = (i[:, None] < i[None, :]).astype(np.float32)
    put(CA_W, CB, "strict", np.concatenate([strict, np.ones((P, P)), strict], 1))
    put(CA_W + CB_W, CC, "rev", np.eye(P)[::-1])
    dist = (T - 1) - np.arange(384)
    n = np.maximum(dist, 0)
    large = 16 + (np.log(np.maximum(n, 1) / 16) / math.log(8) * 16).astype(np.int64)
    bucket = np.where(n < 16, n, np.minimum(large, 31))
    put(CA_W + CB_W, CC, "buckets", ((bucket[None, :] == np.arange(32)[:, None]) & (dist >= 0)[None, :]).astype(np.float32))
    return c


GATE_HALVES = [[] for _ in range(8)]
for _i in range(12):
    GATE_HALVES[2 * (_i // 3) + (_i % 3 == 2)].append((("ga2", "ga3", "gb0", "gb1", "gb2", "gb3")[_i // 2], _i % 2))


def group_plan():
    g = ["gains", "mt0", "mt1", "mt2", "mt3", "xt0", "xt1", "xt2", "xt3", "n_mem", "bucket",
         "kc0", "kc1", "n_mix", "vc0", "vc1", "bj0", "bj1", "bj2", "bj3"]
    g += ["qk0", "qk1", "v0", "v1", "alr", "alpha", "r0", "r1", "qm0", "qm1", "km0", "km1", "vm0", "vm1"]
    g += ["kt", "ms0", "ae", "ao", "ms1", "ke", "ko", "mt_0", "oe", "oo", "ie", "io", "ms2"]
    g += ["zg0", "gn0", "gn1", "mo0", "mt_1", "ms3", "zg1"]
    for h in range(2, 8):
        g += [f"mt_{h}"]
        if h + 2 < 8:
            g += [f"ms{h + 2}"]
        g += [("zg2", "zg3", "zm0", "zm1", "zm2", "zm3")[h - 2]]
        if h % 2 == 0:
            g += [f"mo{h // 2}"]
    g += [f"pa{i}" for i in range(4)] + [f"pb{i}" for i in range(4)] + [f"ou{i}" for i in range(4)]
    g += ["n_cross", "cq0", "cq1"] + ["cs0"]
    for h in range(4):
        g += ([f"cs{h + 1}"] if h < 3 else []) + [f"ct{h}", f"co{h}"]
    g += [f"cw{i}" for i in range(4)]
    g += ["n_moe", "route", "rank"] + [f"ht{i}" for i in range(4)]
    first = list(g)
    second = [f"at{i}" for i in range(4)] + ["n_final"]
    for l in range(LAYERS):
        s = ["n_attn", "dq0", "dq1", "dk0", "dk1", "rq0", "rq1", "rk0", "rk1", "dv0", "dv1", "ds0", "de0",
             "sq0", "sq1", "dt0", "ds1", "de1", "sk0", "sk1", "do0", "dt1", "ds2", "de2", "sv0", "sv1", "do1",
             "dt2", "ds3", "de3", "bz0", "ga0", "do2", "dt3", "bz1", "ba0", "ga1", "do3", "dn0", "dn1"]
        for h in range(8):
            if h < 6:
                s += [f"bz{h + 2}"]
            if h < 7:
                s += [f"ba{h + 1}"]
            s += [name for name, half in GATE_HALVES[h] if half == 0]
            if h % 2 == 0:
                s += [f"bo{h // 2}"]
        s += [f"pa{i}" for i in range(4)] + [f"pb{i}" for i in range(4)] + [f"ou{i}" for i in range(4)]
        s += ["n_ffn"]
        for j in range(11):
            s += [f"fg{j}", f"fu{j}"]
        s += [f"fo{i}" for i in range(4)]
        second += [f"{n}.{l}" for n in s]
    second += ["n_last"] + [f"yt{i}" for i in range(4)]
    plan, use = {}, [0] * 8
    bank = 0
    for name in first:
        plan[name] = (bank, use[bank])
        use[bank] += 1
        bank = (bank + 1) % 8
    before_experts = list(use)
    for i in range(4):
        plan[f"acc{i}"] = (4 + i, use[4 + i])
        use[4 + i] += 1
    bank = 0
    for name in second:
        plan[name] = (bank, use[bank])
        use[bank] += 1
        bank = (bank + 1) % 8
    return plan, before_experts


PLAN, BEFORE_EXPERTS = group_plan()

FIRST_CHUNKS = [("ckv_k", "kc1"), ("ckv_v", "vc1"), ("qk", "qk1"), ("v", "v1"), ("r", "r1"), ("qm", "qm1"),
                ("km", "km1"), ("vm", "vm1"), ("zg0", "zg1"), ("zg1", "zg3"), ("zm0", "zm1"), ("zm1", "zm3"),
                ("proj_gla", "pa3"), ("proj_moba", "pb3"), ("out0", "ou1"), ("out1", "ou3"), ("cq", "cq1"),
                ("co", "cw3")]
LAYER_CHUNKS = ([("dq", "dq1"), ("dk", "dk1"), ("dv", "dv1"), ("sq", "sq1"), ("sk", "sk1"), ("sv", "sv1"),
                 ("ga0", "ga1"), ("ga1", "ga3"), ("gb0", "gb1"), ("gb1", "gb3"), ("proj_diff", "pa3"),
                 ("proj_sb", "pb3"), ("out0", "ou1"), ("out1", "ou3")]
                + [(f"ffn{j}", f"fu{j}") for j in range(11)] + [(f"down{j}", "fo3") for j in range(5)])
assert len(FIRST_CHUNKS) % RING == 0 and len(LAYER_CHUNKS) % RING == 0
MOE_USES = PAIRS
CHUNK = {}
for _i, (_name, _g) in enumerate(FIRST_CHUNKS):
    CHUNK[_name] = (_i % RING, _i // RING)
for _l in range(LAYERS):
    for _i, (_name, _g) in enumerate(LAYER_CHUNKS):
        CHUNK[f"{_name}.{_l}"] = (_i % RING, len(FIRST_CHUNKS) // RING + MOE_USES + _l * len(LAYER_CHUNKS) // RING + _i // RING)

NORMS = ["n_mem", "n_mix", "n_cross", "n_moe", "n_final", "n_attn.0", "n_ffn.0", "n_attn.1", "n_ffn.1", "n_last"]


def build(nc, a, out):
    with ExitStack() as ctx:
        def sb(name, shape, dt=F32):
            return ctx.enter_context(nc.sbuf_tensor(name, shape, dt))

        def sem(name):
            return ctx.enter_context(nc.semaphore(name))

        ring = sb("ring", [P, RING, 4096])
        tail = sb("tail", [P, 2048])
        xres = sb("xres", [P, KT, T])
        hn = sb("hn", [P, KT, T])
        ca = sb("ca", [P, CA_W])
        cb = sb("cb", [P, CB_W])
        gcol = sb("gcol", [P, 128])
        G = sb("G", [P, 6144])
        SZ = sb("SZ", [P, 4096])
        KV = sb("KV", [P, 2048])
        SQ = sb("SQ", [P, 2048])
        TMP = sb("TMP", [P, 1536])
        sm = sb("sm", [P, 96])
        cnt = sb("cnt", [P, 1], I32)
        ps = [ctx.enter_context(nc.psum_tensor(f"bank{i}", [P, HALF], F32)) for i in range(8)]
        hankel_dram = nc.dram_tensor("hankel_rows", (8, 384), F32, kind="Internal").ap()

        def view(t, at, *dims):
            n = int(np.prod(dims))
            v = t[:, at:at + n]
            if len(dims) == 2:
                return v.rearrange("p (a b) -> p a b", b=dims[1])
            if len(dims) == 3:
                return v.rearrange("p (a b c) -> p a b c", b=dims[1], c=dims[2])
            return v

        def const(tile, table, name):
            at, n = table[name]
            return tile[:, at:at + n]

        ident, later, earlier, ones, m64, iota, i100 = (const(ca, CA, n) for n in CA)
        rope, cosT, sinT, causal, strict = (const(cb, CB, n) for n in CB)
        eps_col = sm[:, 0:1]

        def gain(name, k):
            at, n = ROWS[name]
            return gcol[:, at + k:at + k + 1]

        wide = [ring[:, s, :].rearrange("p (k n) -> p k n", k=8) for s in range(RING)]
        tall = [ring[:, s, :].rearrange("p (k n) -> p k n", k=4) for s in range(RING)]
        tail_w = view(tail, 0, 2, 1024)

        mem_tok = hn[:, :, :].rearrange("p a b -> p (a b)").rearrange("p (a b) -> p a b", a=2)
        x_tok = view(G, 4096, 2, 1024)
        mem_f, mem_n = view(SZ, 0, KT, T), view(G, 2048, KT, T)
        hankel = view(SZ, 2048, 8, T)
        rev, buckets, urow = G[:, 0:128], G[0:32, 128:512], G[0:8, 512:896]
        relb = G[0:32, 896:904]
        grows = G[0:NROWS, 1024:1152]
        bias = view(tail, 0, 8, T)
        kc, vc = view(KV, 0, 4, T), view(KV, 1024, TB, HALF)
        qg, kg, vg, rg = view(G, 0, 2, T), view(G, 512, 2, T), view(G, 1024, TB, HALF), view(G, 2048, 4, T)
        qm, km, vm = view(G, 3072, 4, T), view(G, 4096, 4, T), view(G, 5120, TB, HALF)
        og, om = view(G, 0, 4, T), qm
        walr, wau = view(cb, 0, KT, 16), cb[0:16, 128:384]
        wr, brow = view(cb, 384, KT, 36), cb[:, 672:708]
        alr = cb[0:16, 708:964]
        za, t1, bcum, dmid = (view(SZ, 512 * i, 2, T) for i in range(4))
        dlast = za
        ex = [view(SZ, 2048 + 512 * i, 2, T) for i in range(4)]
        att = [view(SZ, 1024 + 512 * i, HALF) for i in range(2)]
        states = view(SZ, 0, 3, 2, P)
        kdt = view(SQ, 0, TB, 2 * P)
        z1, z2 = view(SZ, 0, KT, T), view(SZ, 2048, KT, T)
        hsq, hroot = view(SQ, 0, 4, T), view(SQ, 1024, 4, T)
        prob = [TMP[:, 384 * i:384 * i + 384] for i in range(2)]
        probT = [TMP[:, 768 + 384 * i:768 + 384 * i + 384] for i in range(2)]
        stick = [TMP[:, 384 * i:384 * i + 384] for i in range(4)]
        qc, oc = view(G, 0, 4, T), view(G, 1024, 4, T)
        cprob = [view(G, 2048 + 512 * i, TB, T) for i in range(2)]
        cprobT = [view(G, 3072 + 512 * i, HALF) for i in range(2)]
        htok = view(G, 0, TB, D)
        xe = view(G, 2048, KT, P)
        y = G[:, 3072:4096]
        acc_sb = view(G, 4096, TB, D)
        sel, selw = view(SZ, 0, TB, P), view(SZ, 256, TB, P)
        selT = SZ[:, 512:768]
        gsil, hid, hidT = SZ[:, 768:1280], SZ[:, 1280:1792], view(SZ, 1792, 4, P)
        key, wgt, msk = view(SZ, 2304, TB, KEYS), view(SZ, 2372, TB, NE), view(SZ, 2436, TB, NE)
        lg = view(SZ, 2500, TB, 36)
        zero = SZ[:, 2600:3240]
        rt = SZ[:, 3300:4096]
        def small(at, n):
            return view(rt, at, TB, n)

        d4, e4, t4, oh4, eg = small(0, 4), small(8, 4), small(16, 4), small(24, 4), small(32, 32)
        ein, ein2, t8, oh1, oh2, w8, m8 = (small(96 + 16 * i, 8) for i in range(7))
        gm, rmin, m1, m2, dm, ex2, pg, w1, w2 = (small(208 + 2 * i, 1) for i in range(9))
        lam_s, lam_e, lam, subs = sm[:, 64:68], sm[:, 68:72], sm[:, 72:74], sm[:, 74:75]
        dq, dk, dv = view(G, 0, 4, T), view(G, 1024, 4, T), view(G, 2048, TB, HALF)
        bq, bk, bv = view(G, 3072, 4, T), view(G, 4096, 4, T), view(G, 5120, TB, HALF)
        od, ob = dq, bq
        hidF = view(G, 0, FT, T)
        p1 = [KV[:, 384 * i:384 * i + 384] for i in range(2)]
        p2 = [KV[:, 768 + 384 * i:768 + 384 * i + 384] for i in range(2)]
        lbeta = [tail[:, 384 * i:384 * i + 384] for i in range(2)]
        lrem = [tail[:, 768 + 384 * i:768 + 384 * i + 384] for i in range(2)]
        lamt = view(KV, 1536, LAYERS * 4, 64)
        y_out = view(G, 0, TB, D)

        bank_full = [sem(f"bank_full{i}") for i in range(8)]
        bank_free = [sem(f"bank_free{i}") for i in range(8)]
        slot_landed = [sem(f"slot_landed{i}") for i in range(RING)]
        over_landed = [sem(f"over_landed{i}") for i in range(RING)]
        tail_landed, const_in, rows_in, mem_in, x_in, bias_in, small_in, router_in, cb_in, lam_in = (
            sem(n) for n in ("tail_landed", "const_in", "rows_in", "mem_in", "x_in", "bias_in", "small_in",
                             "router_in", "cb_in", "lam_in"))
        urow_masked, urow_stored, hankel_in = sem("urow_masked"), sem("urow_stored"), sem("hankel_in")
        dve_chain, act_chain = sem("dve_chain"), sem("act_chain")
        eps_ready, sq_ready, h_ready = sem("eps_ready"), sem("sq_ready"), sem("h_ready")
        gla_softplus, gla_diffs, gla_exps, gla_scaled = (sem(n) for n in ("gla_softplus", "gla_diffs", "gla_exps", "gla_scaled"))
        hsq_ready, og_ready, merged_ready = sem("hsq_ready"), sem("og_ready"), sem("merged_ready")
        logit_ready, exp_ready, prob_ready = sem("logit_ready"), sem("exp_ready"), sem("prob_ready")
        z_sig, rotated = sem("z_sigmoid"), sem("rotated")
        route_diff, route_exp, mask_ready, keys_ready, count_ready = (sem(n) for n in (
            "route_diff", "route_exp", "mask_ready", "keys_ready", "count_ready"))
        blank, passed, iota_moved = sem("blank"), sem("passed"), sem("iota_moved")
        sb_logs, sb_rem, sb_exp, sb_prob = (sem(n) for n in ("sb_logs", "sb_rem", "sb_exp", "sb_prob"))
        lam_sums, lam_exps, out_done = sem("lam_sums"), sem("lam_exps"), sem("out_done")
        moe_sems = []
        for tag in ("", "over_"):
            moe_sems.append({n: sem(tag + n) for n in (
                "gate_done", "up_done", "gather_done", "hidT_done", "selT_done", "y0_done", "y1_done",
                "silu_made", "hid_made", "sel_made", "selw_made", "xe_a", "xe_d", "hidT_out", "selT_out", "y0_out", "y1_out")})

        def b(name):
            return ps[PLAN[name][0]]

        def full(eng, name):
            eng.wait_ge(bank_full[PLAN[name][0]], PLAN[name][1] + 1)

        def room(eng, name):
            if PLAN[name][1]:
                eng.wait_ge(bank_free[PLAN[name][0]], PLAN[name][1])

        def fin(ins, name):
            ins.then_inc(bank_full[PLAN[name][0]], 1)

        def emptied(eng, name):
            eng.wait_ge(bank_free[PLAN[name][0]], PLAN[name][1] + 1)

        def freed(ins, name):
            ins.then_inc(bank_free[PLAN[name][0]], 1)

        def landed(eng, name):
            slot, use = CHUNK[name]
            eng.wait_ge(slot_landed[slot], 32 * (use + 1))

        block = ctx.enter_context(nc.Block())

        @block.sync
        def _(sp):
            w_in, w_in2 = a["w_in"][0], a["w_in_2"]
            sp.dma_start(ca[:, :], a["consts"][:, 0:CA_W]).then_inc(const_in, 16)
            sp.dma_start(grows, a["gains"]).then_inc(rows_in, 16)
            sp.dma_start(mem_tok, a["mem"][0].rearrange("(t p) n -> p t n", p=P)).then_inc(mem_in, 16)
            sp.dma_start(x_tok, a["x"][0].rearrange("(t p) n -> p t n", p=P)).then_inc(x_in, 16)
            sp.dma_start(relb, a["rel_bias"][:, :]).then_inc(bias_in, 16)
            sp.dma_start(rev, a["consts"][:, CA_W + CB_W:CA_W + CB_W + 128]).then_inc(bias_in, 16)
            sp.dma_start(buckets, a["consts"][0:32, CA_W + CB_W + 128:CA_W + CB_W + 512]).then_inc(bias_in, 16)

            def cols(w, at, n=HALF):
                return w[:, at:at + n].rearrange("(k p) n -> p k n", p=P)

            def rows4(w, at=0):
                return w[at:at + 512, :].rearrange("(k p) n -> p k n", p=P)

            def fetch(slot, dst, src, k):
                h = k // 2
                sp.dma_start(dst[:, 0:h], src[:, 0:h]).then_inc(slot_landed[slot], 16)
                sp.dma_start(dst[:, h:k], src[:, h:k]).then_inc(slot_landed[slot], 16)

            offs = dict(qk=0, v=512, r=1024, qm=1552, km=2064, vm=2576, zg0=3088, zg1=3600, zm0=4112, zm1=4624)
            for i, (name, _) in enumerate(FIRST_CHUNKS):
                slot = i % RING
                if i >= RING:
                    full(sp, FIRST_CHUNKS[i - RING][1])
                if name in offs:
                    fetch(slot, wide[slot], cols(w_in, offs[name]), 8)
                elif name in ("proj_gla", "proj_moba"):
                    fetch(slot, tall[slot], rows4(a["w_" + name][0]), 4)
                elif name in ("out0", "out1"):
                    fetch(slot, wide[slot], cols(a["w_out"][0], HALF * (name == "out1")), 8)
                elif name in ("ckv_k", "ckv_v"):
                    fetch(slot, wide[slot], cols(a["w_ckv"][0], HALF * (name == "ckv_v")), 8)
                elif name == "cq":
                    fetch(slot, wide[slot], cols(a["w_cq"][0], 0), 8)
                else:
                    fetch(slot, tall[slot], rows4(a["w_co"][0]), 4)

            def expert_pair(p, sems, before):
                for slot in range(RING):
                    w = (a["w_exp_gate"], a["w_exp_up"], a["w_exp_down"])[slot // 2][0]
                    k, dst = (8, wide[slot]) if slot < 4 else (4, tall[slot])
                    src = w[2 * p + slot % 2].rearrange("(k p) n -> p k n", p=P)
                    before(slot)
                    h = k // 2
                    sp.dma_start(dst[:, 0:h], src[:, 0:h]).then_inc(sems[slot], 16)
                    sp.dma_start(dst[:, h:k], src[:, h:k]).then_inc(sems[slot], 16)

            m = moe_sems[0]
            uses = ("gate_done", "gate_done", "up_done", "up_done", "y1_done", "y1_done")
            expert_pair(0, slot_landed, lambda slot: full(sp, FIRST_CHUNKS[len(FIRST_CHUNKS) - RING + slot][1]))
            with sp.Fori(1, PAIRS) as p:
                expert_pair(p, slot_landed, lambda slot: sp.wait_ge(m[uses[slot]], p))

            for slot in range(RING):
                sp.wait_ge(m[uses[slot]], PAIRS)
            sp.wait_ge(count_ready, 1)
            most = sp.value_load(cnt[0:1, 0:1], min_val=0, max_val=T)
            with sp.If(most > SLOTS):
                o = moe_sems[1]
                expert_pair(0, over_landed, lambda slot: None)
                with sp.Fori(1, OVER_PASSES * PAIRS) as i:
                    expert_pair(i % PAIRS, over_landed, lambda slot: sp.wait_ge(o[uses[slot]], i))
                for slot in range(RING):
                    sp.wait_ge(o[uses[slot]], OVER_PASSES * PAIRS)

            for l in range(LAYERS):
                off2 = dict(dq=0, dk=512, dv=1024, sq=1536, sk=2048, sv=2560, ga0=3072, ga1=3584, gb0=4096, gb1=4608)
                for i, (name, _) in enumerate(LAYER_CHUNKS):
                    slot = i % RING
                    if i >= RING:
                        full(sp, LAYER_CHUNKS[i - RING][1] + f".{l}")
                    elif l:
                        full(sp, LAYER_CHUNKS[len(LAYER_CHUNKS) - RING + i][1] + f".{l - 1}")
                    if name in off2:
                        fetch(slot, wide[slot], cols(w_in2[l], off2[name]), 8)
                    elif name == "proj_diff":
                        fetch(slot, tall[slot], rows4(a["w_o_diff_2"][l]), 4)
                    elif name == "proj_sb":
                        fetch(slot, tall[slot], rows4(a["w_o_sb_2"][l]), 4)
                    elif name in ("out0", "out1"):
                        fetch(slot, wide[slot], cols(a["w_out_2"][l], HALF * (name == "out1")), 8)
                    elif name[:3] == "ffn":
                        j = int(name[3:])
                        w = a["w_ffn_in_2"][l]
                        for half in range(2):
                            sp.dma_start(wide[slot][:, :, 256 * half:256 * half + 256],
                                         cols(w, FFN * half + 256 * j, 256)).then_inc(slot_landed[slot], 16)
                    else:
                        fetch(slot, tall[slot], rows4(a["w_ffn_out_2"][l], 512 * int(name[4:])), 4)
                    if name == "down0":
                        full(sp, f"pb3.{l}")
                        sp.dma_start(tail_w, a["w_ffn_out_2"][l][2560:2816, :].rearrange("(k p) n -> p k n", p=P)).then_inc(tail_landed, 16)
            for tb in range(TB):
                emptied(sp, f"yt{2 * tb}")
                emptied(sp, f"yt{2 * tb + 1}")
                sp.dma_start(out[0, tb * P:(tb + 1) * P, :], y_out[:, tb, :]).then_inc(out_done, 16)
            sp.wait_ge(out_done, 32)

        @block.gpsimd
        def _(pool):
            pool.wait_ge(urow_masked, 1)
            emptied(pool, "bucket")
            pool.dma_start(hankel_dram[:, :], urow).then_inc(urow_stored, 16)
            pool.wait_ge(urow_stored, 16)
            pool.dma_start(hankel, bass.AP(hankel_dram.tensor, 0, [[1, P], [384, 8], [1, T]])).then_inc(hankel_in, 16)
            full(pool, "rank")
            pool.dma_start(cb[:, :], a["consts"][:, CA_W:CA_W + CB_W]).then_inc(cb_in, 16)
            pool.dma_start(lamt, bass.AP(a["diff_lambda_2"].tensor, 0, [[0, P], [1, LAYERS * 256]])
                           ).then_inc(lam_in, 16)

        @block.tensor
        def _(pe):
            mm, tr = nc.tensor.matmul, nc.tensor.transpose

            def linear_f(chunk, src, names, k8=True, h_at=None, nk=8):
                landed(pe, chunk)
                w = (wide if nk == 8 else tall)[CHUNK[chunk][0]]
                for j, name in enumerate(names):
                    room(pe, name)
                    for half in range(2):
                        mt = 2 * j + half
                        for k in range(nk):
                            if h_at is not None and mt == 0:
                                pe.wait_ge(h_ready, h_at + k + 1)
                            m = mm(b(name)[:, T * half:T * half + T], w[:, k, P * mt:P * mt + P], src[:, k, :],
                                   start=k == 0, stop=k == nk - 1)
                    fin(m, name)

            def tile_f(chunk, name, mt):
                half = mt % 2
                if half == 0:
                    landed(pe, chunk)
                    room(pe, name)
                for k in range(8):
                    m = mm(b(name)[:, T * half:T * half + T], wide[CHUNK[chunk][0]][:, k, P * mt:P * mt + P], hn[:, k, :],
                           start=k == 0, stop=k == 7)
                if half:
                    fin(m, name)

            def group_f(chunk, name, j):
                tile_f(chunk, name, 2 * j)
                tile_f(chunk, name, 2 * j + 1)

            def linear_t(chunk, src, names):
                landed(pe, chunk)
                w = wide[CHUNK[chunk][0]]
                for tb, name in enumerate(names):
                    room(pe, name)
                    for k in range(8):
                        m = mm(b(name)[:, :], src[:, k, P * tb:P * tb + P], w[:, k, :], start=k == 0, stop=k == 7)
                    fin(m, name)

            def norm_sum(name):
                n = NORMS.index(name)
                room(pe, name)
                sqv = view(SQ, 0, KT, T)
                for k in range(KT):
                    if k % 2 == 0:
                        pe.wait_ge(sq_ready, 4 * n + k // 2 + 1)
                    m = mm(b(name)[:, 0:T], ones, sqv[:, k, :], start=k == 0, stop=k == KT - 1)
                fin(m, name)

            def to_features(src, names, skip_room=False):
                for j, name in enumerate(names):
                    room(pe, name)
                    for kk in range(2):
                        for tb in range(TB):
                            m = tr(b(name)[:, kk * T + tb * P:kk * T + tb * P + P],
                                   src[:, tb, (2 * j + kk) * P:(2 * j + kk + 1) * P], ident)
                    fin(m, name)

            pe.wait_ge(const_in, 16)
            pe.wait_ge(rows_in, 16)
            m = tr(b("gains")[:, 0:NROWS], grows, ident[0:NROWS, 0:NROWS])
            fin(m, "gains")
            pe.wait_ge(mem_in, 16)
            to_features(mem_tok, [f"mt{j}" for j in range(4)])
            pe.wait_ge(x_in, 16)
            to_features(x_tok, [f"xt{j}" for j in range(4)])
            norm_sum("n_mem")
            pe.wait_ge(bias_in, 48)
            room(pe, "bucket")
            m = mm(b("bucket")[0:8, 0:384], relb, buckets, start=True, stop=True)
            fin(m, "bucket")
            linear_f("ckv_k", mem_n, ["kc0", "kc1"], h_at=0)
            norm_sum("n_mix")
            linear_t("ckv_v", mem_n, ["vc0", "vc1"])
            pe.wait_ge(hankel_in, 16)
            for j in range(4):
                room(pe, f"bj{j}")
                m = mm(b(f"bj{j}")[:, :], rev, hankel[:, 2 * j:2 * j + 2, :], start=True, stop=True)
                fin(m, f"bj{j}")
            linear_f("qk", hn, ["qk0", "qk1"], h_at=8)
            linear_t("v", hn, ["v0", "v1"])
            pe.wait_ge(small_in, 32)
            room(pe, "alr")
            for k in range(KT):
                m = mm(b("alr")[0:16, 0:T], walr[:, k, :], hn[:, k, :], start=k == 0, stop=k == KT - 1)
            fin(m, "alr")
            emptied(pe, "alr")
            room(pe, "alpha")
            for t in range(2):
                m = mm(b("alpha")[:, T * t:T * t + T], wau[:, P * t:P * t + P], alr, start=True, stop=True)
            fin(m, "alpha")
            linear_f("r", hn, ["r0", "r1"])
            linear_f("qm", hn, ["qm0", "qm1"])
            linear_f("km", hn, ["km0", "km1"])
            linear_t("vm", hn, ["vm0", "vm1"])

            def causal_scores(name, q, k, h):
                r = 64 * (h % 2)
                room(pe, name)
                mm(b(name)[:, 0:P], q[r:r + 64, h // 2, 0:P], k[r:r + 64, h // 2, 0:P], start=True, stop=True)
                m = mm(b(name)[:, P:P + T], q[r:r + 64, h // 2, P:T], k[r:r + 64, h // 2, :], start=True, stop=True)
                fin(m, name)

            def causal_turn(name, p):
                room(pe, name)
                tr(b(name)[:, 0:P], p[:, 0:P], ident)
                tr(b(name)[:, P:T], p[:, P:T], ident)
                m = tr(b(name)[:, T:T + P], p[:, T:T + P], ident)
                fin(m, name)

            def causal_out(name, pT, v, at, width, r, last):
                mm(b(name)[r:r + width, 0:T], v[:, 0, at:at + width], pT[:, 0:T], start=True, stop=False)
                m = mm(b(name)[r:r + width, P:T], v[:, 1, at:at + width], pT[:, T:T + P], start=False, stop=True)
                if last:
                    fin(m, name)

            pe.wait_ge(gla_scaled, 4)
            room(pe, "kt")
            for tb in range(TB):
                for t in range(2):
                    m = tr(b("kt")[:, T * tb + P * t:T * tb + P * t + P], ex[2][:, t, P * tb:P * tb + P], ident)
            fin(m, "kt")
            for name in ("qm0", "qm1", "km0", "km1"):
                emptied(pe, name)
            emptied(pe, "v1")
            emptied(pe, "vm1")
            causal_scores("ms0", qm, km, 0)
            for par, name in ((0, "ae"), (1, "ao")):
                room(pe, name)
                for h in (par, 2 + par):
                    for n in range(4):
                        c = ((n // 2) * 2 + h // 2) * 64
                        r = 64 * par
                        m = mm(b(name)[64 * (n % 2):64 * (n % 2) + 64, c:c + 64],
                               ex[1][r:r + 64, h // 2, 64 * n:64 * n + 64], ex[0][r:r + 64, h // 2, 64 * n:64 * n + 64],
                               start=True, stop=True)
                fin(m, name)
            causal_scores("ms1", qm, km, 1)
            emptied(pe, "kt")
            for par, name in ((0, "ke"), (1, "ko")):
                room(pe, name)
                for n in ((0, 2) if par == 0 else (1,)):
                    for h in range(4):
                        r = 64 * par
                        c = ((n // 2) * 2 + h // 2) * P
                        m = mm(b(name)[64 * (h % 2):64 * (h % 2) + 64, c:c + P],
                               kdt[r:r + 64, n // 2, 64 * h:64 * h + 64], vg[r:r + 64, n // 2, P * h:P * h + P],
                               start=True, stop=True)
                fin(m, name)
            pe.wait_ge(prob_ready, 1)
            causal_turn("mt_0", prob[0])
            emptied(pe, "ae")
            emptied(pe, "ao")
            for par, name in ((0, "oe"), (1, "oo")):
                room(pe, name)
                r = 64 * par
                for h in range(4):
                    for tb in range(TB):
                        m = mm(b(name)[:, (2 * h + tb) * 64:(2 * h + tb) * 64 + 64], vg[r:r + 64, tb, P * h:P * h + P],
                               att[h % 2][r:r + 64, (2 * tb + h // 2) * 64:(2 * tb + h // 2) * 64 + 64],
                               start=True, stop=True)
                fin(m, name)
            emptied(pe, "ke")
            for par, name in ((0, "ie"), (1, "io")):
                room(pe, name)
                r = 64 * par
                for hp in range(2):
                    for n in range(1, 4):
                        m = mm(b(name)[:, T * hp + 64 * n:T * hp + 64 * n + 64], states[r:r + 64, n - 1, hp, :],
                               ex[3][r:r + 64, hp, 64 * n:64 * n + 64], start=True, stop=True)
                fin(m, name)
            causal_scores("ms2", qm, km, 2)
            group_f("zg0", "zg0", 0)

            def head_norm_sum(names, at):
                pe.wait_ge(hsq_ready, at)
                for i, name in enumerate(names):
                    room(pe, name)
                    m = mm(b(name)[:, :], ones, hsq[:, 2 * i:2 * i + 2, :], start=True, stop=True)
                    fin(m, name)

            head_norm_sum(["gn0", "gn1"], 1)

            def moba_out(h):
                if h % 2 == 0:
                    room(pe, f"mo{h // 2}")
                emptied(pe, f"mt_{h}")
                causal_out(f"mo{h // 2}", probT[h % 2], vm, 64 * h, 64, 64 * (h % 2), h % 2 == 1)

            moba_out(0)
            pe.wait_ge(prob_ready, 2)
            causal_turn("mt_1", prob[1])
            causal_scores("ms3", qm, km, 3)
            group_f("zg0", "zg1", 1)
            moba_out(1)
            for h in range(2, 8):
                pe.wait_ge(prob_ready, h + 1)
                causal_turn(f"mt_{h}", prob[h % 2])
                if h + 2 < 8:
                    causal_scores(f"ms{h + 2}", qm, km, h + 2)
                group_f(("zg1", "zm0", "zm1")[(h - 2) // 2], ("zg2", "zg3", "zm0", "zm1", "zm2", "zm3")[h - 2], h % 2)
                moba_out(h)

            def merge_out(sfx, chunks, o_first, wait_first, o_second, wait_second, n):
                for chunk, o, names, wait in ((chunks[0], o_first, "pa", wait_first), (chunks[1], o_second, "pb", wait_second)):
                    wait()
                    landed(pe, chunk)
                    w = tall[CHUNK[chunk][0]]
                    for j in range(4):
                        name = f"{names}{j}{sfx}"
                        room(pe, name)
                        for half in range(2):
                            for k in range(4):
                                m = mm(b(name)[:, T * half:T * half + T], w[:, k, P * (2 * j + half):P * (2 * j + half) + P],
                                       o[:, k, :], start=k == 0, stop=k == 3)
                        fin(m, name)
                pe.wait_ge(merged_ready, 4 * (n + 1))
                linear_f("out0" + sfx, z1, ["ou0" + sfx, "ou1" + sfx])
                linear_f("out1" + sfx, z1, ["ou2" + sfx, "ou3" + sfx])

            merge_out("", ["proj_gla", "proj_moba"], og, lambda: pe.wait_ge(og_ready, 1),
                      om, lambda: [emptied(pe, f"mo{i}") for i in range(4)], 0)

            norm_sum("n_cross")
            linear_f("cq", hn, ["cq0", "cq1"], h_at=16)

            def cross_scores(h):
                room(pe, f"cs{h}")
                for tb in range(TB):
                    m = mm(b(f"cs{h}")[:, T * tb:T * tb + T], qc[:, h, P * tb:P * tb + P], kc[:, h, :], start=True, stop=True)
                fin(m, f"cs{h}")

            emptied(pe, "cq0")
            emptied(pe, "cq1")
            emptied(pe, "kc0")
            emptied(pe, "kc1")
            cross_scores(0)
            for h in range(4):
                if h < 3:
                    cross_scores(h + 1)
                pe.wait_ge(prob_ready, 8 + h + 1)
                name = f"ct{h}"
                room(pe, name)
                for kb in range(2):
                    for tb in range(TB):
                        m = tr(b(name)[:, T * kb + P * tb:T * kb + P * tb + P], cprob[h % 2][:, tb, P * kb:P * kb + P], ident)
                fin(m, name)
                emptied(pe, f"ct{h}")
                emptied(pe, "vc1")
                name = f"co{h}"
                room(pe, name)
                for kb in range(2):
                    m = mm(b(name)[:, 0:T], vc[:, kb, P * h:P * h + P], cprobT[h % 2][:, T * kb:T * kb + T],
                           start=kb == 0, stop=kb == 1)
                fin(m, name)
            for h in range(4):
                emptied(pe, f"co{h}")
            landed(pe, "co")
            w = tall[CHUNK["co"][0]]
            for j in range(4):
                name = f"cw{j}"
                room(pe, name)
                for half in range(2):
                    for k in range(4):
                        m = mm(b(name)[:, T * half:T * half + T], w[:, k, P * (2 * j + half):P * (2 * j + half) + P],
                               oc[:, k, :], start=k == 0, stop=k == 3)
                fin(m, name)

            norm_sum("n_moe")
            pe.wait_ge(h_ready, 32)
            pe.wait_ge(router_in, 64)
            room(pe, "route")
            for tb in range(TB):
                for k in range(KT):
                    m = mm(b("route")[:, 36 * tb:36 * tb + 36], hn[:, k, P * tb:P * tb + P], wr[:, k, :],
                           start=k == 0, stop=k == KT - 1)
            fin(m, "route")
            pe.wait_ge(mask_ready, 1)
            room(pe, "rank")
            mm(b("rank")[:, 0:32], later, msk[:, 0, :], start=True, stop=True)
            mm(b("rank")[:, 32:64], later, msk[:, 1, :], start=True, stop=False)
            mm(b("rank")[:, 32:64], ones, msk[:, 0, :], start=False, stop=True)
            mm(b("rank")[:, 64:96], ones, msk[:, 0, :], start=True, stop=False)
            m = mm(b("rank")[:, 64:96], ones, msk[:, 1, :], start=False, stop=True)
            fin(m, "rank")
            for j in range(4):
                name = f"ht{j}"
                room(pe, name)
                for kk in range(4):
                    m = tr(b(name)[:, P * kk:P * kk + P], hn[:, 4 * (j % 2) + kk, P * (j // 2):P * (j // 2) + P], ident)
                fin(m, name)

            for bank in range(8):
                pe.wait_ge(bank_free[bank], BEFORE_EXPERTS[bank])
            pe.wait_ge(blank, 1)
            for i in range(4):
                mm(ps[4 + i][:, :], zero[0:P, 0:P], zero[:, P:P + HALF], start=True, stop=False, skip_group_check=True)

            def gather(s, n):
                pe.wait_ge(s["sel_made"], 4 * n + 4)
                for k in range(KT):
                    for tb in range(TB):
                        m = mm(ps[2 + k // 4][:, P * (k % 4):P * (k % 4) + P], htok[:, tb, P * k:P * k + P], sel[:, tb, :],
                               start=tb == 0, stop=tb == TB - 1)
                m.then_inc(s["gather_done"], 1)

            def combine():
                for tb in range(TB):
                    for half in range(2):
                        m = mm(ps[4 + 2 * tb + half][:, :], selT[:, P * tb:P * tb + P], y[:, HALF * half:HALF * half + HALF],
                               start=False, stop=False, skip_group_check=True)
                return m

            def pair(s, sl, n, g, lb):
                for up in range(2):
                    if up == 0:
                        pe.wait_ge(s["xe_a"], g + 1)
                        pe.wait_ge(s["xe_d"], g + 1)
                        pe.wait_ge(s["y0_out"], n + 1)
                    else:
                        pe.wait_ge(s["y1_out"], n + 1)
                    pe.wait_ge(sl[2 * up], n * 32 + (lb + 32))
                    pe.wait_ge(sl[2 * up + 1], n * 32 + (lb + 32))
                    for k in range(KT):
                        mm(ps[up][0:64, :], xe[:, k, 0:64], wide[2 * up][:, k, :], start=k == 0, stop=k == KT - 1)
                        m = mm(ps[up][64:128, :], xe[:, k, 64:128], wide[2 * up + 1][:, k, :], start=k == 0, stop=k == KT - 1)
                    m.then_inc(s[("gate_done", "up_done")[up]], 1)
                combine()
                gather(s, g + 1)
                pe.wait_ge(s["hid_made"], n + 1)
                for kk in range(4):
                    m = tr(ps[0][:, P * kk:P * kk + P], hid[:, P * kk:P * kk + P], ident)
                m.then_inc(s["hidT_done"], 1)
                pe.wait_ge(s["selw_made"], 4 * n + 4)
                for tb in range(TB):
                    m = tr(ps[1][:, P * tb:P * tb + P], selw[:, tb, :], ident)
                m.then_inc(s["selT_done"], 1)
                pe.wait_ge(sl[4], n * 32 + (lb + 32))
                pe.wait_ge(sl[5], n * 32 + (lb + 32))
                for half in range(2):
                    if half == 0:
                        pe.wait_ge(s["hidT_out"], n + 1)
                    else:
                        pe.wait_ge(s["selT_out"], n + 1)
                    for kk in range(4):
                        mm(ps[half][0:64, :], hidT[:, kk, 0:64], tall[4][:, kk, HALF * half:HALF * half + HALF],
                           start=kk == 0, stop=kk == 3)
                        m = mm(ps[half][64:128, :], hidT[:, kk, 64:128], tall[5][:, kk, HALF * half:HALF * half + HALF],
                               start=kk == 0, stop=kk == 3)
                    m.then_inc(s[("y0_done", "y1_done")[half]], 1)

            s = moe_sems[0]
            gather(s, 0)
            with pe.Fori(0, PAIRS) as p:
                pair(s, slot_landed, p, p, 32 * (len(FIRST_CHUNKS) // RING))
            pe.wait_ge(s["y0_out"], PAIRS + 1)
            pe.wait_ge(s["y1_out"], PAIRS + 1)
            combine().then_inc(passed, 1)
            pe.wait_ge(s["xe_a"], PAIRS + 1)
            pe.wait_ge(s["xe_d"], PAIRS + 1)
            pe.wait_ge(count_ready, 1)
            most = pe.value_load(cnt[0:1, 0:1], min_val=0, max_val=T)
            with pe.If(most > SLOTS):
                o = moe_sems[1]
                with pe.Fori(0, OVER_PASSES) as q:
                    pe.wait_ge(blank, q + 2)
                    gather(o, q * (PAIRS + 1))
                    with pe.Fori(0, PAIRS) as p:
                        n = q * PAIRS + p
                        pair(o, over_landed, n, q * (PAIRS + 1) + p, 0)
                    pe.wait_ge(o["y0_out"], q * PAIRS + (PAIRS + 1))
                    pe.wait_ge(o["y1_out"], q * PAIRS + (PAIRS + 1))
                    combine().then_inc(passed, 1)
                    pe.wait_ge(o["xe_a"], (q + 1) * (PAIRS + 1))
                    pe.wait_ge(o["xe_d"], (q + 1) * (PAIRS + 1))
            for i in range(4):
                m = mm(ps[4 + i][:, :], zero[0:P, 0:P], zero[:, P:P + HALF], start=False, stop=True, skip_group_check=True)
                fin(m, f"acc{i}")
            for i in range(4):
                emptied(pe, f"acc{i}")
            to_features(acc_sb, [f"at{j}" for j in range(4)])
            norm_sum("n_final")

            for l in range(LAYERS):
                x = f".{l}"
                norm_sum("n_attn" + x)
                linear_f("dq" + x, hn, ["dq0" + x, "dq1" + x], h_at=40 + 16 * l)
                linear_f("dk" + x, hn, ["dk0" + x, "dk1" + x])
                for name in ("dq0", "dq1", "dk0", "dk1"):
                    emptied(pe, name + x)
                pe.wait_ge(cb_in, 16)
                for i, (t, name) in enumerate(((dq, "rq"), (dk, "rk"))):
                    for j in range(2):
                        room(pe, f"{name}{j}{x}")
                        m = mm(b(f"{name}{j}{x}")[:, :], rope, t[:, 2 * j:2 * j + 2, :], start=True, stop=True)
                        fin(m, f"{name}{j}{x}")
                linear_t("dv" + x, hn, ["dv0" + x, "dv1" + x])

                def diff_scores(h):
                    for i in range(2):
                        causal_scores(f"{('ds', 'de')[i]}{h}{x}", dq, dk, 2 * h + i)

                def diff_turn(h):
                    pe.wait_ge(prob_ready, 12 + 4 * l + h + 1)
                    causal_turn(f"dt{h}{x}", p1[h % 2])

                def diff_out(h):
                    emptied(pe, f"dt{h}{x}")
                    room(pe, f"do{h}{x}")
                    causal_out(f"do{h}{x}", probT[h % 2], dv, P * h, P, 0, True)

                pe.wait_ge(rotated, 4 * (l + 1))
                diff_scores(0)
                linear_f("sq" + x, hn, ["sq0" + x, "sq1" + x])
                diff_turn(0)
                diff_scores(1)
                linear_f("sk" + x, hn, ["sk0" + x, "sk1" + x])
                emptied(pe, "dv1" + x)
                diff_out(0)
                diff_turn(1)
                diff_scores(2)
                linear_t("sv" + x, hn, ["sv0" + x, "sv1" + x])
                diff_out(1)
                diff_turn(2)
                diff_scores(3)

                def sb_scores(h):
                    name = f"bz{h}{x}"
                    r = 64 * (h % 2)
                    room(pe, name)
                    mm(b(name)[:, 0:T], bk[r:r + 64, h // 2, 0:P], bq[r:r + 64, h // 2, :], start=True, stop=True)
                    m = mm(b(name)[:, T:T + P], bk[r:r + 64, h // 2, P:T], bq[r:r + 64, h // 2, P:T], start=True, stop=True)
                    fin(m, name)

                def sb_after_sum(h):
                    name = f"ba{h}{x}"
                    room(pe, name)
                    pe.wait_ge(sb_rem, 8 * l + h + 1)
                    lr = lrem[h % 2]
                    mm(b(name)[:, 0:T], earlier, lr[:, 0:T], start=True, stop=False)
                    mm(b(name)[:, P:T], ones, lr[:, T:T + P], start=False, stop=True)
                    m = mm(b(name)[:, T:T + P], earlier, lr[:, T:T + P], start=True, stop=True)
                    fin(m, name)

                def sb_out(h):
                    if h % 2 == 0:
                        room(pe, f"bo{h // 2}{x}")
                    pe.wait_ge(sb_prob, 8 * l + h + 1)
                    causal_out(f"bo{h // 2}{x}", stick[h % 4], bv, 64 * h, 64, 64 * (h % 2), h % 2 == 1)

                for name in ("sq0", "sq1", "sk0", "sk1", "sv1"):
                    emptied(pe, name + x)
                sb_scores(0)
                group_f("ga0" + x, "ga0" + x, 0)
                diff_out(2)
                diff_turn(3)
                sb_scores(1)
                sb_after_sum(0)
                group_f("ga0" + x, "ga1" + x, 1)
                diff_out(3)
                head_norm_sum(["dn0" + x, "dn1" + x], l + 2)
                for h in range(8):
                    if h < 6:
                        sb_scores(h + 2)
                    if h < 7:
                        sb_after_sum(h + 1)
                    for name, half in GATE_HALVES[h]:
                        j = int(name[2])
                        tile_f(f"{name[:2]}{j // 2}{x}", name + x, 2 * (j % 2) + half)
                    sb_out(h)
                merge_out(x, ["proj_diff" + x, "proj_sb" + x], od, lambda: pe.wait_ge(og_ready, l + 2),
                          ob, lambda: [emptied(pe, f"bo{i}{x}") for i in range(4)], l + 1)

                norm_sum("n_ffn" + x)
                for j in range(11):
                    landed(pe, f"ffn{j}{x}")
                    w = wide[CHUNK[f"ffn{j}{x}"][0]]
                    for i, name in enumerate((f"fg{j}{x}", f"fu{j}{x}")):
                        room(pe, name)
                        for half in range(2):
                            for k in range(8):
                                if i == 0 and j == 0 and half == 0:
                                    pe.wait_ge(h_ready, 48 + 16 * l + k + 1)
                                m = mm(b(name)[:, T * half:T * half + T], w[:, k, P * (2 * i + half):P * (2 * i + half) + P],
                                       hn[:, k, :], start=k == 0, stop=k == 7)
                        fin(m, name)
                for i in range(4):
                    room(pe, f"fo{i}{x}")
                for c in range(6):
                    if c < 5:
                        landed(pe, f"down{c}{x}")
                        w, nk = tall[CHUNK[f"down{c}{x}"][0]], 4
                    else:
                        pe.wait_ge(tail_landed, 16 * (l + 1))
                        w, nk = tail_w, 2
                    for kk in range(nk):
                        f = 4 * c + kk
                        if f % 2 == 0:
                            emptied(pe, f"fu{f // 2}{x}")
                        for mt in range(8) if c < 5 else ():
                            mm(b(f"fo{mt // 2}{x}")[:, T * (mt % 2):T * (mt % 2) + T], w[:, kk, P * mt:P * mt + P],
                               hidF[:, f, :], start=f == 0 and mt % 2 == 0, stop=False, skip_group_check=True)
                for mt in range(8):
                    for kk in range(2):
                        m = mm(b(f"fo{mt // 2}{x}")[:, T * (mt % 2):T * (mt % 2) + T], tail_w[:, kk, P * mt:P * mt + P],
                               hidF[:, FT - 2 + kk, :], start=False, stop=kk == 1, skip_group_check=True)
                    if mt % 2 == 1:
                        fin(m, f"fo{mt // 2}{x}")

            norm_sum("n_last")
            pe.wait_ge(h_ready, 8 * len(NORMS))
            for j in range(4):
                name = f"yt{j}"
                room(pe, name)
                for kk in range(4):
                    m = tr(b(name)[:, P * kk:P * kk + P], hn[:, 4 * (j % 2) + kk, P * (j // 2):P * (j // 2) + P], ident)
                fin(m, name)

        @block.scalar
        def _(act):
            A = nc.scalar.activation
            chain = [0]

            def link(ins):
                chain[0] += 1
                ins.then_inc(act_chain, 1)
                act.wait_ge(act_chain, chain[0])

            act.dma_start(walr, a["w_in"][0][:, 1536:1552].rearrange("(k p) n -> p k n", p=P)).then_inc(small_in, 16)
            act.dma_start(wau, a["w_alpha_up"][0]).then_inc(small_in, 16)
            act.dma_start(wr[:, :, 0:4], a["w_router_group"][0].rearrange("(k p) n -> p k n", p=P)).then_inc(router_in, 16)
            act.dma_start(wr[:, :, 4:36], a["w_router_expert"][0].rearrange("(k p) n -> p k n", p=P)).then_inc(router_in, 16)
            act.dma_start(brow[:, 0:4], bass.AP(a["b_router_group"].tensor, 0, [[0, P], [1, 4]])).then_inc(router_in, 16)
            act.dma_start(brow[:, 4:36], bass.AP(a["b_router_expert"].tensor, 0, [[0, P], [1, 32]])).then_inc(router_in, 16)

            act.wait_ge(eps_ready, 1)

            def take(name, dst, scale=1.0, func=ACT.Copy):
                full(act, name)
                n = dst.shape[-1] if len(dst.shape) == 3 else None
                src = b(name)[:, :] if n is None else b(name)[:, :].rearrange("p (a b) -> p a b", b=n)
                freed(A(dst, src, func, scale=scale), name)

            def two(t, j):
                return t[:, 2 * j:2 * j + 2, :]

            def norm_squares(name, src, made=None):
                n = NORMS.index(name)
                if n:
                    act.wait_ge(h_ready, 8 * n)
                for j in range(4):
                    if made:
                        emptied(act, made[j])
                    A(two(view(SQ, 0, KT, T), j), two(src, j), ACT.Square).then_inc(sq_ready, 1)

            def norm_root(name):
                full(act, name)
                freed(A(SQ[:, 0:T], b(name)[:, 0:T], ACT.Sqrt, bias=eps_col, scale=1.0 / D), name)

            def head_roots(names):
                for i, name in enumerate(names):
                    full(act, name)
                    freed(A(hroot[:, 2 * i:2 * i + 2, :], b(name)[:, :].rearrange("p (a b) -> p a b", b=T), ACT.Sqrt,
                            bias=eps_col, scale=1.0 / P), name)

            for j in range(4):
                take(f"mt{j}", two(mem_f, j))
            norm_squares("n_mem", mem_f, [f"mt{j}" for j in range(4)])
            norm_root("n_mem")
            norm_squares("n_mix", xres, [f"xt{j}" for j in range(4)])
            take("kc0", two(kc, 0))
            take("kc1", two(kc, 1))
            norm_root("n_mix")
            take("vc0", vc[:, 0, :])
            take("vc1", vc[:, 1, :])
            for j in range(4):
                take(f"bj{j}", two(bias, j))
            take("qk0", qg, scale=64 ** -0.5)
            take("qk1", kg)
            emptied(act, "alpha")
            link(A(t1, za, ACT.Abs))
            link(A(t1, t1, ACT.Exp, scale=-1.0))
            A(t1, t1, ACT.Ln, bias=1.0).then_inc(gla_softplus, 1)
            take("r0", two(rg, 0), func=ACT.Silu)
            take("r1", two(rg, 1), func=ACT.Silu)
            take("qm0", two(qm, 0))
            take("qm1", two(qm, 1))
            act.wait_ge(gla_diffs, 1)
            for i, (src, scale) in enumerate(((dmid, 1), (dmid, -1), (dlast, -1), (bcum, 1))):
                A(ex[i], src, ACT.Exp, scale=scale / 16.0).then_inc(gla_exps, 1)

            def nm(i, j):
                return sm[:, 4 + 8 * (i % 2) + j:5 + 8 * (i % 2) + j]

            def sums(i, j):
                return sm[:, 20 + 8 * (i % 2) + j:21 + 8 * (i % 2) + j]

            def causal_exp(i, bufs):
                act.wait_ge(logit_ready, i + 1)
                for j, p in enumerate(bufs):
                    A(p[:, 0:P], p[:, 0:P], ACT.Exp, bias=nm(i, 2 * j), accum_out=sums(i, 2 * j))
                    last = A(p[:, P:384], p[:, P:384], ACT.Exp, bias=nm(i, 2 * j + 1), accum_out=sums(i, 2 * j + 1))
                last.then_inc(exp_ready, 1)

            def take_turned(name, i):
                full(act, name)
                freed(A(probT[i % 2], b(name)[:, 0:384], ACT.Copy), name)

            take("kt", kdt.rearrange("p a b -> p (a b)"))
            causal_exp(0, [prob[0]])
            causal_exp(1, [prob[1]])
            take_turned("mt_0", 0)
            take("zg0", two(z1, 0))
            head_roots(["gn0", "gn1"])
            take_turned("mt_1", 1)
            causal_exp(2, [prob[0]])
            causal_exp(3, [prob[1]])
            take("zg1", two(z1, 1))
            for h in range(2, 8):
                take_turned(f"mt_{h}", h)
                if h + 2 < 8:
                    causal_exp(h + 2, [prob[h % 2]])
                take(("zg2", "zg3", "zm0", "zm1", "zm2", "zm3")[h - 2], two(z1, h) if h < 4 else two(z2, h - 4))

            def sigmoids(names):
                for z, name in ((z1, names[0]), (z2, names[1])):
                    emptied(act, name)
                    A(z, z, ACT.Sigmoid).then_inc(z_sig, 1)

            sigmoids(["zg3", "zm3"])

            norm_squares("n_cross", xres, [f"ou{j}" for j in range(4)])
            norm_root("n_cross")
            take("cq0", two(qc, 0))
            take("cq1", two(qc, 1))

            def cross_exp(h):
                i = 8 + h
                full(act, f"cs{h}")
                act.wait_ge(logit_ready, i + 1)
                for tb in range(TB):
                    last = A(cprob[h % 2][:, tb, :], b(f"cs{h}")[:, T * tb:T * tb + T], ACT.Exp, bias=nm(i, tb),
                             scale=P ** -0.5, accum_out=sums(i, tb))
                freed(last, f"cs{h}")

            cross_exp(0)
            for h in range(4):
                if h < 3:
                    cross_exp(h + 1)
                take(f"ct{h}", cprobT[h % 2])
            norm_squares("n_moe", xres, [f"cw{j}" for j in range(4)])
            norm_root("n_moe")

            act.wait_ge(route_diff, 1)
            A(e4, d4, ACT.Exp).then_inc(route_exp, 1)
            act.wait_ge(route_diff, 2)
            A(ex2, dm, ACT.Exp).then_inc(route_exp, 1)
            for j in range(4):
                take(f"ht{j}", htok[:, j // 2, HALF * (j % 2):HALF * (j % 2) + HALF])

            def take_gather(s, g):
                act.wait_ge(s["gather_done"], g + 1)
                A(xe[:, 4:8, :], ps[3][:, :].rearrange("p (a b) -> p a b", b=P), ACT.Copy).then_inc(s["xe_a"], 1)

            def act_pair(s, n, g):
                act.wait_ge(s["gate_done"], n + 1)
                A(gsil, ps[0][:, :], ACT.Silu).then_inc(s["silu_made"], 1)
                take_gather(s, g + 1)
                act.wait_ge(s["hidT_done"], n + 1)
                A(hidT, ps[0][:, :].rearrange("p (a b) -> p a b", b=P), ACT.Copy).then_inc(s["hidT_out"], 1)
                act.wait_ge(s["y0_done"], n + 1)
                A(y[:, 0:HALF], ps[0][:, :], ACT.Copy).then_inc(s["y0_out"], 1)

            s = moe_sems[0]
            take_gather(s, 0)
            with act.Fori(0, PAIRS) as p:
                act_pair(s, p, p)
            act.wait_ge(count_ready, 1)
            most = act.value_load(cnt[0:1, 0:1], min_val=0, max_val=T)
            with act.If(most > SLOTS):
                o = moe_sems[1]
                with act.Fori(0, OVER_PASSES) as q:
                    take_gather(o, q * (PAIRS + 1))
                    with act.Fori(0, PAIRS) as p:
                        act_pair(o, q * PAIRS + p, q * (PAIRS + 1) + p)
            for i in range(2):
                take(f"acc{i}", acc_sb[:, 0, HALF * i:HALF * i + HALF])
            norm_squares("n_final", xres, [f"at{j}" for j in range(4)])
            norm_root("n_final")

            for l in range(LAYERS):
                x = f".{l}"
                norm_squares("n_attn" + x, xres, [f"fo{j}.{l - 1}" for j in range(4)] if l else None)
                norm_root("n_attn" + x)
                if l == 0:
                    act.wait_ge(lam_sums, 1)
                    A(lam_e, lam_s, ACT.Exp).then_inc(lam_exps, 1)
                for i, t in (("dq", dq), ("dk", dk)):
                    take(i + "0" + x, two(t, 0))
                    take(i + "1" + x, two(t, 1))
                i0 = 12 + 4 * l

                def diff_exp(h):
                    causal_exp(i0 + h, [p1[h % 2], p2[h % 2]])

                def sb_softplus(h):
                    full(act, f"bz{h}{x}")
                    link(A(stick[h % 4], b(f"bz{h}{x}")[:, 0:384], ACT.Abs, scale=64 ** -0.5))
                    link(A(stick[h % 4], stick[h % 4], ACT.Exp, scale=-1.0))
                    A(stick[h % 4], stick[h % 4], ACT.Ln, bias=1.0).then_inc(sb_logs, 1)

                def sb_weights(h):
                    emptied(act, f"ba{h}{x}")
                    A(stick[h % 4], lbeta[h % 2], ACT.Exp).then_inc(sb_exp, 1)

                def gates(names, z, g0, row):
                    for j, name in enumerate(names):
                        full(act, name)
                        for half in range(2):
                            last = A(z[:, 2 * (g0 + j) + half, :], b(name)[:, T * half:T * half + T], ACT.Identity,
                                     bias=gain("b_gate_2", 16 * l + row + 2 * (g0 + j) + half))
                        freed(last, name)

                diff_exp(0)
                take("sq0" + x, two(bq, 0))
                take("sq1" + x, two(bq, 1))
                take_turned("dt0" + x, 0)
                diff_exp(1)
                take("sk0" + x, two(bk, 0))
                take("sk1" + x, two(bk, 1))
                take_turned("dt1" + x, 1)
                diff_exp(2)
                take_turned("dt2" + x, 0)
                diff_exp(3)
                sb_softplus(0)
                gates(["ga0" + x], z1, 0, 0)
                take_turned("dt3" + x, 1)
                sb_softplus(1)
                sb_weights(0)
                gates(["ga1" + x], z1, 1, 0)
                head_roots(["dn0" + x, "dn1" + x])
                for h in range(8):
                    if h < 6:
                        sb_softplus(h + 2)
                    if h < 7:
                        sb_weights(h + 1)
                    for name, half in GATE_HALVES[h]:
                        if half:
                            g = int(name[2])
                            gates([name + x], *((z1, g, 0) if name[1] == "a" else (z2, g, 8)))
                sigmoids(["ga3" + x, "gb3" + x])
                norm_squares("n_ffn" + x, xres, [f"ou{j}{x}" for j in range(4)])
                norm_root("n_ffn" + x)
                for j in range(11):
                    take(f"fg{j}{x}", two(hidF, j), func=ACT.Silu)
            norm_squares("n_last", xres, [f"fo{j}.{LAYERS - 1}" for j in range(4)])
            norm_root("n_last")
            for j in range(2):
                take(f"yt{j}", y_out[:, 0, HALF * j:HALF * j + HALF])

        @block.vector
        def _(dve):
            v = nc.vector
            chain = [0]

            def link(ins):
                chain[0] += 1
                ins.then_inc(dve_chain, 1)
                dve.wait_ge(dve_chain, chain[0])

            def two(t, j):
                return t[:, 2 * j:2 * j + 2, :]

            def src_of(name, dst):
                return b(name)[:, :] if len(dst.shape) == 2 else b(name)[:, :].rearrange("p (a b) -> p a b", b=dst.shape[-1])

            def take(name, dst):
                full(dve, name)
                freed(v.tensor_copy(dst, src_of(name, dst)), name)

            def residual(names):
                for j, name in enumerate(names):
                    full(dve, name)
                    freed(v.tensor_tensor(two(xres, j), src_of(name, two(xres, j)), two(xres, j), ALU.add), name)

            def norm_apply(name, src, dst, row, at=0):
                emptied(dve, name)
                link(v.reciprocal(SQ[:, 0:T], SQ[:, 0:T]))
                for k in range(KT):
                    v.scalar_tensor_tensor(dst[:, k, :], src[:, k, :], gain(row, at + k), SQ[:, 0:T], ALU.mult, ALU.mult).then_inc(h_ready, 1)

            v.memset(eps_col, EPS).then_inc(eps_ready, 1)
            v.memset(urow, -BIG).then_inc(urow_masked, 1)
            full(dve, "gains")
            freed(v.tensor_copy(gcol[:, 0:NROWS], b("gains")[:, 0:NROWS]), "gains")
            for j in range(4):
                take(f"xt{j}", two(xres, j))
            emptied(dve, "gains")
            norm_apply("n_mem", mem_f, mem_n, "g_mem")
            full(dve, "bucket")
            dve.wait_ge(urow_masked, 1)
            freed(v.tensor_copy(urow[:, 0:T], b("bucket")[0:8, 0:T]), "bucket")
            for j in range(4):
                emptied(dve, f"xt{j}")
            norm_apply("n_mix", xres, hn, "g_mix")
            take("v0", vg[:, 0, :])
            take("v1", vg[:, 1, :])
            full(dve, "alr")
            freed(v.tensor_copy(alr, b("alr")[0:16, 0:T]), "alr")
            full(dve, "alpha")
            for t in range(2):
                last = v.tensor_scalar(za[:, t, :], b("alpha")[:, T * t:T * t + T], gain("b_alpha", t), None, ALU.add)
            freed(last, "alpha")
            dve.wait_ge(gla_softplus, 1)
            link(v.scalar_tensor_tensor(t1, za, 0.0, t1, ALU.min, ALU.subtract))
            for t in range(2):
                for n in range(4):
                    last = v.tensor_tensor_scan(bcum[:, t, 64 * n:64 * n + 64], ones[:, 0:64], t1[:, t, 64 * n:64 * n + 64],
                                                0.0, ALU.mult, ALU.add)
            link(last)

            def chunks(t):
                return t.rearrange("p a (n c) -> p (a n) c", c=64)

            v.tensor_tensor(chunks(dmid), chunks(bcum), chunks(bcum)[:, :, 31:32].to_broadcast([P, 8, 64]), ALU.subtract)
            v.tensor_tensor(chunks(dlast), chunks(bcum), chunks(bcum)[:, :, 63:64].to_broadcast([P, 8, 64]), ALU.subtract).then_inc(gla_diffs, 1)
            take("km0", two(km, 0))
            take("km1", two(km, 1))
            take("vm0", vm[:, 0, :])
            take("vm1", vm[:, 1, :])
            dve.wait_ge(gla_exps, 4)
            emptied(dve, "qk0")
            emptied(dve, "qk1")
            decay = sm[:, 52:60].rearrange("p (a n) -> p a n", n=4)
            link(v.tensor_copy(decay, ex[3].rearrange("p a (n c) -> p a n c", c=64)[:, :, :, 63]))
            for i, t in enumerate((qg, kg, kg, qg)):
                v.tensor_tensor(ex[i], ex[i], t, ALU.mult).then_inc(gla_scaled, 1)
            v.memset(att[0], 0.0)
            link(v.memset(att[1], 0.0))

            def nm(i, j, n=1):
                return sm[:, 4 + 8 * (i % 2) + j:4 + n + 8 * (i % 2) + j]

            def sums(i, j, n=1):
                return sm[:, 20 + 8 * (i % 2) + j:20 + n + 8 * (i % 2) + j]

            def recs(i, j, n=1):
                return sm[:, 36 + 8 * (i % 2) + j:36 + n + 8 * (i % 2) + j]

            def maxima(i, j, p):
                v.reduce_max(nm(i, j), p[:, 0:P], AX, negate=True)
                return v.reduce_max(nm(i, j + 1), p[:, P:384], AX, negate=True)

            def moba_logits(h):
                p = prob[h % 2]
                full(dve, f"ms{h}")
                v.scalar_tensor_tensor(p[:, 0:P], b(f"ms{h}")[:, 0:P], 64 ** -0.5, bias[:, h, P:T], ALU.mult, ALU.add)
                freed(v.scalar_tensor_tensor(p[:, P:384], b(f"ms{h}")[:, P:384], 64 ** -0.5, bias[:, h, :], ALU.mult, ALU.add), f"ms{h}")
                emptied(dve, f"ms{h}")
                maxima(h, 0, p).then_inc(logit_ready, 1)

            def moba_norm(h):
                p = prob[h % 2]
                dve.wait_ge(exp_ready, h + 1)
                link(v.reciprocal(recs(h, 0, 2), sums(h, 0, 2)))
                v.tensor_scalar(p[:, 0:P], p[:, 0:P], recs(h, 0), None, ALU.mult)
                v.tensor_scalar(p[:, P:384], p[:, P:384], recs(h, 1), None, ALU.mult).then_inc(prob_ready, 1)

            for j in range(4):
                emptied(dve, f"bj{j}")
            moba_logits(0)
            for i, name in enumerate(("ae", "ao")):
                full(dve, name)
                mask = m64.bitcast(U32).rearrange("p (a c) -> p a c", a=1).to_broadcast([P, 8, 64])
                freed(v.copy_predicated(att[i].rearrange("p (a c) -> p a c", c=64), mask,
                                        b(name)[:, :].rearrange("p (a c) -> p a c", c=64)), name)
            moba_logits(1)
            full(dve, "ke")
            full(dve, "ko")
            link(v.tensor_copy(states[:, 0, :, :], b("ke")[:, 0:T].rearrange("p (a b) -> p a b", b=P)))
            for hp in range(2):
                last = v.scalar_tensor_tensor(states[:, 1, hp, :], states[:, 0, hp, :], decay[:, hp, 1:2],
                                              b("ko")[:, P * hp:P * hp + P], ALU.mult, ALU.add)
            freed(last, "ko")
            emptied(dve, "ko")
            for hp in range(2):
                last = v.scalar_tensor_tensor(states[:, 2, hp, :], states[:, 1, hp, :], decay[:, hp, 2:3],
                                              b("ke")[:, T + P * hp:T + P * hp + P], ALU.mult, ALU.add)
            freed(last, "ke")
            moba_norm(0)
            moba_norm(1)
            og5 = og.rearrange("p h (t e c) -> p (h t) e c", e=2, c=64)
            for e, name in enumerate(("oe", "oo")):
                full(dve, name)
                freed(v.tensor_copy(og5[:, :, e, :], b(name)[:, :].rearrange("p (a c) -> p a c", c=64)), name)
                emptied(dve, name)
            for e, name in enumerate(("ie", "io")):
                full(dve, name)
                o2 = og[:, e:4:2, 64:T]
                freed(v.tensor_tensor(o2, b(name)[:, :].rearrange("p (a c) -> p a c", c=T)[:, :, 64:T], o2, ALU.add), name)
                emptied(dve, name)

            def head_squares(o):
                v.tensor_tensor(hsq, o, o, ALU.mult).then_inc(hsq_ready, 1)

            def head_apply(o, names, cols):
                for name in names:
                    emptied(dve, name)
                link(v.reciprocal(hroot, hroot))
                for h in range(4):
                    last = v.scalar_tensor_tensor(o[:, h, :], o[:, h, :], cols[h], hroot[:, h, :], ALU.mult, ALU.mult)
                return last

            head_squares(og)
            full(dve, "mt_0")
            moba_logits(2)
            link(head_apply(og, ["gn0", "gn1"], [gain("g_gla_head", h) for h in range(4)]))
            emptied(dve, "r0")
            emptied(dve, "r1")
            v.tensor_tensor(og, og, rg, ALU.mult).then_inc(og_ready, 1)
            full(dve, "mt_1")
            moba_logits(3)
            for h in range(2, 8):
                moba_norm(h)
                if h % 2 == 0:
                    name = f"mo{h // 2 - 1}"
                    full(dve, name)
                    freed(v.tensor_copy(om[:, h // 2 - 1, :], b(name)[:, 0:T]), name)
                if h + 2 < 8:
                    full(dve, f"mt_{h}")
                    moba_logits(h + 2)
            full(dve, "mo3")
            freed(v.tensor_copy(om[:, 3, :], b("mo3")[:, 0:T]), "mo3")

            def merge(x, n):
                for z, names, c in ((z1, "pa", 2 * n + 1), (z2, "pb", 2 * n + 2)):
                    dve.wait_ge(z_sig, c)
                    for j in range(4):
                        name = f"{names}{j}{x}"
                        full(dve, name)
                        freed(v.tensor_tensor(two(z, j), src_of(name, two(z, j)), two(z, j), ALU.mult), name)
                        if names == "pb":
                            emptied(dve, name)
                            v.tensor_tensor(two(z1, j), two(z1, j), two(z2, j), ALU.add).then_inc(merged_ready, 1)
                residual([f"ou{j}{x}" for j in range(4)])

            for j in range(4):
                emptied(dve, f"zg{j}")
            merge("", 0)

            for j in range(4):
                emptied(dve, f"ou{j}")
            norm_apply("n_cross", xres, hn, "g_cross")

            def cross_max(h):
                i = 8 + h
                full(dve, f"cs{h}")
                link(v.reduce_max(nm(i, 0, 2), b(f"cs{h}")[:, :].rearrange("p (a c) -> p a c", c=T), AX, negate=True))
                v.tensor_scalar(nm(i, 0, 2), nm(i, 0, 2), P ** -0.5, None, ALU.mult).then_inc(logit_ready, 1)

            def take_co(h):
                full(dve, f"co{h}")
                freed(v.tensor_copy(oc[:, h, :], b(f"co{h}")[:, 0:T]), f"co{h}")

            cross_max(0)
            for h in range(4):
                i = 8 + h
                if h < 3:
                    cross_max(h + 1)
                emptied(dve, f"cs{h}")
                link(v.reciprocal(recs(i, 0, 2), sums(i, 0, 2)))
                for tb in range(TB):
                    last = v.tensor_scalar(cprob[h % 2][:, tb, :], cprob[h % 2][:, tb, :], recs(i, tb), None, ALU.mult)
                last.then_inc(prob_ready, 1)
                if h:
                    take_co(h - 1)
            take_co(3)
            residual([f"cw{j}" for j in range(4)])
            for j in range(4):
                emptied(dve, f"cw{j}")
            norm_apply("n_moe", xres, hn, "g_moe")

            dve.wait_ge(router_in, 64)
            full(dve, "route")
            freed(v.tensor_tensor(lg, b("route")[:, 0:72].rearrange("p (a c) -> p a c", c=36),
                                  brow.rearrange("p (a c) -> p a c", a=1).to_broadcast([P, TB, 36]), ALU.add), "route")
            emptied(dve, "route")

            def bc(t, n):
                return t.to_broadcast([P, TB, n])

            def first_of(dst, value, top, n, t):
                link(v.tensor_tensor(t, value, bc(top, n), ALU.is_equal))
                link(v.tensor_scalar(t, t, -100.0, None, ALU.mult))
                link(v.tensor_tensor(t, t, i100[:, 0:n].rearrange("p (a c) -> p a c", a=1).to_broadcast([P, TB, n]), ALU.add))
                link(v.tensor_reduce(rmin, t, AX, ALU.min))
                link(v.tensor_tensor(dst, t, bc(rmin, n), ALU.is_equal))

            lg4 = lg[:, :, 0:4]
            link(v.reduce_max(gm, lg4, AX))
            v.tensor_tensor(d4, lg4, bc(gm, 4), ALU.subtract).then_inc(route_diff, 1)
            first_of(oh4, lg4, gm, 4, t4)
            for tb in range(TB):
                last = v.tensor_tensor(eg[:, tb, :].rearrange("p (g e) -> p g e", g=4),
                                       lg[:, tb, 4:36].rearrange("p (g e) -> p g e", g=4),
                                       oh4[:, tb, :].rearrange("p (g a) -> p g a", a=1).to_broadcast([P, 4, 8]), ALU.mult)
            link(last)
            for tb in range(TB):
                last = v.reduce_sum(ein[:, tb, :], eg[:, tb, :].rearrange("p (g e) -> p e g", g=4), AX)
            link(last)
            link(v.reduce_max(m1, ein, AX))
            first_of(oh1, ein, m1, 8, t8)
            link(v.scalar_tensor_tensor(ein2, oh1, -BIG, ein, ALU.mult, ALU.add))
            link(v.reduce_max(m2, ein2, AX))
            v.tensor_tensor(dm, m2, m1, ALU.subtract).then_inc(route_diff, 1)
            first_of(oh2, ein2, m2, 8, t8)
            dve.wait_ge(route_exp, 2)
            link(v.reduce_sum(pg, e4, AX))
            link(v.tensor_scalar(dm, ex2, 1.0, None, ALU.add))
            link(v.tensor_tensor(pg, pg, dm, ALU.mult))
            link(v.reciprocal(w1, pg))
            link(v.tensor_tensor(w2, w1, ex2, ALU.mult))
            link(v.tensor_tensor(t8, oh1, bc(w1, 8), ALU.mult))
            link(v.tensor_tensor(w8, oh2, bc(w2, 8), ALU.mult))
            link(v.tensor_tensor(w8, w8, t8, ALU.add))
            link(v.tensor_tensor(m8, oh1, oh2, ALU.add))
            for dst, s8, s_done in ((wgt, w8, None), (msk, m8, mask_ready)):
                for tb in range(TB):
                    last = v.tensor_tensor(dst[:, tb, :].rearrange("p (g e) -> p g e", g=4),
                                           oh4[:, tb, :].rearrange("p (g a) -> p g a", a=1).to_broadcast([P, 4, 8]),
                                           s8[:, tb, :].rearrange("p (a e) -> p a e", a=1).to_broadcast([P, 4, 8]), ALU.mult)
                if s_done is not None:
                    last.then_inc(s_done, 1)
            v.memset(zero, 0.0)
            v.memset(y[:, 0:HALF], 0.0).then_inc(moe_sems[0]["y0_out"], 1)
            v.memset(y[:, HALF:D], 0.0).then_inc(moe_sems[0]["y1_out"], 1)
            v.memset(selT, 0.0).then_inc(blank, 1)
            v.memset(key, 0.0).then_inc(keys_ready, 1)
            dve.wait_ge(keys_ready, 1)
            full(dve, "rank")
            dve.wait_ge(mask_ready, 1)
            v.scalar_tensor_tensor(key[:, :, 0:NE], b("rank")[:, 0:64].rearrange("p (a c) -> p a c", c=NE), 1.0, msk,
                                   ALU.add, ALU.mult)
            link(v.reduce_max(gm[:, 0, :], b("rank")[:, 64:96], AX))
            freed(v.tensor_copy(cnt[:, :], gm[:, 0, :]), "rank")
            emptied(dve, "rank")
            v.tensor_scalar(key, key, -1.0, None, ALU.add).then_inc(count_ready, 1)
            dve.wait_ge(count_ready, 1)

            def select(s, e):
                for tb in range(TB):
                    for j in range(2):
                        v.tensor_scalar(sel[:, tb, 64 * j:64 * j + 64], iota[:, 0:64], key[:, tb, bass.ds(e + j, 1)], None,
                                        ALU.is_equal).then_inc(s["sel_made"], 1)

            def take_gather(s, g):
                dve.wait_ge(s["gather_done"], g + 1)
                v.tensor_copy(xe[:, 0:4, :], ps[2][:, :].rearrange("p (a b) -> p a b", b=P)).then_inc(s["xe_d"], 1)

            def dve_pair(s, n, g, p):
                dve.wait_ge(s["gather_done"], g + 1)
                select(s, 2 * p + 2)
                dve.wait_ge(s["up_done"], n + 1)
                dve.wait_ge(s["silu_made"], n + 1)
                v.tensor_tensor(hid, ps[1][:, :], gsil, ALU.mult).then_inc(s["hid_made"], 1)
                for tb in range(TB):
                    for j in range(2):
                        v.tensor_scalar(selw[:, tb, 64 * j:64 * j + 64], iota[:, 0:64], key[:, tb, bass.ds(2 * p + j, 1)],
                                        wgt[:, tb, bass.ds(2 * p + j, 1)], ALU.is_equal, ALU.mult).then_inc(s["selw_made"], 1)
                take_gather(s, g + 1)
                dve.wait_ge(s["selT_done"], n + 1)
                v.tensor_copy(selT, ps[1][:, 0:T]).then_inc(s["selT_out"], 1)
                dve.wait_ge(s["y1_done"], n + 1)
                v.tensor_copy(y[:, HALF:D], ps[1][:, :]).then_inc(s["y1_out"], 1)

            s = moe_sems[0]
            select(s, 0)
            take_gather(s, 0)
            with dve.Fori(0, PAIRS) as p:
                dve_pair(s, p, p, p)
            most = dve.value_load(cnt[0:1, 0:1], min_val=0, max_val=T)
            with dve.If(most > SLOTS):
                o = moe_sems[1]
                v.memset(sm[:, 1:2], 0.0).then_inc(o["y0_out"], 1)
                v.memset(sm[:, 2:3], 0.0).then_inc(o["y1_out"], 1)
                with dve.Fori(0, OVER_PASSES) as q:
                    dve.wait_ge(passed, q + 1)
                    v.memset(selT, 0.0).then_inc(blank, 1)
                    v.tensor_scalar(iota, iota, float(SLOTS), None, ALU.add).then_inc(iota_moved, 1)
                    dve.wait_ge(iota_moved, q + 1)
                    select(o, 0)
                    take_gather(o, q * (PAIRS + 1))
                    with dve.Fori(0, PAIRS) as p:
                        dve_pair(o, q * PAIRS + p, q * (PAIRS + 1) + p, p)
            for i in range(2):
                take(f"acc{2 + i}", acc_sb[:, 1, HALF * i:HALF * i + HALF])
            residual([f"at{j}" for j in range(4)])
            for j in range(4):
                emptied(dve, f"at{j}")
            norm_apply("n_final", xres, xres, "g_final")
            dve.wait_ge(lam_in, 16)
            lp = lamt.rearrange("p (a b) c -> p a b c", b=2)
            link(v.tensor_tensor(lamt[:, 0:8:2, :], lamt[:, 0:8:2, :], lamt[:, 1:8:2, :], ALU.mult))
            v.reduce_sum(lam_s, lamt[:, 0:8:2, :], AX).then_inc(lam_sums, 1)

            for l in range(LAYERS):
                x = f".{l}"
                lam_init = 0.8 - 0.6 * math.exp(-0.3 * l)
                norm_apply("n_attn" + x, xres, hn, "norm_attn_2", 8 * l)
                if l == 0:
                    dve.wait_ge(lam_exps, 1)
                link(v.tensor_tensor(lam[:, l:l + 1], lam_e[:, 2 * l:2 * l + 1], lam_e[:, 2 * l + 1:2 * l + 2], ALU.subtract))
                link(v.tensor_scalar(lam[:, l:l + 1], lam[:, l:l + 1], lam_init, None, ALU.add))
                link(v.tensor_scalar(subs, gain("diff_subln_2", l), 1.0 - lam_init, None, ALU.mult))
                dve.wait_ge(cb_in, 16)
                for j, (t, name) in enumerate(((dq, "rq0"), (dq, "rq1"), (dk, "rk0"), (dk, "rk1"))):
                    tt = two(t, j % 2)
                    tmp = TMP[:, 512 * (j % 2):512 * (j % 2) + 512].rearrange("p (a b) -> p a b", b=T)
                    full(dve, name + x)
                    freed(v.tensor_tensor(tmp, src_of(name + x, tmp), sinT.rearrange("p (a b) -> p a b", a=1).to_broadcast([P, 2, T]), ALU.mult), name + x)
                    link(v.tensor_tensor(tt, tt, cosT.rearrange("p (a b) -> p a b", a=1).to_broadcast([P, 2, T]), ALU.mult))
                    v.tensor_tensor(tt, tt, tmp, ALU.add).then_inc(rotated, 1)
                take("dv0" + x, dv[:, 0, :])
                take("dv1" + x, dv[:, 1, :])
                i0 = 12 + 4 * l

                def diff_logits(h):
                    for j, (p, name) in enumerate(((p1[h % 2], f"ds{h}{x}"), (p2[h % 2], f"de{h}{x}"))):
                        full(dve, name)
                        freed(v.scalar_tensor_tensor(p, b(name)[:, 0:384], 64 ** -0.5, causal, ALU.mult, ALU.add), name)
                        emptied(dve, name)
                        last = maxima(i0 + h, 2 * j, p)
                    last.then_inc(logit_ready, 1)

                def diff_norm(h):
                    i = i0 + h
                    dve.wait_ge(exp_ready, i - 4 + 1)
                    link(v.reciprocal(recs(i, 0, 4), sums(i, 0, 4)))
                    link(v.tensor_scalar(recs(i, 2, 2), recs(i, 2, 2), lam[:, l:l + 1], None, ALU.mult))
                    for j, (at, to) in enumerate(((0, P), (P, 384))):
                        last = v.tensor_scalar(p2[h % 2][:, at:to], p2[h % 2][:, at:to], recs(i, 2 + j), None, ALU.mult)
                    link(last)
                    for j, (at, to) in enumerate(((0, P), (P, 384))):
                        last = v.scalar_tensor_tensor(p1[h % 2][:, at:to], p1[h % 2][:, at:to], recs(i, j), p2[h % 2][:, at:to],
                                                      ALU.mult, ALU.subtract)
                    last.then_inc(prob_ready, 1)

                def take_do(h):
                    full(dve, f"do{h}{x}")
                    freed(v.tensor_copy(od[:, h, :], b(f"do{h}{x}")[:, 0:T]), f"do{h}{x}")

                def sb_logs_of(h):
                    name = f"bz{h}{x}"
                    dve.wait_ge(sb_logs, 8 * l + h + 1)
                    lb, lr = lbeta[h % 2], lrem[h % 2]
                    link(v.tensor_scalar(lb, b(name)[:, 0:384], 64 ** -0.5, 0.0, ALU.mult, ALU.min))
                    link(v.tensor_tensor(lb, lb, stick[h % 4], ALU.subtract))
                    freed(v.scalar_tensor_tensor(lr, b(name)[:, 0:384], -(64 ** -0.5), lb, ALU.mult, ALU.add), name)
                    emptied(dve, name)
                    v.tensor_tensor(lr, lr, strict, ALU.mult).then_inc(sb_rem, 1)

                def sb_add(h):
                    name = f"ba{h}{x}"
                    full(dve, name)
                    freed(v.tensor_tensor(lbeta[h % 2], b(name)[:, 0:384], lbeta[h % 2], ALU.add), name)

                def sb_mask(h):
                    dve.wait_ge(sb_exp, 8 * l + h + 1)
                    v.tensor_tensor(stick[h % 4], stick[h % 4], strict, ALU.mult).then_inc(sb_prob, 1)

                diff_logits(0)
                diff_norm(0)
                diff_logits(1)
                diff_norm(1)
                take_do(0)
                full(dve, "dt0" + x)
                diff_logits(2)
                take("sv0" + x, bv[:, 0, :])
                take("sv1" + x, bv[:, 1, :])
                diff_norm(2)
                take_do(1)
                full(dve, "dt1" + x)
                diff_logits(3)
                diff_norm(3)
                sb_logs_of(0)
                take_do(2)
                sb_logs_of(1)
                sb_add(0)
                sb_mask(0)
                take_do(3)
                emptied(dve, "do3" + x)
                head_squares(od)
                for h in range(8):
                    if h < 6:
                        sb_logs_of(h + 2)
                    if h < 7:
                        sb_add(h + 1)
                        sb_mask(h + 1)
                    if h == 0:
                        head_apply(od, ["dn0" + x, "dn1" + x], [subs] * 4).then_inc(og_ready, 1)
                    if h % 2 == 1:
                        name = f"bo{h // 2}{x}"
                        full(dve, name)
                        freed(v.tensor_copy(ob[:, h // 2, :], b(name)[:, 0:T]), name)
                merge(x, l + 1)
                for j in range(4):
                    emptied(dve, f"ou{j}{x}")
                norm_apply("n_ffn" + x, xres, hn, "norm_ffn_2", 8 * l)
                for j in range(11):
                    emptied(dve, f"fg{j}{x}")
                    full(dve, f"fu{j}{x}")
                    freed(v.tensor_tensor(two(hidF, j), src_of(f"fu{j}{x}", two(hidF, j)), two(hidF, j), ALU.mult), f"fu{j}{x}")
                residual([f"fo{j}{x}" for j in range(4)])
                for j in range(4):
                    emptied(dve, f"fo{j}{x}")
            norm_apply("n_last", xres, hn, "norm_final_2")
            for j in range(2, 4):
                take(f"yt{j}", y_out[:, 1, HALF * (j % 2):HALF * (j % 2) + HALF])


_INS = ["x", "mem", "g_mem", "rel_bias", "g_mix", "w_in", "w_alpha_up", "b_alpha", "g_gla_head", "w_proj_gla",
        "w_proj_moba", "w_out", "g_cross", "w_cq", "w_ckv", "w_co", "g_moe", "w_router_group", "b_router_group",
        "w_router_expert", "b_router_expert", "w_exp_gate", "w_exp_up", "w_exp_down", "g_final", "norm_attn_2",
        "w_in_2", "b_gate_2", "diff_lambda_2", "diff_subln_2", "w_o_diff_2", "w_o_sb_2", "w_out_2", "norm_ffn_2",
        "w_ffn_in_2", "w_ffn_out_2", "norm_final_2"]


def kernel(**inputs):
    import concourse.bacc as bacc
    from concourse.bass_utils import run_bass_kernel_spmd

    nc = bacc.Bacc("TRN2", target_bir_lowering=False, num_devices=1)
    arrays, aps = {}, {}
    data = {n: np.ascontiguousarray(inputs[n]) for n in _INS}
    data["gains"] = np.concatenate([data.pop(n).reshape(-1, P) for n in ROWS])
    data["consts"] = constants()
    for n, v in data.items():
        arrays[f"in_{n}"] = v
        aps[n] = nc.dram_tensor(f"in_{n}", v.shape, mybir.dt.from_np(v.dtype), kind="ExternalInput").ap()
    out = nc.dram_tensor("out_0", (1, T, D), F32, kind="ExternalOutput").ap()
    build(nc, aps, out)
    r = run_bass_kernel_spmd(nc, [arrays], core_ids=[0])
    return r.results[0]["out_0"]
```

```python
import math
from contextlib import ExitStack

import concourse.bass as bass
import numpy as np
from concourse import mybir

F32 = mybir.dt.float32
F32R = mybir.dt.float32r
BF16 = mybir.dt.bfloat16
I32 = mybir.dt.int32
U32 = mybir.dt.uint32
ALU = mybir.AluOpType
ACT = mybir.ActivationFunctionType
AX = mybir.AxisListType.X

P = 128
T = 256
TB = T // P
D = 1024
KT = D // P
EPS = 1e-6
BIG = 1.0e30
HALF = 512

NE = 32
PAIRS = NE // 2
SLOTS = 64
OVER_PASSES = T // SLOTS - 1
KEYS = NE + 2

FFN = 2816
FT = FFN // P
RING = 6
LAYERS = 2

CA = dict(ident=(0, 128), later=(128, 128), earlier=(256, 128), ones=(384, 128), m64=(512, 64), iota=(576, 128),
          i100=(704, 8))
CA_W = 712
CB = dict(rope=(0, 128), cos=(128, 256), sin=(384, 256), causal=(640, 384), strict=(1024, 384))
CB_W = 1408
CC = dict(rev=(0, 128), buckets=(128, 384))
CC_W = 512

ROWS = {}
_n = 0
for _name, _k in (("g_mem", 8), ("g_mix", 8), ("g_cross", 8), ("g_moe", 8), ("g_final", 8), ("g_gla_head", 4),
                  ("b_alpha", 2), ("norm_attn_2", 16), ("norm_ffn_2", 16), ("b_gate_2", 32), ("diff_subln_2", 2),
                  ("norm_final_2", 8)):
    ROWS[_name] = (_n, _k)
    _n += _k
NROWS = _n


def constants():
    i = np.arange(P)
    c = np.zeros((P, CA_W + CB_W + CC_W), np.float32)

    def put(base, table, name, value):
        at, n = table[name]
        c[:value.shape[0], base + at:base + at + n] = value

    put(0, CA, "ident", np.eye(P))
    put(0, CA, "later", (i[:, None] < i[None, :]).astype(np.float32))
    put(0, CA, "earlier", (i[:, None] > i[None, :]).astype(np.float32))
    put(0, CA, "ones", np.ones((P, P)))
    put(0, CA, "m64", ((i % 64)[:, None] <= np.arange(64)[None, :]).astype(np.float32))
    put(0, CA, "iota", np.tile(np.arange(P) % SLOTS, (P, 1)))
    put(0, CA, "i100", np.tile(np.arange(8) + 100, (P, 1)))
    rope = np.zeros((P, P))
    for h in range(0, P, 64):
        for d in range(32):
            rope[h + 32 + d, h + d] = -1.0
            rope[h + d, h + 32 + d] = 1.0
    inv = np.float32(10000.0) ** (-np.arange(0, 64, 2, dtype=np.float32) / np.float32(64))
    ang = np.arange(T, dtype=np.float32)[None, :] * inv[i % 32][:, None]
    put(CA_W, CB, "rope", rope)
    put(CA_W, CB, "cos", np.cos(ang))
    put(CA_W, CB, "sin", np.sin(ang))
    q = np.arange(P)[:, None]
    diag = np.where(i[None, :] <= q, 0.0, -BIG)
    put(CA_W, CB, "causal", np.concatenate([diag, np.zeros((P, P)), diag], 1))
    strict = (i[:, None] < i[None, :]).astype(np.float32)
    put(CA_W, CB, "strict", np.concatenate([strict, np.ones((P, P)), strict], 1))
    put(CA_W + CB_W, CC, "rev", np.eye(P)[::-1])
    dist = (T - 1) - np.arange(384)
    n = np.maximum(dist, 0)
    large = 16 + (np.log(np.maximum(n, 1) / 16) / math.log(8) * 16).astype(np.int64)
    bucket = np.where(n < 16, n, np.minimum(large, 31))
    put(CA_W + CB_W, CC, "buckets", ((bucket[None, :] == np.arange(32)[:, None]) & (dist >= 0)[None, :]).astype(np.float32))
    return c


GATE_HALVES = [[] for _ in range(8)]
for _i in range(12):
    GATE_HALVES[2 * (_i // 3) + (_i % 3 == 2)].append((("ga2", "ga3", "gb0", "gb1", "gb2", "gb3")[_i // 2], _i % 2))


def group_plan():
    g = ["gains", "mt0", "mt1", "mt2", "mt3", "xt0", "xt1", "xt2", "xt3", "n_mem", "bucket",
         "kc0", "kc1", "n_mix", "vc0", "vc1", "bj0", "bj1", "bj2", "bj3"]
    g += ["qk0", "qk1", "alr", "v0", "v1", "alpha", "r0", "r1", "qm0", "qm1", "km0", "km1", "vm0", "vm1"]
    g += ["kt", "ms0", "ae", "ao", "ms1", "ke", "ko", "mt_0", "oe", "oo", "ie", "io", "ms2"]
    g += ["zg0", "gn0", "gn1", "mo0", "mt_1", "ms3", "zg1"]
    for h in range(2, 8):
        g += [f"mt_{h}"]
        if h + 2 < 8:
            g += [f"ms{h + 2}"]
        g += [("zg2", "zg3", "zm0", "zm1", "zm2", "zm3")[h - 2]]
        if h % 2 == 0:
            g += [f"mo{h // 2}"]
    g += [f"pa{i}" for i in range(4)] + [f"pb{i}" for i in range(4)] + [f"ou{i}" for i in range(4)]
    g += ["n_cross", "cq0", "cq1"] + [f"cs{h}" for h in range(4)]
    g += ["ct0", "ct1", "co0", "ct2", "co1", "ct3", "co2", "co3"]
    g += [f"cw{i}" for i in range(4)]
    g += ["n_moe", "routeT", "route"] + [f"ht{i}" for i in range(4)] + ["rank"]
    first = list(g)
    second = [f"at{i}" for i in range(4)] + ["n_final"]
    for l in range(LAYERS):
        s = ["n_attn", "dq0", "dq1", "dk0", "dk1", "rq0", "rq1", "rk0", "rk1", "dv0", "dv1", "ds0", "de0",
             "sq0", "sq1", "dt0", "ds1", "de1", "sk0", "sk1", "do0", "dt1", "ds2", "de2", "sv0", "sv1", "do1",
             "dt2", "ds3", "de3", "bz0", "bz1", "ga0", "do2", "dt3", "ba0", "ga1", "do3"]
        for h in range(8):
            if h in (0, 2, 4):
                s += [f"bz{h + 2}", f"bz{h + 3}"]
            if h < 7:
                s += [f"ba{h + 1}"]
            s += [name for name, half in GATE_HALVES[h] if half == 0]
            if h == 0:
                s += ["dn0", "dn1"]
            if h % 2 == 0:
                s += [f"bo{h // 2}"]
        s += [f"pa{i}" for i in range(4)] + [f"pb{i}" for i in range(4)] + [f"ou{i}" for i in range(4)]
        s += ["n_ffn"]
        for j in range(11):
            s += [f"fg{j}", f"fu{j}"]
        s += [f"fo{i}" for i in range(4)]
        second += [f"{n}.{l}" for n in s]
    second += ["n_last"] + [f"yt{i}" for i in range(4)]
    plan, use = {}, [0] * 8
    bank = 0
    for name in first:
        plan[name] = (bank, use[bank])
        use[bank] += 1
        bank = (bank + 1) % 8
    before_experts = list(use)
    for i in range(4):
        plan[f"acc{i}"] = (4 + i, use[4 + i])
        use[4 + i] += 1
    bank = 0
    for name in second:
        plan[name] = (bank, use[bank])
        use[bank] += 1
        bank = (bank + 1) % 8
    return plan, before_experts


PLAN, BEFORE_EXPERTS = group_plan()

FIRST_CHUNKS = [("ckv_k", "kc1"), ("ckv_v", "vc1"), ("qk", "qk1"), ("v", "v1"), ("r", "r1"), ("qm", "qm1"),
                ("km", "km1"), ("vm", "vm1"), ("zg0", "zg1"), ("zg1", "zg3"), ("zm0", "zm1"), ("zm1", "zm3"),
                ("proj_gla", "pa3"), ("proj_moba", "pb3"), ("out0", "ou1"), ("out1", "ou3"), ("cq", "cq1"),
                ("co", "cw3")]
LAYER_CHUNKS = ([("dq", "dq1"), ("dk", "dk1"), ("dv", "dv1"), ("sq", "sq1"), ("sk", "sk1"), ("sv", "sv1"),
                 ("ga0", "ga1"), ("ga1", "ga3"), ("gb0", "gb1"), ("gb1", "gb3"), ("proj_diff", "pa3"),
                 ("proj_sb", "pb3"), ("out0", "ou1"), ("out1", "ou3")]
                + [(f"ffn{j}", f"fu{j}") for j in range(11)] + [(f"down{j}", "fo3") for j in range(5)])
RAW = 2
assert len(FIRST_CHUNKS) % RAW == 0 and len(LAYER_CHUNKS) % RAW == 0
MOE_USES = PAIRS
CHUNK = {}
LAST_GROUP = {}
for _i, (_name, _g) in enumerate(FIRST_CHUNKS):
    CHUNK[_name] = (_i % RAW, _i // RAW)
    LAST_GROUP[_name] = _g
for _l in range(LAYERS):
    for _i, (_name, _g) in enumerate(LAYER_CHUNKS):
        CHUNK[f"{_name}.{_l}"] = (_i % RAW, len(FIRST_CHUNKS) // RAW + MOE_USES + _l * len(LAYER_CHUNKS) // RAW + _i // RAW)
        LAST_GROUP[f"{_name}.{_l}"] = f"{_g}.{_l}"
ALL_CHUNKS = list(CHUNK)
SPLIT = [n for n in ALL_CHUNKS if not n.startswith(("ckv", "proj", "cq", "co"))]

NORMS = ["n_mem", "n_mix", "n_cross", "n_moe", "n_final", "n_attn.0", "n_ffn.0", "n_attn.1", "n_ffn.1", "n_last"]
SPLIT_NORMS = ["n_mix", "n_attn.0", "n_ffn.0", "n_attn.1", "n_ffn.1"]


def build(nc, a, out):
    with ExitStack() as ctx:
        def sb(name, shape, dt=F32):
            return ctx.enter_context(nc.sbuf_tensor(name, shape, dt))

        def sem(name):
            return ctx.enter_context(nc.semaphore(name))

        tail = sb("tail", [P, 2048])
        xres = sb("xres", [P, KT, T])
        hn = sb("hn", [P, KT, T])
        hnr = sb("hnr", [P, 2, KT, T], F32R)
        ca = sb("ca", [P, CA_W])
        cb = sb("cb", [P, CB_W])
        gcol = sb("gcol", [P, 128])
        SQ = sb("SQ", [P, 2048])
        TMP = sb("TMP", [P, 1536])
        sm = sb("sm", [P, 96])
        cnt = sb("cnt", [P, 1], I32)
        with ExitStack() as over:
            G, SZ, KV, ring = (over.enter_context(nc.sbuf_tensor(n, [P, w], F32)) for n, w in (
                ("G", 6144),
                ("SZ", 4096),
                ("KV", 2048),
                ("ring", RING * 4096)))
            ring = ring[:, :].rearrange("p (s n) -> p s n", s=RING)
        Gr = sb("Gr", [P, 6144], F32R)
        SKr = sb("SKr", [P, 6144], F32R)
        sb("raw_space", [P, RAW * 4096])
        parts = sb("parts", [P, 4, 4096], F32R)
        ps = [ctx.enter_context(nc.psum_tensor(f"bank{i}", [P, HALF], F32)) for i in range(8)]
        hankel_dram = nc.dram_tensor("hankel_rows", (8, 384), F32, kind="Internal").ap()

        def view(t, at, *dims):
            n = int(np.prod(dims))
            v = t[:, at:at + n]
            if len(dims) == 2:
                return v.rearrange("p (a b) -> p a b", b=dims[1])
            if len(dims) == 3:
                return v.rearrange("p (a b c) -> p a b c", b=dims[1], c=dims[2])
            return v

        def const(tile, table, name):
            at, n = table[name]
            return tile[:, at:at + n]

        ident, later, earlier, ones, m64, iota, i100 = (const(ca, CA, n) for n in CA)
        rope, cosT, sinT, causal, strict = (const(cb, CB, n) for n in CB)
        eps_col = sm[:, 0:1]

        def gain(name, k):
            at, n = ROWS[name]
            return gcol[:, at + k:at + k + 1]

        wide = [ring[:, s, :].rearrange("p (k n) -> p k n", k=8) for s in range(RING)]
        tall = [ring[:, s, :].rearrange("p (k n) -> p k n", k=4) for s in range(RING)]
        tail_w = view(tail, 0, 2, 1024)

        def part(chunk, which):
            name = chunk.split(".")[0]
            k = 4 if name.startswith("down") else 8
            return parts[:, 2 * (SPLIT.index(chunk) % 2) + which, :].rearrange("p (k n) -> p k n", k=k)

        hn_parts = (hnr[:, 0], hnr[:, 1])
        z_parts = (view(SKr, 2048, KT, T), view(SKr, 0, KT, T))
        hid_parts = (view(Gr, 0, FT, T), view(SKr, 0, FT, T))
        hid_raw = [view(TMP, 512 * i, 2, T) for i in range(3)]

        root = TMP[:, 0:T]
        ffn_root = SQ[:, 1024:1280]

        mem_tok = hn[:, :, :].rearrange("p a b -> p (a b)").rearrange("p (a b) -> p a b", a=2)
        x_tok = view(G, 4096, 2, 1024)
        mem_f, mem_n = view(SZ, 0, KT, T), view(G, 2048, KT, T)
        hankel = view(SZ, 2048, 8, T)
        rev, buckets, urow = G[:, 0:128], G[0:32, 128:512], G[0:8, 512:896]
        relb = G[0:32, 896:904]
        grows = G[0:NROWS, 1024:1152]
        bias = view(tail, 0, 8, T)
        kc, vc = view(KV, 0, 4, T), view(KV, 1024, TB, HALF)
        qg, kg, vg, rg = view(G, 0, 2, T), view(G, 512, 2, T), view(G, 1024, TB, HALF), view(G, 2048, 4, T)
        qm, km, vm = view(G, 3072, 4, T), view(G, 4096, 4, T), view(G, 5120, TB, HALF)
        og, om = view(G, 0, 4, T), qm
        walr, wau = view(cb, 0, KT, 16), cb[0:16, 128:384]
        wr, brow = view(cb, 384, KT, 36), cb[:, 672:708]
        alr = cb[0:16, 708:964]
        za, t1, bcum, dmid = (view(SZ, 512 * i, 2, T) for i in range(4))
        dlast = za
        ex = [view(SZ, 2048 + 512 * i, 2, T) for i in range(4)]
        att = [view(SZ, 1024 + 512 * i, HALF) for i in range(2)]
        states = view(SZ, 0, 3, 2, P)
        kdt = view(SQ, 0, TB, 2 * P)
        z1, z2 = view(SZ, 0, KT, T), view(SZ, 2048, KT, T)
        hsq, hroot = view(SQ, 0, 4, T), view(SQ, 1024, 4, T)
        prob = [TMP[:, 384 * i:384 * i + 384] for i in range(2)]
        probT = [TMP[:, 768 + 384 * i:768 + 384 * i + 384] for i in range(2)]
        stick = [TMP[:, 384 * i:384 * i + 384] for i in range(4)]
        qc, oc = view(G, 0, 4, T), view(G, 1024, 4, T)
        cprob = [view(G, at, TB, T) for at in (2048, 2560, 4096, 4608)]
        cprobT = [view(G, 3072 + 512 * i, HALF) for i in range(2)]
        htok = view(G, 0, TB, D)
        xe = view(G, 2048, KT, P)
        y = G[:, 3072:4096]
        acc_sb = view(G, 4096, TB, D)
        sel, selw = view(SZ, 0, TB, P), view(SZ, 256, TB, P)
        selT = SZ[:, 512:768]
        gsil, hid, hidT = SZ[:, 768:1280], SZ[:, 1280:1792], view(SZ, 1792, 4, P)
        key, wgt, msk = view(SZ, 2304, TB, KEYS), view(SZ, 2372, TB, NE), view(SZ, 2436, TB, NE)
        lg = view(SZ, 2500, TB, 36)
        zero = SZ[:, 2600:2920].bitcast(BF16)
        rt = SZ[:, 3300:3600]
        lgT = SZ[0:36, 3600:3856]
        def small(at, n):
            return view(rt, at, TB, n)

        d4, e4, t4, oh4, eg = small(0, 4), small(8, 4), small(16, 4), small(24, 4), small(32, 32)
        ein, ein2, t8, oh1, oh2, w8, m8 = (small(96 + 16 * i, 8) for i in range(7))
        gm, rmin, m1, m2, dm, ex2, pg, w1, w2 = (small(208 + 2 * i, 1) for i in range(9))
        lam_s, lam_e, lam, subs = sm[:, 64:68], sm[:, 68:72], sm[:, 72:74], sm[:, 74:75]
        dq, dk, dv = view(G, 0, 4, T), view(G, 1024, 4, T), view(G, 2048, TB, HALF)
        bq, bk, bv = view(G, 3072, 4, T), view(G, 4096, 4, T), view(G, 5120, TB, HALF)
        od, ob = dq, bq
        p1 = [KV[:, 384 * i:384 * i + 384] for i in range(2)]
        p2 = [KV[:, 768 + 384 * i:768 + 384 * i + 384] for i in range(2)]
        lbeta = [tail[:, 384 * i:384 * i + 384] for i in range(2)]
        lrem = [tail[:, 768 + 384 * i:768 + 384 * i + 384] for i in range(2)]
        lamt = view(KV, 1536, LAYERS * 4, 64)
        y_out = view(G, 0, TB, D)

        bank_full = [sem(f"bank_full{i}") for i in range(8)]
        bank_free = [sem(f"bank_free{i}") for i in range(8)]
        slot_landed = [sem(f"slot_landed{i}") for i in range(RING)]
        over_landed = [sem(f"over_landed{i}") for i in range(RING)]
        tail_landed, const_in, rows_in, mem_in, x_in, bias_in, small_in, router_in, cb_in, lam_in = (
            sem(n) for n in ("tail_landed", "const_in", "rows_in", "mem_in", "x_in", "bias_in", "small_in",
                             "router_in", "cb_in", "lam_in"))
        urow_masked, urow_stored, hankel_in = sem("urow_masked"), sem("urow_stored"), sem("hankel_in")
        high_made, low_made, down_used = sem("high_parts_made"), sem("low_parts_made"), sem("down_chunk_used")
        hn_high, hn_split, z_high, z_split = sem("hn_high"), sem("hn_split"), sem("z_high"), sem("z_split")
        hid_high, hid_split = sem("hid_high"), sem("hid_split")
        hid_silu, hid_scaled = sem("hid_silu"), sem("hid_scaled")
        xg_ready, xg_high, xg_split = sem("x_by_gain"), sem("x_by_gain_high"), sem("x_by_gain_split")
        dve_chain, act_chain = sem("dve_chain"), sem("act_chain")
        eps_ready, sq_ready, h_ready = sem("eps_ready"), sem("sq_ready"), sem("h_ready")
        gla_softplus, gla_diffs, gla_exps, gla_scaled = (sem(n) for n in ("gla_softplus", "gla_diffs", "gla_exps", "gla_scaled"))
        hsq_ready, og_ready, merged_ready = sem("hsq_ready"), sem("og_ready"), sem("merged_ready")
        logit_ready, exp_ready, prob_ready = sem("logit_ready"), sem("exp_ready"), sem("prob_ready")
        z_sig, rotated = sem("z_sigmoid"), sem("rotated")
        route_diff, route_exp, mask_ready, keys_ready, count_ready = (sem(n) for n in (
            "route_diff", "route_exp", "mask_ready", "keys_ready", "count_ready"))
        blank, passed, iota_moved = sem("blank"), sem("passed"), sem("iota_moved")
        sb_logs, sb_rem, sb_exp, sb_prob = (sem(n) for n in ("sb_logs", "sb_rem", "sb_exp", "sb_prob"))
        lam_sums, lam_exps, out_done = sem("lam_sums"), sem("lam_exps"), sem("out_done")
        moe_sems = []
        for tag in ("", "over_"):
            moe_sems.append({n: sem(tag + n) for n in (
                "gate_done", "up_done", "gather_done", "hidT_done", "selT_done", "y0_done", "y1_done",
                "silu_made", "hid_made", "sel_made", "selw_made", "xe_a", "xe_d", "hidT_out", "selT_out", "y0_out", "y1_out")})

        def b(name):
            return ps[PLAN[name][0]]

        def full(eng, name):
            eng.wait_ge(bank_full[PLAN[name][0]], PLAN[name][1] + 1)

        def room(eng, name):
            if PLAN[name][1]:
                eng.wait_ge(bank_free[PLAN[name][0]], PLAN[name][1])

        def fin(ins, name):
            ins.then_inc(bank_full[PLAN[name][0]], 1)

        def emptied(eng, name):
            eng.wait_ge(bank_free[PLAN[name][0]], PLAN[name][1] + 1)

        def freed(ins, name):
            ins.then_inc(bank_free[PLAN[name][0]], 1)

        def used(eng, name):
            if name.startswith("down"):
                eng.wait_ge(down_used, 5 * int(name[-1]) + int(name[4]) + 1)
            else:
                full(eng, LAST_GROUP[name])

        def landed(eng, name):
            slot, use = CHUNK[name]
            eng.wait_ge(slot_landed[slot], 32 * (use + 1))

        block = ctx.enter_context(nc.Block())

        @block.sync
        def _(sp):
            w_in, w_in2 = a["w_in"][0], a["w_in_2"]
            sp.dma_start(ca[:, :], a["consts"][:, 0:CA_W]).then_inc(const_in, 16)
            sp.dma_start(grows, a["gains"]).then_inc(rows_in, 16)
            sp.dma_start(mem_tok, a["mem"][0].rearrange("(t p) n -> p t n", p=P)).then_inc(mem_in, 16)
            sp.dma_start(x_tok, a["x"][0].rearrange("(t p) n -> p t n", p=P)).then_inc(x_in, 16)
            sp.dma_start(relb, a["rel_bias"][:, :]).then_inc(bias_in, 16)
            sp.dma_start(rev, a["consts"][:, CA_W + CB_W:CA_W + CB_W + 128]).then_inc(bias_in, 16)
            sp.dma_start(buckets, a["consts"][0:32, CA_W + CB_W + 128:CA_W + CB_W + 512]).then_inc(bias_in, 16)

            def cols(w, at, n=HALF):
                return w[:, at:at + n].rearrange("(k p) n -> p k n", p=P)

            def rows4(w, at=0):
                return w[at:at + 512, :].rearrange("(k p) n -> p k n", p=P)

            def fetch(slot, dst, src, k):
                h = k // 2
                sp.dma_start(dst[:, 0:h], src[:, 0:h]).then_inc(slot_landed[slot], 16)
                sp.dma_start(dst[:, h:k], src[:, h:k]).then_inc(slot_landed[slot], 16)

            def released(name):
                i = ALL_CHUNKS.index(name)
                before = ALL_CHUNKS[i - RAW] if i >= RAW else None
                if before in SPLIT:
                    sp.wait_ge(low_made, 2 * SPLIT.index(before) + 2)
                elif before:
                    used(sp, before)

            offs = dict(qk=0, v=512, r=1024, qm=1552, km=2064, vm=2576, zg0=3088, zg1=3600, zm0=4112, zm1=4624)
            for i, (name, _) in enumerate(FIRST_CHUNKS):
                slot = i % RAW
                released(name)
                if name in offs:
                    fetch(slot, wide[slot], cols(w_in, offs[name]), 8)
                elif name in ("proj_gla", "proj_moba"):
                    fetch(slot, tall[slot], rows4(a["w_" + name][0]), 4)
                elif name in ("out0", "out1"):
                    fetch(slot, wide[slot], cols(a["w_out"][0], HALF * (name == "out1")), 8)
                elif name in ("ckv_k", "ckv_v"):
                    fetch(slot, wide[slot], cols(a["w_ckv"][0], HALF * (name == "ckv_v")), 8)
                elif name == "cq":
                    fetch(slot, wide[slot], cols(a["w_cq"][0], 0), 8)
                else:
                    fetch(slot, tall[slot], rows4(a["w_co"][0]), 4)

            def expert_pair(p, sems, before):
                for slot in ORDER:
                    w = (a["w_exp_down"], a["w_exp_gate"], a["w_exp_up"])[slot // 2][0]
                    k, dst = (8, wide[slot]) if slot >= 2 else (4, tall[slot])
                    src = w[2 * p + slot % 2].rearrange("(k p) n -> p k n", p=P)
                    before(slot)
                    h = k // 2
                    sp.dma_start(dst[:, 0:h], src[:, 0:h]).then_inc(sems[slot], 16)
                    sp.dma_start(dst[:, h:k], src[:, h:k]).then_inc(sems[slot], 16)

            def dense_used(slot):
                used(sp, ("cq", "co", "out0", "out0", "out1", "out1")[slot])

            ORDER = (2, 3, 4, 5, 0, 1)
            m = moe_sems[0]
            uses = ("y1_done", "y1_done", "gate_done", "gate_done", "up_done", "up_done")
            expert_pair(0, slot_landed, dense_used)
            with sp.Fori(1, PAIRS) as p:
                expert_pair(p, slot_landed, lambda slot: sp.wait_ge(m[uses[slot]], p))

            for slot in range(RING):
                sp.wait_ge(m[uses[slot]], PAIRS)
            sp.wait_ge(count_ready, 1)
            most = sp.value_load(cnt[0:1, 0:1], min_val=0, max_val=T)
            with sp.If(most > SLOTS):
                o = moe_sems[1]
                expert_pair(0, over_landed, lambda slot: None)
                with sp.Fori(1, OVER_PASSES * PAIRS) as i:
                    expert_pair(i % PAIRS, over_landed, lambda slot: sp.wait_ge(o[uses[slot]], i))
                for slot in range(RING):
                    sp.wait_ge(o[uses[slot]], OVER_PASSES * PAIRS)

            for l in range(LAYERS):
                off2 = dict(dq=0, dk=512, dv=1024, sq=1536, sk=2048, sv=2560, ga0=3072, ga1=3584, gb0=4096, gb1=4608)
                for i, (name, _) in enumerate(LAYER_CHUNKS):
                    slot = i % RAW
                    if l or i >= RAW:
                        released(f"{name}.{l}")
                    if name in off2:
                        fetch(slot, wide[slot], cols(w_in2[l], off2[name]), 8)
                    elif name == "proj_diff":
                        fetch(slot, tall[slot], rows4(a["w_o_diff_2"][l]), 4)
                    elif name == "proj_sb":
                        fetch(slot, tall[slot], rows4(a["w_o_sb_2"][l]), 4)
                    elif name in ("out0", "out1"):
                        fetch(slot, wide[slot], cols(a["w_out_2"][l], HALF * (name == "out1")), 8)
                    elif name[:3] == "ffn":
                        j = int(name[3:])
                        w = a["w_ffn_in_2"][l]
                        for half in range(2):
                            sp.dma_start(wide[slot][:, :, 256 * half:256 * half + 256],
                                         cols(w, FFN * half + 256 * j, 256)).then_inc(slot_landed[slot], 16)
                    else:
                        fetch(slot, tall[slot], rows4(a["w_ffn_out_2"][l], 512 * int(name[4:])), 4)
                    if name == "down0":
                        full(sp, f"pb3.{l}")
                        sp.dma_start(tail_w, a["w_ffn_out_2"][l][2560:2816, :].rearrange("(k p) n -> p k n", p=P)).then_inc(tail_landed, 16)
            for tb in range(TB):
                emptied(sp, f"yt{2 * tb}")
                emptied(sp, f"yt{2 * tb + 1}")
                sp.dma_start(out[0, tb * P:(tb + 1) * P, :], y_out[:, tb, :]).then_inc(out_done, 16)
            sp.wait_ge(out_done, 32)

        @block.gpsimd
        def _(pool):
            pool.wait_ge(urow_masked, 1)
            emptied(pool, "bucket")
            pool.dma_start(hankel_dram[:, :], urow).then_inc(urow_stored, 16)
            pool.wait_ge(urow_stored, 16)
            pool.dma_start(hankel, bass.AP(hankel_dram.tensor, 0, [[1, P], [384, 8], [1, T]])).then_inc(hankel_in, 16)
            full(pool, "rank")
            pool.dma_start(cb[:, :], a["consts"][:, CA_W:CA_W + CB_W]).then_inc(cb_in, 16)
            pool.dma_start(lamt, bass.AP(a["diff_lambda_2"].tensor, 0, [[0, P], [1, LAYERS * 256]])
                           ).then_inc(lam_in, 16)

        @block.tensor
        def _(pe):
            mm, tr = nc.tensor.matmul, nc.tensor.transpose

            def linear_f(chunk, src, names, h_at):
                landed(pe, chunk)
                w = wide[CHUNK[chunk][0]]
                for j, name in enumerate(names):
                    room(pe, name)
                    for half in range(2):
                        mt = 2 * j + half
                        for k in range(KT):
                            if mt == 0:
                                pe.wait_ge(h_ready, h_at + k + 1)
                            m = mm(b(name)[:, T * half:T * half + T], w[:, k, P * mt:P * mt + P], src[:, k, :],
                                   start=k == 0, stop=k == KT - 1)
                    fin(m, name)

            PASSES = ((0, 1), (0, 0), (1, 0))

            def ready(chunk, k, nk=8):
                if k % (nk // 2) == 0:
                    pe.wait_ge(low_made, 2 * SPLIT.index(chunk) + k // (nk // 2) + 1)

            def split_tile(chunk, src, name, mt, fresh=None):
                half = mt % 2
                if half == 0:
                    room(pe, name)
                for k in range(KT):
                    ready(chunk, k)
                    if fresh and k % 2 == 0:
                        pe.wait_ge(fresh[0], fresh[1] + k // 2 + 1)
                    for i, (ws, xs) in enumerate(PASSES):
                        m = mm(b(name)[:, T * half:T * half + T], part(chunk, ws)[:, k, P * mt:P * mt + P], src[xs][:, k, :],
                               start=k == 0 and i == 0, stop=k == KT - 1 and i == 2)
                if half:
                    fin(m, name)

            def split_f(chunk, src, names, fresh=None):
                for j, name in enumerate(names):
                    split_tile(chunk, src, name, 2 * j, fresh if j == 0 else None)
                    split_tile(chunk, src, name, 2 * j + 1)

            def hn_fresh(name):
                return hn_split, 4 * SPLIT_NORMS.index(name)

            def group_f(chunk, name, j):
                split_tile(chunk, hn_parts, name, 2 * j)
                split_tile(chunk, hn_parts, name, 2 * j + 1)

            def split_t(chunk, names):
                for tb, name in enumerate(names):
                    room(pe, name)
                    for k in range(KT):
                        ready(chunk, k)
                        for i, (xs, ws) in enumerate(PASSES):
                            m = mm(b(name)[:, :], hn_parts[xs][:, k, P * tb:P * tb + P], part(chunk, ws)[:, k, :],
                                   start=k == 0 and i == 0, stop=k == KT - 1 and i == 2)
                    fin(m, name)

            def linear_t(chunk, src, names):
                landed(pe, chunk)
                w = wide[CHUNK[chunk][0]]
                for tb, name in enumerate(names):
                    room(pe, name)
                    for k in range(8):
                        m = mm(b(name)[:, :], src[:, k, P * tb:P * tb + P], w[:, k, :], start=k == 0, stop=k == 7)
                    fin(m, name)

            def norm_sum(name):
                n = NORMS.index(name)
                room(pe, name)
                sqv = view(SQ, 0, KT, T)
                for k in range(KT):
                    if k % 2 == 0:
                        pe.wait_ge(sq_ready, 4 * n + k // 2 + 1)
                    m = mm(b(name)[:, 0:T], ones, sqv[:, k, :], start=k == 0, stop=k == KT - 1)
                fin(m, name)

            def to_features(src, names):
                for j, name in enumerate(names):
                    room(pe, name)
                    for kk in range(2):
                        for tb in range(TB):
                            m = tr(b(name)[:, kk * T + tb * P:kk * T + tb * P + P],
                                   src[:, tb, (2 * j + kk) * P:(2 * j + kk + 1) * P], ident)
                    fin(m, name)

            pe.wait_ge(const_in, 16)
            pe.wait_ge(rows_in, 16)
            m = tr(b("gains")[:, 0:NROWS], grows, ident[0:NROWS, 0:NROWS])
            fin(m, "gains")
            pe.wait_ge(mem_in, 16)
            to_features(mem_tok, [f"mt{j}" for j in range(4)])
            pe.wait_ge(x_in, 16)
            to_features(x_tok, [f"xt{j}" for j in range(4)])
            norm_sum("n_mem")
            pe.wait_ge(bias_in, 48)
            room(pe, "bucket")
            m = mm(b("bucket")[0:8, 0:384], relb, buckets, start=True, stop=True)
            fin(m, "bucket")
            linear_f("ckv_k", mem_n, ["kc0", "kc1"], h_at=0)
            norm_sum("n_mix")
            linear_t("ckv_v", mem_n, ["vc0", "vc1"])
            pe.wait_ge(hankel_in, 16)
            for j in range(4):
                room(pe, f"bj{j}")
                m = mm(b(f"bj{j}")[:, :], rev, hankel[:, 2 * j:2 * j + 2, :], start=True, stop=True)
                fin(m, f"bj{j}")
            split_f("qk", hn_parts, ["qk0", "qk1"], hn_fresh("n_mix"))
            pe.wait_ge(small_in, 32)
            room(pe, "alr")
            for k in range(KT):
                m = mm(b("alr")[0:16, 0:T], walr[:, k, :], hn[:, k, :], start=k == 0, stop=k == KT - 1)
            fin(m, "alr")
            split_t("v", ["v0", "v1"])
            emptied(pe, "alr")
            room(pe, "alpha")
            for t in range(2):
                m = mm(b("alpha")[:, T * t:T * t + T], wau[:, P * t:P * t + P], alr, start=True, stop=True)
            fin(m, "alpha")
            split_f("r", hn_parts, ["r0", "r1"])
            split_f("qm", hn_parts, ["qm0", "qm1"])
            split_f("km", hn_parts, ["km0", "km1"])
            split_t("vm", ["vm0", "vm1"])

            def causal_scores(name, q, k, h):
                r = 64 * (h % 2)
                room(pe, name)
                mm(b(name)[:, 0:P], q[r:r + 64, h // 2, 0:P], k[r:r + 64, h // 2, 0:P], start=True, stop=True)
                m = mm(b(name)[:, P:P + T], q[r:r + 64, h // 2, P:T], k[r:r + 64, h // 2, :], start=True, stop=True)
                fin(m, name)

            def causal_turn(name, p):
                room(pe, name)
                tr(b(name)[:, 0:P], p[:, 0:P], ident)
                tr(b(name)[:, P:T], p[:, P:T], ident)
                m = tr(b(name)[:, T:T + P], p[:, T:T + P], ident)
                fin(m, name)

            def causal_out(name, pT, v, at, width, r, last):
                mm(b(name)[r:r + width, 0:T], v[:, 0, at:at + width], pT[:, 0:T], start=True, stop=False)
                m = mm(b(name)[r:r + width, P:T], v[:, 1, at:at + width], pT[:, T:T + P], start=False, stop=True)
                if last:
                    fin(m, name)

            pe.wait_ge(gla_scaled, 4)
            room(pe, "kt")
            for tb in range(TB):
                for t in range(2):
                    m = tr(b("kt")[:, T * tb + P * t:T * tb + P * t + P], ex[2][:, t, P * tb:P * tb + P], ident)
            fin(m, "kt")
            for name in ("qm0", "qm1", "km0", "km1"):
                emptied(pe, name)
            emptied(pe, "v1")
            emptied(pe, "vm1")
            causal_scores("ms0", qm, km, 0)
            for par, name in ((0, "ae"), (1, "ao")):
                room(pe, name)
                for h in (par, 2 + par):
                    for n in range(4):
                        c = ((n // 2) * 2 + h // 2) * 64
                        r = 64 * par
                        m = mm(b(name)[64 * (n % 2):64 * (n % 2) + 64, c:c + 64],
                               ex[1][r:r + 64, h // 2, 64 * n:64 * n + 64], ex[0][r:r + 64, h // 2, 64 * n:64 * n + 64],
                               start=True, stop=True)
                fin(m, name)
            causal_scores("ms1", qm, km, 1)
            emptied(pe, "kt")
            for par, name in ((0, "ke"), (1, "ko")):
                room(pe, name)
                for n in ((0, 2) if par == 0 else (1,)):
                    for h in range(4):
                        r = 64 * par
                        c = ((n // 2) * 2 + h // 2) * P
                        m = mm(b(name)[64 * (h % 2):64 * (h % 2) + 64, c:c + P],
                               kdt[r:r + 64, n // 2, 64 * h:64 * h + 64], vg[r:r + 64, n // 2, P * h:P * h + P],
                               start=True, stop=True)
                fin(m, name)
            pe.wait_ge(prob_ready, 1)
            causal_turn("mt_0", prob[0])
            emptied(pe, "ae")
            emptied(pe, "ao")
            for par, name in ((0, "oe"), (1, "oo")):
                room(pe, name)
                r = 64 * par
                for h in range(4):
                    for tb in range(TB):
                        m = mm(b(name)[:, (2 * h + tb) * 64:(2 * h + tb) * 64 + 64], vg[r:r + 64, tb, P * h:P * h + P],
                               att[h % 2][r:r + 64, (2 * tb + h // 2) * 64:(2 * tb + h // 2) * 64 + 64],
                               start=True, stop=True)
                fin(m, name)
            emptied(pe, "ke")
            for par, name in ((0, "ie"), (1, "io")):
                room(pe, name)
                r = 64 * par
                for hp in range(2):
                    for n in range(1, 4):
                        m = mm(b(name)[:, T * hp + 64 * n:T * hp + 64 * n + 64], states[r:r + 64, n - 1, hp, :],
                               ex[3][r:r + 64, hp, 64 * n:64 * n + 64], start=True, stop=True)
                fin(m, name)
            causal_scores("ms2", qm, km, 2)
            group_f("zg0", "zg0", 0)

            def head_norm_sum(names, at):
                pe.wait_ge(hsq_ready, at)
                for i, name in enumerate(names):
                    room(pe, name)
                    m = mm(b(name)[:, :], ones, hsq[:, 2 * i:2 * i + 2, :], start=True, stop=True)
                    fin(m, name)

            head_norm_sum(["gn0", "gn1"], 1)

            def moba_out(h):
                if h % 2 == 0:
                    room(pe, f"mo{h // 2}")
                emptied(pe, f"mt_{h}")
                causal_out(f"mo{h // 2}", probT[h % 2], vm, 64 * h, 64, 64 * (h % 2), h % 2 == 1)

            moba_out(0)
            pe.wait_ge(prob_ready, 2)
            causal_turn("mt_1", prob[1])
            causal_scores("ms3", qm, km, 3)
            group_f("zg0", "zg1", 1)
            moba_out(1)
            for h in range(2, 8):
                pe.wait_ge(prob_ready, h + 1)
                causal_turn(f"mt_{h}", prob[h % 2])
                if h + 2 < 8:
                    causal_scores(f"ms{h + 2}", qm, km, h + 2)
                group_f(("zg1", "zm0", "zm1")[(h - 2) // 2], ("zg2", "zg3", "zm0", "zm1", "zm2", "zm3")[h - 2], h % 2)
                moba_out(h)

            def merge_out(sfx, chunks, o_first, wait_first, o_second, wait_second, n):
                for chunk, o, names, wait in ((chunks[0], o_first, "pa", wait_first), (chunks[1], o_second, "pb", wait_second)):
                    wait()
                    landed(pe, chunk)
                    w = tall[CHUNK[chunk][0]]
                    for j in range(4):
                        name = f"{names}{j}{sfx}"
                        room(pe, name)
                        for half in range(2):
                            for k in range(4):
                                m = mm(b(name)[:, T * half:T * half + T], w[:, k, P * (2 * j + half):P * (2 * j + half) + P],
                                       o[:, k, :], start=k == 0, stop=k == 3)
                        fin(m, name)
                split_f("out0" + sfx, z_parts, ["ou0" + sfx, "ou1" + sfx], (z_split, 4 * n))
                split_f("out1" + sfx, z_parts, ["ou2" + sfx, "ou3" + sfx])

            merge_out("", ["proj_gla", "proj_moba"], og, lambda: pe.wait_ge(og_ready, 1),
                      om, lambda: [emptied(pe, f"mo{i}") for i in range(4)], 0)

            norm_sum("n_cross")
            linear_f("cq", hn, ["cq0", "cq1"], h_at=16)

            def cross_scores(h):
                room(pe, f"cs{h}")
                for tb in range(TB):
                    m = mm(b(f"cs{h}")[:, T * tb:T * tb + T], qc[:, h, P * tb:P * tb + P], kc[:, h, :], start=True, stop=True)
                fin(m, f"cs{h}")

            emptied(pe, "cq0")
            emptied(pe, "cq1")
            emptied(pe, "kc0")
            emptied(pe, "kc1")
            for h in range(4):
                cross_scores(h)

            def cross_turn(h):
                pe.wait_ge(prob_ready, 8 + h + 1)
                name = f"ct{h}"
                room(pe, name)
                for kb in range(2):
                    for tb in range(TB):
                        m = tr(b(name)[:, T * kb + P * tb:T * kb + P * tb + P], cprob[h][:, tb, P * kb:P * kb + P], ident)
                fin(m, name)

            def cross_out(h):
                emptied(pe, f"ct{h}")
                emptied(pe, "vc1")
                name = f"co{h}"
                room(pe, name)
                for kb in range(2):
                    m = mm(b(name)[:, 0:T], vc[:, kb, P * h:P * h + P], cprobT[h % 2][:, T * kb:T * kb + T],
                           start=kb == 0, stop=kb == 1)
                fin(m, name)

            for h in range(4):
                cross_turn(h)
                if h:
                    cross_out(h - 1)
            cross_out(3)
            for h in range(4):
                emptied(pe, f"co{h}")
            landed(pe, "co")
            w = tall[CHUNK["co"][0]]
            for j in range(4):
                name = f"cw{j}"
                room(pe, name)
                for half in range(2):
                    for k in range(4):
                        m = mm(b(name)[:, T * half:T * half + T], w[:, k, P * (2 * j + half):P * (2 * j + half) + P],
                               oc[:, k, :], start=k == 0, stop=k == 3)
                fin(m, name)

            norm_sum("n_moe")
            pe.wait_ge(router_in, 64)
            room(pe, "routeT")
            for k in range(KT):
                pe.wait_ge(h_ready, 24 + k + 1)
                m = mm(b("routeT")[0:36, 0:T], wr[:, k, :], hn[:, k, :], start=k == 0, stop=k == KT - 1)
            fin(m, "routeT")
            emptied(pe, "routeT")
            room(pe, "route")
            for tb in range(TB):
                m = tr(b("route")[:, 36 * tb:36 * tb + 36], lgT[:, P * tb:P * tb + P], ident[0:36, 0:36])
            fin(m, "route")
            for j in range(4):
                name = f"ht{j}"
                room(pe, name)
                for kk in range(4):
                    m = tr(b(name)[:, P * kk:P * kk + P], hn[:, 4 * (j % 2) + kk, P * (j // 2):P * (j // 2) + P], ident)
                fin(m, name)
            pe.wait_ge(mask_ready, 1)
            room(pe, "rank")
            mm(b("rank")[:, 0:32], later, msk[:, 0, :], start=True, stop=True)
            mm(b("rank")[:, 32:64], later, msk[:, 1, :], start=True, stop=False)
            mm(b("rank")[:, 32:64], ones, msk[:, 0, :], start=False, stop=True)
            mm(b("rank")[:, 64:96], ones, msk[:, 0, :], start=True, stop=False)
            m = mm(b("rank")[:, 64:96], ones, msk[:, 1, :], start=False, stop=True)
            fin(m, "rank")

            for bank in range(8):
                pe.wait_ge(bank_free[bank], BEFORE_EXPERTS[bank])
            pe.wait_ge(blank, 1)
            for i in range(4):
                mm(ps[4 + i][:, :], zero[0:P, 0:P], zero[:, P:P + HALF], start=True, stop=False, skip_group_check=True)

            def gather(s, n):
                pe.wait_ge(s["sel_made"], 4 * n + 4)
                for k in range(KT):
                    for tb in range(TB):
                        m = mm(ps[2 + k // 4][:, P * (k % 4):P * (k % 4) + P], htok[:, tb, P * k:P * k + P], sel[:, tb, :],
                               start=tb == 0, stop=tb == TB - 1)
                m.then_inc(s["gather_done"], 1)

            def combine():
                for tb in range(TB):
                    for half in range(2):
                        m = mm(ps[4 + 2 * tb + half][:, :], selT[:, P * tb:P * tb + P], y[:, HALF * half:HALF * half + HALF],
                               start=False, stop=False, skip_group_check=True)
                return m

            def pair(s, sl, n, g, lb):
                for up in range(2):
                    if up == 0:
                        pe.wait_ge(s["xe_a"], g + 1)
                        pe.wait_ge(s["xe_d"], g + 1)
                        pe.wait_ge(s["y0_out"], n + 1)
                    else:
                        pe.wait_ge(s["y1_out"], n + 1)
                    pe.wait_ge(sl[2 + 2 * up], n * 32 + 32)
                    pe.wait_ge(sl[3 + 2 * up], n * 32 + 32)
                    for k in range(KT):
                        mm(ps[up][0:64, :], xe[:, k, 0:64], wide[2 + 2 * up][:, k, :], start=k == 0, stop=k == KT - 1)
                        m = mm(ps[up][64:128, :], xe[:, k, 64:128], wide[3 + 2 * up][:, k, :], start=k == 0, stop=k == KT - 1)
                    m.then_inc(s[("gate_done", "up_done")[up]], 1)
                combine()
                gather(s, g + 1)
                pe.wait_ge(s["hid_made"], n + 1)
                for kk in range(4):
                    m = tr(ps[0][:, P * kk:P * kk + P], hid[:, P * kk:P * kk + P], ident)
                m.then_inc(s["hidT_done"], 1)
                pe.wait_ge(s["selw_made"], 4 * n + 4)
                for tb in range(TB):
                    m = tr(ps[1][:, P * tb:P * tb + P], selw[:, tb, :], ident)
                m.then_inc(s["selT_done"], 1)
                pe.wait_ge(sl[0], n * 32 + (lb + 32))
                pe.wait_ge(sl[1], n * 32 + (lb + 32))
                for half in range(2):
                    if half == 0:
                        pe.wait_ge(s["hidT_out"], n + 1)
                    else:
                        pe.wait_ge(s["selT_out"], n + 1)
                    for kk in range(4):
                        mm(ps[half][0:64, :], hidT[:, kk, 0:64], tall[0][:, kk, HALF * half:HALF * half + HALF],
                           start=kk == 0, stop=kk == 3)
                        m = mm(ps[half][64:128, :], hidT[:, kk, 64:128], tall[1][:, kk, HALF * half:HALF * half + HALF],
                               start=kk == 0, stop=kk == 3)
                    m.then_inc(s[("y0_done", "y1_done")[half]], 1)

            s = moe_sems[0]
            gather(s, 0)
            with pe.Fori(0, PAIRS) as p:
                pair(s, slot_landed, p, p, 32 * (len(FIRST_CHUNKS) // RAW))
            pe.wait_ge(s["y0_out"], PAIRS + 1)
            pe.wait_ge(s["y1_out"], PAIRS + 1)
            combine().then_inc(passed, 1)
            pe.wait_ge(s["xe_a"], PAIRS + 1)
            pe.wait_ge(s["xe_d"], PAIRS + 1)
            pe.wait_ge(count_ready, 1)
            most = pe.value_load(cnt[0:1, 0:1], min_val=0, max_val=T)
            with pe.If(most > SLOTS):
                o = moe_sems[1]
                with pe.Fori(0, OVER_PASSES) as q:
                    pe.wait_ge(blank, q + 2)
                    gather(o, q * (PAIRS + 1))
                    with pe.Fori(0, PAIRS) as p:
                        n = q * PAIRS + p
                        pair(o, over_landed, n, q * (PAIRS + 1) + p, 0)
                    pe.wait_ge(o["y0_out"], q * PAIRS + (PAIRS + 1))
                    pe.wait_ge(o["y1_out"], q * PAIRS + (PAIRS + 1))
                    combine().then_inc(passed, 1)
                    pe.wait_ge(o["xe_a"], (q + 1) * (PAIRS + 1))
                    pe.wait_ge(o["xe_d"], (q + 1) * (PAIRS + 1))
            for i in range(4):
                m = mm(ps[4 + i][:, :], zero[0:P, 0:P], zero[:, P:P + HALF], start=False, stop=True, skip_group_check=True)
                fin(m, f"acc{i}")
            for i in range(4):
                emptied(pe, f"acc{i}")
            to_features(acc_sb, [f"at{j}" for j in range(4)])
            norm_sum("n_final")

            for l in range(LAYERS):
                x = f".{l}"
                norm_sum("n_attn" + x)
                split_f("dq" + x, z_parts, ["dq0" + x, "dq1" + x], (xg_split, 4 * l))
                split_f("dk" + x, z_parts, ["dk0" + x, "dk1" + x])
                for name in ("dq0", "dq1", "dk0", "dk1"):
                    emptied(pe, name + x)
                pe.wait_ge(cb_in, 16)
                for i, (t, name) in enumerate(((dq, "rq"), (dk, "rk"))):
                    for j in range(2):
                        room(pe, f"{name}{j}{x}")
                        m = mm(b(f"{name}{j}{x}")[:, :], rope, t[:, 2 * j:2 * j + 2, :], start=True, stop=True)
                        fin(m, f"{name}{j}{x}")
                pe.wait_ge(hn_split, 4 * SPLIT_NORMS.index("n_attn" + x) + 4)
                split_t("dv" + x, ["dv0" + x, "dv1" + x])

                def diff_scores(h):
                    for i in range(2):
                        causal_scores(f"{('ds', 'de')[i]}{h}{x}", dq, dk, 2 * h + i)

                def diff_turn(h):
                    pe.wait_ge(prob_ready, 12 + 4 * l + h + 1)
                    causal_turn(f"dt{h}{x}", p1[h % 2])

                def diff_out(h):
                    emptied(pe, f"dt{h}{x}")
                    room(pe, f"do{h}{x}")
                    causal_out(f"do{h}{x}", probT[h % 2], dv, P * h, P, 0, True)

                pe.wait_ge(rotated, 4 * (l + 1))
                diff_scores(0)
                split_f("sq" + x, hn_parts, ["sq0" + x, "sq1" + x])
                diff_turn(0)
                diff_scores(1)
                split_f("sk" + x, hn_parts, ["sk0" + x, "sk1" + x])
                emptied(pe, "dv1" + x)
                diff_out(0)
                diff_turn(1)
                diff_scores(2)
                split_t("sv" + x, ["sv0" + x, "sv1" + x])
                diff_out(1)
                diff_turn(2)
                diff_scores(3)

                def sb_scores(h):
                    name = f"bz{h}{x}"
                    r = 64 * (h % 2)
                    room(pe, name)
                    mm(b(name)[:, 0:T], bk[r:r + 64, h // 2, 0:P], bq[r:r + 64, h // 2, :], start=True, stop=True)
                    m = mm(b(name)[:, T:T + P], bk[r:r + 64, h // 2, P:T], bq[r:r + 64, h // 2, P:T], start=True, stop=True)
                    fin(m, name)

                def sb_after_sum(h):
                    name = f"ba{h}{x}"
                    room(pe, name)
                    pe.wait_ge(sb_rem, 8 * l + h + 1)
                    lr = lrem[h % 2]
                    mm(b(name)[:, 0:T], earlier, lr[:, 0:T], start=True, stop=False)
                    mm(b(name)[:, P:T], ones, lr[:, T:T + P], start=False, stop=True)
                    m = mm(b(name)[:, T:T + P], earlier, lr[:, T:T + P], start=True, stop=True)
                    fin(m, name)

                def sb_out(h):
                    if h % 2 == 0:
                        room(pe, f"bo{h // 2}{x}")
                    pe.wait_ge(sb_prob, 8 * l + h + 1)
                    causal_out(f"bo{h // 2}{x}", stick[h % 4], bv, 64 * h, 64, 64 * (h % 2), h % 2 == 1)

                for name in ("sq0", "sq1", "sk0", "sk1", "sv1"):
                    emptied(pe, name + x)
                sb_scores(0)
                sb_scores(1)
                group_f("ga0" + x, "ga0" + x, 0)
                diff_out(2)
                diff_turn(3)
                sb_after_sum(0)
                group_f("ga0" + x, "ga1" + x, 1)
                diff_out(3)
                for h in range(8):
                    if h in (0, 2, 4):
                        sb_scores(h + 2)
                        sb_scores(h + 3)
                    if h < 7:
                        sb_after_sum(h + 1)
                    for name, half in GATE_HALVES[h]:
                        j = int(name[2])
                        split_tile(f"{name[:2]}{j // 2}{x}", hn_parts, name + x, 2 * (j % 2) + half)
                    if h == 0:
                        head_norm_sum(["dn0" + x, "dn1" + x], l + 2)
                    sb_out(h)
                merge_out(x, ["proj_diff" + x, "proj_sb" + x], od, lambda: pe.wait_ge(og_ready, l + 2),
                          ob, lambda: [emptied(pe, f"bo{i}{x}") for i in range(4)], l + 1)

                norm_sum("n_ffn" + x)
                for j in range(11):
                    split_f(f"ffn{j}{x}", hn_parts, [f"fg{j}{x}", f"fu{j}{x}"], hn_fresh("n_ffn" + x) if j == 0 else None)
                for i in range(4):
                    room(pe, f"fo{i}{x}")
                for c in range(5):
                    for kk in range(4):
                        f = 4 * c + kk
                        ready(f"down{c}{x}", kk, 4)
                        if f % 2 == 0:
                            pe.wait_ge(hid_split, 11 * l + f // 2 + 1)
                        for mt in range(8):
                            for i, (ws, xs) in enumerate(PASSES):
                                m = mm(b(f"fo{mt // 2}{x}")[:, T * (mt % 2):T * (mt % 2) + T],
                                       part(f"down{c}{x}", ws)[:, kk, P * mt:P * mt + P], hid_parts[xs][:, f, :],
                                       start=f == 0 and i == 0 and mt % 2 == 0, stop=False, skip_group_check=True)
                    m.then_inc(down_used, 1)
                pe.wait_ge(tail_landed, 16 * (l + 1))
                pe.wait_ge(hid_scaled, 11 * (l + 1))
                for mt in range(8):
                    for kk in range(2):
                        m = mm(b(f"fo{mt // 2}{x}")[:, T * (mt % 2):T * (mt % 2) + T], tail_w[:, kk, P * mt:P * mt + P],
                               hid_raw[10 % 3][:, kk, :], start=False, stop=kk == 1, skip_group_check=True)
                    if mt % 2 == 1:
                        fin(m, f"fo{mt // 2}{x}")

            norm_sum("n_last")
            for j in (0, 2, 1, 3):
                name = f"yt{j}"
                room(pe, name)
                for kk in range(4):
                    pe.wait_ge(h_ready, 8 * NORMS.index("n_last") + 4 * (j % 2) + kk + 1)
                    m = tr(b(name)[:, P * kk:P * kk + P], hn[:, 4 * (j % 2) + kk, P * (j // 2):P * (j // 2) + P], ident)
                fin(m, name)

        @block.scalar
        def _(act):
            A = nc.scalar.activation
            chain = [0]

            def link(ins):
                chain[0] += 1
                ins.then_inc(act_chain, 1)
                act.wait_ge(act_chain, chain[0])

            act.dma_start(walr, a["w_in"][0][:, 1536:1552].rearrange("(k p) n -> p k n", p=P)).then_inc(small_in, 16)
            act.dma_start(wau, a["w_alpha_up"][0]).then_inc(small_in, 16)
            act.dma_start(wr[:, :, 0:4], a["w_router_group"][0].rearrange("(k p) n -> p k n", p=P)).then_inc(router_in, 16)
            act.dma_start(wr[:, :, 4:36], a["w_router_expert"][0].rearrange("(k p) n -> p k n", p=P)).then_inc(router_in, 16)
            act.dma_start(brow[:, 0:4], bass.AP(a["b_router_group"].tensor, 0, [[0, P], [1, 4]])).then_inc(router_in, 16)
            act.dma_start(brow[:, 4:36], bass.AP(a["b_router_expert"].tensor, 0, [[0, P], [1, 32]])).then_inc(router_in, 16)

            act.wait_ge(eps_ready, 1)

            def take(name, dst, scale=1.0, func=ACT.Copy):
                full(act, name)
                n = dst.shape[-1] if len(dst.shape) == 3 else None
                src = b(name)[:, :] if n is None else b(name)[:, :].rearrange("p (a b) -> p a b", b=n)
                freed(A(dst, src, func, scale=scale), name)

            def two(t, j):
                return t[:, 2 * j:2 * j + 2, :]

            def norm_squares(name, src, made=None, beside=None):
                for j in range(4):
                    if name == "n_attn.0":
                        act.wait_ge(h_ready, 8 * NORMS.index("n_final") + 2 * j + 2)
                    if made:
                        emptied(act, made[j])
                    A(two(view(SQ, 0, KT, T), j), two(src, j), ACT.Square).then_inc(sq_ready, 1)
                    if beside:
                        beside(j)

            def norm_root(name):
                full(act, name)
                if NORMS.index(name):
                    act.wait_ge(h_ready, 8 * NORMS.index(name))
                freed(A(ffn_root if name.startswith("n_ffn") else root, b(name)[:, 0:T], ACT.Sqrt, bias=eps_col, scale=1.0 / D), name)

            def head_roots(names):
                for i, name in enumerate(names):
                    full(act, name)
                    freed(A(hroot[:, 2 * i:2 * i + 2, :], b(name)[:, :].rearrange("p (a b) -> p a b", b=T), ACT.Sqrt,
                            bias=eps_col, scale=1.0 / P), name)

            for j in range(4):
                take(f"mt{j}", two(mem_f, j))
            def high(chunk, halves=(0, 1)):
                r = SPLIT.index(chunk)
                landed(act, chunk)
                if chunk in ("dq.0", "dk.0"):
                    full(act, "acc3")
                elif r >= 2:
                    used(act, SPLIT[r - 2])
                for i in halves:
                    A(parts[:, 2 * (r % 2), 2048 * i:2048 * i + 2048], ring[:, CHUNK[chunk][0], 2048 * i:2048 * i + 2048],
                      ACT.Copy).then_inc(high_made, 1)

            def hn_highs(name, tiles=range(4)):
                for j in tiles:
                    act.wait_ge(h_ready, 8 * NORMS.index(name) + 2 * j + 2)
                    A(two(hn_parts[0], j), two(hn, j), ACT.Copy).then_inc(hn_high, 1)

            def z_highs(n):
                for j in range(4):
                    act.wait_ge(merged_ready, 4 * n + j + 1)
                    A(two(z_parts[0], j), two(z1, j), ACT.Copy).then_inc(z_high, 1)

            norm_squares("n_mem", mem_f, [f"mt{j}" for j in range(4)])
            norm_root("n_mem")
            norm_squares("n_mix", xres, [f"xt{j}" for j in range(4)])
            take("kc0", two(kc, 0))
            take("kc1", two(kc, 1))
            norm_root("n_mix")
            hn_highs("n_mix")
            high("qk")
            take("vc0", vc[:, 0, :])
            take("vc1", vc[:, 1, :])
            for j in range(4):
                take(f"bj{j}", two(bias, j))
            high("v")
            take("qk0", qg, scale=64 ** -0.5)
            take("qk1", kg)
            high("r")
            high("qm")
            emptied(act, "alpha")
            link(A(t1, za, ACT.Abs))
            link(A(t1, t1, ACT.Exp, scale=-1.0))
            A(t1, t1, ACT.Ln, bias=1.0).then_inc(gla_softplus, 1)
            take("r0", two(rg, 0), func=ACT.Silu)
            take("r1", two(rg, 1), func=ACT.Silu)
            high("km")
            take("qm0", two(qm, 0))
            take("qm1", two(qm, 1))
            high("vm")
            act.wait_ge(gla_diffs, 1)
            for i, (src, scale) in enumerate(((dmid, 1), (dmid, -1), (dlast, -1), (bcum, 1))):
                A(ex[i], src, ACT.Exp, scale=scale / 16.0).then_inc(gla_exps, 1)

            def nm(i, j):
                return sm[:, 4 + 8 * (i % 2) + j:5 + 8 * (i % 2) + j]

            def sums(i, j):
                return sm[:, 20 + 8 * (i % 2) + j:21 + 8 * (i % 2) + j]

            def causal_exp(i, bufs):
                act.wait_ge(logit_ready, i + 1)
                for j, p in enumerate(bufs):
                    A(p[:, 0:P], p[:, 0:P], ACT.Exp, bias=nm(i, 2 * j), accum_out=sums(i, 2 * j))
                    last = A(p[:, P:384], p[:, P:384], ACT.Exp, bias=nm(i, 2 * j + 1), accum_out=sums(i, 2 * j + 1))
                last.then_inc(exp_ready, 1)

            def take_turned(name, i):
                full(act, name)
                freed(A(probT[i % 2], b(name)[:, 0:384], ACT.Copy), name)

            high("zg0")
            high("zg1")
            take("kt", kdt.rearrange("p a b -> p (a b)"))
            causal_exp(0, [prob[0]])
            causal_exp(1, [prob[1]])
            take_turned("mt_0", 0)
            take("zg0", two(z1, 0))
            head_roots(["gn0", "gn1"])
            take_turned("mt_1", 1)
            causal_exp(2, [prob[0]])
            causal_exp(3, [prob[1]])
            take("zg1", two(z1, 1))
            high("zm0", [0])
            for h in range(2, 8):
                take_turned(f"mt_{h}", h)
                if h + 2 < 8:
                    causal_exp(h + 2, [prob[h % 2]])
                take(("zg2", "zg3", "zm0", "zm1", "zm2", "zm3")[h - 2], two(z1, h) if h < 4 else two(z2, h - 4))
                if h == 2:
                    high("zm0", [1])
                if h in (3, 4):
                    high("zm1", [h - 3])

            def sigmoids(names):
                for z, name in ((z1, names[0]), (z2, names[1])):
                    emptied(act, name)
                    A(z, z, ACT.Sigmoid).then_inc(z_sig, 1)

            sigmoids(["zg3", "zm3"])
            high("out0")
            z_highs(0)
            high("out1")

            norm_squares("n_cross", xres, [f"ou{j}" for j in range(4)])
            norm_root("n_cross")

            def cross_exp(h):
                i = 8 + h
                full(act, f"cs{h}")
                act.wait_ge(logit_ready, i + 1)
                for tb in range(TB):
                    last = A(cprob[h][:, tb, :], b(f"cs{h}")[:, T * tb:T * tb + T], ACT.Exp, bias=nm(i, tb),
                             scale=P ** -0.5, accum_out=sums(i, tb))
                freed(last, f"cs{h}")

            cross_exp(0)
            for h in range(4):
                if h < 3:
                    cross_exp(h + 1)
                take(f"ct{h}", cprobT[h % 2])
            norm_squares("n_moe", xres, [f"cw{j}" for j in range(4)])
            norm_root("n_moe")

            act.wait_ge(route_diff, 1)
            A(e4, d4, ACT.Exp).then_inc(route_exp, 1)
            act.wait_ge(route_diff, 2)
            A(ex2, dm, ACT.Exp).then_inc(route_exp, 1)
            for j in range(4):
                take(f"ht{j}", htok[:, j // 2, HALF * (j % 2):HALF * (j % 2) + HALF])

            def take_gather(s, g):
                act.wait_ge(s["gather_done"], g + 1)
                A(xe[:, 4:8, :], ps[3][:, :].rearrange("p (a b) -> p a b", b=P), ACT.Copy).then_inc(s["xe_a"], 1)

            def act_pair(s, n, g):
                act.wait_ge(s["gate_done"], n + 1)
                A(gsil, ps[0][:, :], ACT.Silu).then_inc(s["silu_made"], 1)
                take_gather(s, g + 1)
                act.wait_ge(s["hidT_done"], n + 1)
                A(hidT, ps[0][:, :].rearrange("p (a b) -> p a b", b=P), ACT.Copy).then_inc(s["hidT_out"], 1)
                act.wait_ge(s["y0_done"], n + 1)
                A(y[:, 0:HALF], ps[0][:, :], ACT.Copy).then_inc(s["y0_out"], 1)

            s = moe_sems[0]
            take_gather(s, 0)
            with act.Fori(0, PAIRS) as p:
                act_pair(s, p, p)
            act.wait_ge(count_ready, 1)
            most = act.value_load(cnt[0:1, 0:1], min_val=0, max_val=T)
            with act.If(most > SLOTS):
                o = moe_sems[1]
                with act.Fori(0, OVER_PASSES) as q:
                    take_gather(o, q * (PAIRS + 1))
                    with act.Fori(0, PAIRS) as p:
                        act_pair(o, q * PAIRS + p, q * (PAIRS + 1) + p)
            for i in range(2):
                take(f"acc{i}", acc_sb[:, 0, HALF * i:HALF * i + HALF])
            norm_squares("n_final", xres, [f"at{j}" for j in range(4)])
            norm_root("n_final")
            high("dq.0", [0])

            for l in range(LAYERS):
                x = f".{l}"

                def xg_highs(j):
                    act.wait_ge(xg_ready, 8 * l + 2 * j + 2)
                    A(two(z_parts[0], j), two(hn, j), ACT.Copy).then_inc(xg_high, 1)

                norm_squares("n_attn" + x, xres, [f"fo{j}.{l - 1}" for j in range(4)] if l else None, xg_highs)
                if l == 0:
                    high("dq.0", [1])
                norm_root("n_attn" + x)
                hn_highs("n_attn" + x)
                if l == 0:
                    high("dk.0")
                if l == 0:
                    act.wait_ge(lam_sums, 1)
                    A(lam_e, lam_s, ACT.Exp).then_inc(lam_exps, 1)
                for i, t, after in (("dq", dq, "dv"), ("dk", dk, "sq")):
                    emptied(act, i + "1" + x)
                    high(after + x)
                i0 = 12 + 4 * l

                def diff_exp(h):
                    causal_exp(i0 + h, [p1[h % 2], p2[h % 2]])

                def sb_exps(h):
                    for i in (h, h + 1):
                        full(act, f"bz{i}{x}")
                        last = A(stick[i % 4], b(f"bz{i}{x}")[:, 0:384], ACT.Abs, scale=64 ** -0.5)
                    link(last)
                    for i in (h, h + 1):
                        last = A(stick[i % 4], stick[i % 4], ACT.Exp, scale=-1.0)
                    link(last)

                def sb_softplus(h):
                    for i in (h, h + 1):
                        A(stick[i % 4], stick[i % 4], ACT.Ln, bias=1.0).then_inc(sb_logs, 1)

                def sb_weights(h):
                    emptied(act, f"ba{h}{x}")
                    A(stick[h % 4], lbeta[h % 2], ACT.Exp).then_inc(sb_exp, 1)

                def gates(names, z, g0, row):
                    for j, name in enumerate(names):
                        full(act, name)
                        for half in range(2):
                            last = A(z[:, 2 * (g0 + j) + half, :], b(name)[:, T * half:T * half + T], ACT.Identity,
                                     bias=gain("b_gate_2", 16 * l + row + 2 * (g0 + j) + half))
                        freed(last, name)

                diff_exp(0)
                high("sk" + x)
                take("sq0" + x, two(bq, 0))
                take("sq1" + x, two(bq, 1))
                take_turned("dt0" + x, 0)
                diff_exp(1)
                high("sv" + x)
                take("sk0" + x, two(bk, 0))
                take("sk1" + x, two(bk, 1))
                take_turned("dt1" + x, 1)
                diff_exp(2)
                high("ga0" + x)
                take_turned("dt2" + x, 0)
                diff_exp(3)
                sb_exps(0)
                sb_softplus(0)
                high("ga1" + x, [0])
                gates(["ga0" + x], z1, 0, 0)
                high("ga1" + x, [1])
                take_turned("dt3" + x, 1)
                sb_weights(0)
                gates(["ga1" + x], z1, 1, 0)
                high("gb0" + x)
                for h in range(8):
                    if h in (0, 2, 4):
                        sb_exps(h + 2)
                    if h < 7:
                        sb_weights(h + 1)
                    if h in (0, 2, 4):
                        sb_softplus(h + 2)
                    for name, half in GATE_HALVES[h]:
                        if half:
                            g = int(name[2])
                            gates([name + x], *((z1, g, 0) if name[1] == "a" else (z2, g, 8)))
                    if h == 0:
                        head_roots(["dn0" + x, "dn1" + x])
                    if h in (2, 3):
                        high("gb1" + x, [h - 2])
                sigmoids(["ga3" + x, "gb3" + x])
                high("out0" + x)
                z_highs(l + 1)
                high("out1" + x)

                def ffn_beside(j):
                    hn_highs("n_ffn" + x, [j])
                    if j == 1:
                        high("ffn0" + x)

                norm_squares("n_ffn" + x, xres, [f"ou{j}{x}" for j in range(4)], ffn_beside)
                norm_root("n_ffn" + x)
                high("ffn1" + x)
                for j in range(11):
                    emptied(act, f"fg{j}{x}")
                    A(hid_raw[j % 3], hid_raw[j % 3], ACT.Silu).then_inc(hid_silu, 1)
                    act.wait_ge(hid_scaled, 11 * l + j + 1)
                    A(two(hid_parts[0], j), hid_raw[j % 3], ACT.Copy).then_inc(hid_high, 1)
                    high(SPLIT[SPLIT.index(f"ffn{j}{x}") + 2])
                for c in range(5 if l + 1 < LAYERS else 3):
                    high(SPLIT[SPLIT.index(f"down{c}{x}") + 2])
            norm_squares("n_last", xres, [f"fo{j}.{LAYERS - 1}" for j in range(4)])
            norm_root("n_last")
            for j in range(2):
                take(f"yt{j}", y_out[:, 0, HALF * j:HALF * j + HALF])

        @block.vector
        def _(dve):
            v = nc.vector
            chain = [0]

            def link(ins):
                chain[0] += 1
                ins.then_inc(dve_chain, 1)
                dve.wait_ge(dve_chain, chain[0])

            def two(t, j):
                return t[:, 2 * j:2 * j + 2, :]

            def src_of(name, dst):
                return b(name)[:, :] if len(dst.shape) == 2 else b(name)[:, :].rearrange("p (a b) -> p a b", b=dst.shape[-1])

            def take(name, dst):
                full(dve, name)
                freed(v.tensor_copy(dst, src_of(name, dst)), name)

            def take_scaled(name, dst, by):
                full(dve, name)
                freed(v.tensor_tensor(dst, src_of(name, dst), by, ALU.mult), name)

            def residual(names, at=0):
                for j, name in enumerate(names, at):
                    full(dve, name)
                    freed(v.tensor_tensor(two(xres, j), src_of(name, two(xres, j)), two(xres, j), ALU.add), name)

            def norm_apply(name, src, dst, row, at=0):
                emptied(dve, name)
                link(v.reciprocal(root, root))
                for k in range(KT):
                    v.scalar_tensor_tensor(dst[:, k, :], src[:, k, :], gain(row, at + k), root, ALU.mult, ALU.mult).then_inc(h_ready, 1)
                    if name in SPLIT_NORMS and k >= 3 and k % 2:
                        hn_low(name, k // 2 - 1)
                if name in SPLIT_NORMS:
                    hn_low(name, 3)

            def hn_low(name, j):
                dve.wait_ge(hn_high, 4 * SPLIT_NORMS.index(name) + j + 1)
                v.tensor_tensor(two(hn_parts[1], j), two(hn, j), two(hn_parts[0], j).bitcast(F32), ALU.subtract).then_inc(hn_split, 1)

            def gain_apply(row, at, j, ready=h_ready):
                for k in (2 * j, 2 * j + 1):
                    v.tensor_scalar(hn[:, k, :], xres[:, k, :], gain(row, at + k), None, ALU.mult).then_inc(ready, 1)

            def over_tiles(t):
                return t.rearrange("p (a c) -> p a c", a=1).to_broadcast([P, 2, T])

            def low(chunk, halves=(0, 1)):
                r = SPLIT.index(chunk)
                for i in halves:
                    dve.wait_ge(high_made, 2 * r + i + 1)
                    at = slice(2048 * i, 2048 * i + 2048)
                    v.tensor_tensor(parts[:, 2 * (r % 2) + 1, at], ring[:, CHUNK[chunk][0], at],
                                    parts[:, 2 * (r % 2), at].bitcast(F32), ALU.subtract).then_inc(low_made, 1)

            v.memset(eps_col, EPS).then_inc(eps_ready, 1)
            v.memset(urow, -BIG).then_inc(urow_masked, 1)
            full(dve, "gains")
            freed(v.tensor_copy(gcol[:, 0:NROWS], b("gains")[:, 0:NROWS]), "gains")
            for j in range(4):
                take(f"xt{j}", two(xres, j))
            emptied(dve, "gains")
            norm_apply("n_mem", mem_f, mem_n, "g_mem")
            full(dve, "bucket")
            dve.wait_ge(urow_masked, 1)
            freed(v.tensor_copy(urow[:, 0:T], b("bucket")[0:8, 0:T]), "bucket")
            for j in range(4):
                emptied(dve, f"xt{j}")
            norm_apply("n_mix", xres, hn, "g_mix")
            low("qk")
            low("v")
            full(dve, "alr")
            freed(v.tensor_copy(alr, b("alr")[0:16, 0:T]), "alr")
            low("r")
            take("v0", vg[:, 0, :])
            take("v1", vg[:, 1, :])
            full(dve, "alpha")
            for t in range(2):
                last = v.tensor_scalar(za[:, t, :], b("alpha")[:, T * t:T * t + T], gain("b_alpha", t), None, ALU.add)
            freed(last, "alpha")
            low("qm")
            dve.wait_ge(gla_softplus, 1)
            link(v.scalar_tensor_tensor(t1, za, 0.0, t1, ALU.min, ALU.subtract))
            for t in range(2):
                for n in range(4):
                    last = v.tensor_tensor_scan(bcum[:, t, 64 * n:64 * n + 64], ones[:, 0:64], t1[:, t, 64 * n:64 * n + 64],
                                                0.0, ALU.mult, ALU.add)
            link(last)

            def chunks(t):
                return t.rearrange("p a (n c) -> p (a n) c", c=64)

            v.tensor_tensor(chunks(dmid), chunks(bcum), chunks(bcum)[:, :, 31:32].to_broadcast([P, 8, 64]), ALU.subtract)
            v.tensor_tensor(chunks(dlast), chunks(bcum), chunks(bcum)[:, :, 63:64].to_broadcast([P, 8, 64]), ALU.subtract).then_inc(gla_diffs, 1)
            low("km")
            low("vm")
            take("km0", two(km, 0))
            take("km1", two(km, 1))
            low("zg0")
            take("vm0", vm[:, 0, :])
            take("vm1", vm[:, 1, :])
            dve.wait_ge(gla_exps, 4)
            emptied(dve, "qk0")
            emptied(dve, "qk1")
            decay = sm[:, 52:60].rearrange("p (a n) -> p a n", n=4)
            link(v.tensor_copy(decay, ex[3].rearrange("p a (n c) -> p a n c", c=64)[:, :, :, 63]))
            for i, t in enumerate((qg, kg, kg, qg)):
                v.tensor_tensor(ex[i], ex[i], t, ALU.mult).then_inc(gla_scaled, 1)
            v.memset(att[0], 0.0)
            link(v.memset(att[1], 0.0))

            def nm(i, j, n=1):
                return sm[:, 4 + 8 * (i % 2) + j:4 + n + 8 * (i % 2) + j]

            def sums(i, j, n=1):
                return sm[:, 20 + 8 * (i % 2) + j:20 + n + 8 * (i % 2) + j]

            def recs(i, j, n=1):
                return sm[:, 36 + 8 * (i % 2) + j:36 + n + 8 * (i % 2) + j]

            def maxima(i, j, p):
                v.reduce_max(nm(i, j), p[:, 0:P], AX, negate=True)
                return v.reduce_max(nm(i, j + 1), p[:, P:384], AX, negate=True)

            def moba_logits(h):
                p = prob[h % 2]
                full(dve, f"ms{h}")
                v.scalar_tensor_tensor(p[:, 0:P], b(f"ms{h}")[:, 0:P], 64 ** -0.5, bias[:, h, P:T], ALU.mult, ALU.add)
                freed(v.scalar_tensor_tensor(p[:, P:384], b(f"ms{h}")[:, P:384], 64 ** -0.5, bias[:, h, :], ALU.mult, ALU.add), f"ms{h}")
                emptied(dve, f"ms{h}")
                maxima(h, 0, p).then_inc(logit_ready, 1)

            def moba_norm(h):
                p = prob[h % 2]
                dve.wait_ge(exp_ready, h + 1)
                link(v.reciprocal(recs(h, 0, 2), sums(h, 0, 2)))
                v.tensor_scalar(p[:, 0:P], p[:, 0:P], recs(h, 0), None, ALU.mult)
                v.tensor_scalar(p[:, P:384], p[:, P:384], recs(h, 1), None, ALU.mult).then_inc(prob_ready, 1)

            low("zg1")
            for j in range(4):
                emptied(dve, f"bj{j}")
            moba_logits(0)
            for i, name in enumerate(("ae", "ao")):
                full(dve, name)
                mask = m64.bitcast(U32).rearrange("p (a c) -> p a c", a=1).to_broadcast([P, 8, 64])
                freed(v.copy_predicated(att[i].rearrange("p (a c) -> p a c", c=64), mask,
                                        b(name)[:, :].rearrange("p (a c) -> p a c", c=64)), name)
            moba_logits(1)
            full(dve, "ke")
            full(dve, "ko")
            link(v.tensor_copy(states[:, 0, :, :], b("ke")[:, 0:T].rearrange("p (a b) -> p a b", b=P)))
            for hp in range(2):
                last = v.scalar_tensor_tensor(states[:, 1, hp, :], states[:, 0, hp, :], decay[:, hp, 1:2],
                                              b("ko")[:, P * hp:P * hp + P], ALU.mult, ALU.add)
            freed(last, "ko")
            emptied(dve, "ko")
            for hp in range(2):
                last = v.scalar_tensor_tensor(states[:, 2, hp, :], states[:, 1, hp, :], decay[:, hp, 2:3],
                                              b("ke")[:, T + P * hp:T + P * hp + P], ALU.mult, ALU.add)
            freed(last, "ke")
            moba_norm(0)
            moba_norm(1)
            og5 = og.rearrange("p h (t e c) -> p (h t) e c", e=2, c=64)
            for e, name in enumerate(("oe", "oo")):
                full(dve, name)
                freed(v.tensor_copy(og5[:, :, e, :], b(name)[:, :].rearrange("p (a c) -> p a c", c=64)), name)
                emptied(dve, name)
            for e, name in enumerate(("ie", "io")):
                full(dve, name)
                o2 = og[:, e:4:2, 64:T]
                freed(v.tensor_tensor(o2, b(name)[:, :].rearrange("p (a c) -> p a c", c=T)[:, :, 64:T], o2, ALU.add), name)
                emptied(dve, name)

            def head_squares(o):
                v.tensor_tensor(hsq, o, o, ALU.mult).then_inc(hsq_ready, 1)

            def head_apply(o, names, h, col):
                emptied(dve, names[h // 2])
                link(v.reciprocal(hroot[:, h, :], hroot[:, h, :]))
                return v.scalar_tensor_tensor(o[:, h, :], o[:, h, :], col, hroot[:, h, :], ALU.mult, ALU.mult)

            head_squares(og)
            full(dve, "mt_0")
            moba_logits(2)
            full(dve, "mt_1")
            moba_logits(3)
            for h in range(2, 8):
                moba_norm(h)
                if h % 2 == 0:
                    name = f"mo{h // 2 - 1}"
                    full(dve, name)
                    freed(v.tensor_copy(om[:, h // 2 - 1, :], b(name)[:, 0:T]), name)
                if h + 2 < 8:
                    full(dve, f"mt_{h}")
                    moba_logits(h + 2)
                if h < 6:
                    last = head_apply(og, ["gn0", "gn1"], h - 2, gain("g_gla_head", h - 2))
                if h == 5:
                    link(last)
                    emptied(dve, "r0")
                    emptied(dve, "r1")
                    v.tensor_tensor(og, og, rg, ALU.mult).then_inc(og_ready, 1)
                if h < 6:
                    low("zm0" if h < 4 else "zm1", [h % 2])
            full(dve, "mo3")
            freed(v.tensor_copy(om[:, 3, :], b("mo3")[:, 0:T]), "mo3")

            def xg_low(l, j):
                dve.wait_ge(xg_high, 4 * l + j + 1)
                v.tensor_tensor(two(z_parts[1], j), two(hn, j), two(z_parts[0], j).bitcast(F32), ALU.subtract).then_inc(xg_split, 1)

            def z_low(n, j):
                dve.wait_ge(z_high, 4 * n + j + 1)
                v.tensor_tensor(two(z_parts[1], j), two(z1, j), two(z_parts[0], j).bitcast(F32), ALU.subtract).then_inc(z_split, 1)

            def merge(x, n):
                for z, names, c in ((z1, "pa", 2 * n + 1), (z2, "pb", 2 * n + 2)):
                    dve.wait_ge(z_sig, c)
                    for j in range(4):
                        name = f"{names}{j}{x}"
                        full(dve, name)
                        freed(v.tensor_tensor(two(z, j), src_of(name, two(z, j)), two(z, j), ALU.mult), name)
                        if names == "pb":
                            emptied(dve, name)
                            v.tensor_tensor(two(z1, j), two(z1, j), two(z2, j), ALU.add).then_inc(merged_ready, 1)
                            if j == 1:
                                low("out0" + x)
                                z_low(n, 0)
                            if j == 2:
                                z_low(n, 1)
                for j in range(2, 4):
                    z_low(n, j)
                low("out1" + x)
                for j in range(4):
                    residual([f"ou{j}{x}"], j)
                    emptied(dve, f"ou{j}{x}")
                    if not x:
                        gain_apply("g_cross", 0, j)
                    else:
                        gain_apply("norm_ffn_2", 8 * (n - 1), j)
                        if j:
                            hn_low("n_ffn" + x, j - 1)
                        if j == 1:
                            low("ffn0" + x)

            for j in range(4):
                emptied(dve, f"zg{j}")
            merge("", 0)

            emptied(dve, "n_cross")
            link(v.reciprocal(root, root))
            take_scaled("cq0", two(qc, 0), over_tiles(root))
            take_scaled("cq1", two(qc, 1), over_tiles(root))

            def cross_max(h):
                i = 8 + h
                full(dve, f"cs{h}")
                link(v.reduce_max(nm(i, 0, 2), b(f"cs{h}")[:, :].rearrange("p (a c) -> p a c", c=T), AX, negate=True))
                v.tensor_scalar(nm(i, 0, 2), nm(i, 0, 2), P ** -0.5, None, ALU.mult).then_inc(logit_ready, 1)

            def take_co(h):
                full(dve, f"co{h}")
                freed(v.tensor_copy(oc[:, h, :], b(f"co{h}")[:, 0:T]), f"co{h}")

            cross_max(0)
            cross_max(1)
            for h in range(4):
                i = 8 + h
                emptied(dve, f"cs{h}")
                link(v.reciprocal(recs(i, 0, 2), sums(i, 0, 2)))
                for tb in range(TB):
                    last = v.tensor_scalar(cprob[h][:, tb, :], cprob[h][:, tb, :], recs(i, tb), None, ALU.mult)
                last.then_inc(prob_ready, 1)
                if h < 2:
                    cross_max(h + 2)
                else:
                    take_co(h - 2)
            take_co(2)
            take_co(3)
            residual([f"cw{j}" for j in range(4)])
            for j in range(4):
                emptied(dve, f"cw{j}")
            norm_apply("n_moe", xres, hn, "g_moe")

            dve.wait_ge(router_in, 64)
            full(dve, "routeT")
            freed(v.tensor_copy(lgT, b("routeT")[0:36, 0:T]), "routeT")
            full(dve, "route")
            freed(v.tensor_tensor(lg, b("route")[:, 0:72].rearrange("p (a c) -> p a c", c=36),
                                  brow.rearrange("p (a c) -> p a c", a=1).to_broadcast([P, TB, 36]), ALU.add), "route")
            emptied(dve, "route")

            def bc(t, n):
                return t.to_broadcast([P, TB, n])

            def first_of(dst, value, top, n, t):
                link(v.tensor_tensor(t, value, bc(top, n), ALU.is_equal))
                link(v.tensor_scalar(t, t, -100.0, None, ALU.mult))
                link(v.tensor_tensor(t, t, i100[:, 0:n].rearrange("p (a c) -> p a c", a=1).to_broadcast([P, TB, n]), ALU.add))
                link(v.tensor_reduce(rmin, t, AX, ALU.min))
                link(v.tensor_tensor(dst, t, bc(rmin, n), ALU.is_equal))

            lg4 = lg[:, :, 0:4]
            link(v.reduce_max(gm, lg4, AX))
            v.tensor_tensor(d4, lg4, bc(gm, 4), ALU.subtract).then_inc(route_diff, 1)
            first_of(oh4, lg4, gm, 4, t4)
            for tb in range(TB):
                last = v.tensor_tensor(eg[:, tb, :].rearrange("p (g e) -> p g e", g=4),
                                       lg[:, tb, 4:36].rearrange("p (g e) -> p g e", g=4),
                                       oh4[:, tb, :].rearrange("p (g a) -> p g a", a=1).to_broadcast([P, 4, 8]), ALU.mult)
            link(last)
            for tb in range(TB):
                last = v.reduce_sum(ein[:, tb, :], eg[:, tb, :].rearrange("p (g e) -> p e g", g=4), AX)
            link(last)
            link(v.reduce_max(m1, ein, AX))
            first_of(oh1, ein, m1, 8, t8)
            link(v.scalar_tensor_tensor(ein2, oh1, -BIG, ein, ALU.mult, ALU.add))
            link(v.reduce_max(m2, ein2, AX))
            v.tensor_tensor(dm, m2, m1, ALU.subtract).then_inc(route_diff, 1)
            first_of(oh2, ein2, m2, 8, t8)
            dve.wait_ge(route_exp, 2)
            link(v.reduce_sum(pg, e4, AX))
            link(v.tensor_scalar(dm, ex2, 1.0, None, ALU.add))
            link(v.tensor_tensor(pg, pg, dm, ALU.mult))
            link(v.reciprocal(w1, pg))
            link(v.tensor_tensor(w2, w1, ex2, ALU.mult))
            link(v.tensor_tensor(t8, oh1, bc(w1, 8), ALU.mult))
            link(v.tensor_tensor(w8, oh2, bc(w2, 8), ALU.mult))
            link(v.tensor_tensor(w8, w8, t8, ALU.add))
            link(v.tensor_tensor(m8, oh1, oh2, ALU.add))
            for dst, s8, s_done in ((wgt, w8, None), (msk, m8, mask_ready)):
                for tb in range(TB):
                    last = v.tensor_tensor(dst[:, tb, :].rearrange("p (g e) -> p g e", g=4),
                                           oh4[:, tb, :].rearrange("p (g a) -> p g a", a=1).to_broadcast([P, 4, 8]),
                                           s8[:, tb, :].rearrange("p (a e) -> p a e", a=1).to_broadcast([P, 4, 8]), ALU.mult)
                if s_done is not None:
                    last.then_inc(s_done, 1)
            v.memset(SZ[:, 2600:2920], 0.0)
            v.memset(y[:, 0:HALF], 0.0).then_inc(moe_sems[0]["y0_out"], 1)
            v.memset(y[:, HALF:D], 0.0).then_inc(moe_sems[0]["y1_out"], 1)
            v.memset(selT, 0.0).then_inc(blank, 1)
            v.memset(key, 0.0).then_inc(keys_ready, 1)
            dve.wait_ge(keys_ready, 1)
            full(dve, "rank")
            dve.wait_ge(mask_ready, 1)
            v.scalar_tensor_tensor(key[:, :, 0:NE], b("rank")[:, 0:64].rearrange("p (a c) -> p a c", c=NE), 1.0, msk,
                                   ALU.add, ALU.mult)
            link(v.reduce_max(gm[:, 0, :], b("rank")[:, 64:96], AX))
            freed(v.tensor_copy(cnt[:, :], gm[:, 0, :]), "rank")
            emptied(dve, "rank")
            v.tensor_scalar(key, key, -1.0, None, ALU.add).then_inc(count_ready, 1)
            dve.wait_ge(count_ready, 1)

            def select(s, e):
                for tb in range(TB):
                    for j in range(2):
                        v.tensor_scalar(sel[:, tb, 64 * j:64 * j + 64], iota[:, 0:64], key[:, tb, bass.ds(e + j, 1)], None,
                                        ALU.is_equal).then_inc(s["sel_made"], 1)

            def take_gather(s, g):
                dve.wait_ge(s["gather_done"], g + 1)
                v.tensor_copy(xe[:, 0:4, :], ps[2][:, :].rearrange("p (a b) -> p a b", b=P)).then_inc(s["xe_d"], 1)

            def dve_pair(s, n, g, p):
                dve.wait_ge(s["gather_done"], g + 1)
                select(s, 2 * p + 2)
                dve.wait_ge(s["up_done"], n + 1)
                dve.wait_ge(s["silu_made"], n + 1)
                v.tensor_tensor(hid, ps[1][:, :], gsil, ALU.mult).then_inc(s["hid_made"], 1)
                for tb in range(TB):
                    for j in range(2):
                        v.tensor_scalar(selw[:, tb, 64 * j:64 * j + 64], iota[:, 0:64], key[:, tb, bass.ds(2 * p + j, 1)],
                                        wgt[:, tb, bass.ds(2 * p + j, 1)], ALU.is_equal, ALU.mult).then_inc(s["selw_made"], 1)
                take_gather(s, g + 1)
                dve.wait_ge(s["selT_done"], n + 1)
                v.tensor_copy(selT, ps[1][:, 0:T]).then_inc(s["selT_out"], 1)
                dve.wait_ge(s["y1_done"], n + 1)
                v.tensor_copy(y[:, HALF:D], ps[1][:, :]).then_inc(s["y1_out"], 1)

            s = moe_sems[0]
            select(s, 0)
            take_gather(s, 0)
            with dve.Fori(0, PAIRS) as p:
                dve_pair(s, p, p, p)
            most = dve.value_load(cnt[0:1, 0:1], min_val=0, max_val=T)
            with dve.If(most > SLOTS):
                o = moe_sems[1]
                v.memset(sm[:, 1:2], 0.0).then_inc(o["y0_out"], 1)
                v.memset(sm[:, 2:3], 0.0).then_inc(o["y1_out"], 1)
                with dve.Fori(0, OVER_PASSES) as q:
                    dve.wait_ge(passed, q + 1)
                    v.memset(selT, 0.0).then_inc(blank, 1)
                    v.tensor_scalar(iota, iota, float(SLOTS), None, ALU.add).then_inc(iota_moved, 1)
                    dve.wait_ge(iota_moved, q + 1)
                    select(o, 0)
                    take_gather(o, q * (PAIRS + 1))
                    with dve.Fori(0, PAIRS) as p:
                        dve_pair(o, q * PAIRS + p, q * (PAIRS + 1) + p, p)
            for i in range(2):
                take(f"acc{2 + i}", acc_sb[:, 1, HALF * i:HALF * i + HALF])
            residual([f"at{j}" for j in range(4)])
            for j in range(4):
                emptied(dve, f"at{j}")
            norm_apply("n_final", xres, xres, "g_final")
            dve.wait_ge(h_ready, 8 * NORMS.index("n_final") + 8)
            dve.wait_ge(lam_in, 16)
            lp = lamt.rearrange("p (a b) c -> p a b c", b=2)
            link(v.tensor_tensor(lamt[:, 0:8:2, :], lamt[:, 0:8:2, :], lamt[:, 1:8:2, :], ALU.mult))
            v.reduce_sum(lam_s, lamt[:, 0:8:2, :], AX).then_inc(lam_sums, 1)

            for l in range(LAYERS):
                x = f".{l}"
                lam_init = 0.8 - 0.6 * math.exp(-0.3 * l)
                name = "n_attn" + x
                for j in range(4):
                    if l:
                        residual([f"fo{j}.0"], j)
                        emptied(dve, f"fo{j}.0")
                    gain_apply("norm_attn_2", 8 * l, j, xg_ready)
                    if l == 0 and j == 1:
                        low("dq.0", [0])
                    if j:
                        xg_low(l, j - 1)
                xg_low(l, 3)
                if l == 0:
                    low("dq.0", [1])
                emptied(dve, name)
                link(v.reciprocal(root, root))
                for j in range(4):
                    v.tensor_tensor(two(hn, j), two(hn, j), over_tiles(root), ALU.mult).then_inc(h_ready, 2)
                    if j:
                        hn_low(name, j - 1)
                hn_low(name, 3)
                take_scaled("dq0" + x, two(dq, 0), over_tiles(root))
                if l == 0:
                    low("dk.0")
                take_scaled("dq1" + x, two(dq, 1), over_tiles(root))
                low("dv" + x)
                take_scaled("dk0" + x, two(dk, 0), over_tiles(root))
                take_scaled("dk1" + x, two(dk, 1), over_tiles(root))
                if l == 0:
                    dve.wait_ge(lam_exps, 1)
                link(v.tensor_tensor(lam[:, l:l + 1], lam_e[:, 2 * l:2 * l + 1], lam_e[:, 2 * l + 1:2 * l + 2], ALU.subtract))
                link(v.tensor_scalar(lam[:, l:l + 1], lam[:, l:l + 1], lam_init, None, ALU.add))
                link(v.tensor_scalar(subs, gain("diff_subln_2", l), 1.0 - lam_init, None, ALU.mult))
                dve.wait_ge(cb_in, 16)
                for j, (t, name) in enumerate(((dq, "rq0"), (dq, "rq1"), (dk, "rk0"), (dk, "rk1"))):
                    tt = two(t, j % 2)
                    tmp = TMP[:, 512 * (j % 2):512 * (j % 2) + 512].rearrange("p (a b) -> p a b", b=T)
                    full(dve, name + x)
                    freed(v.tensor_tensor(tmp, src_of(name + x, tmp), sinT.rearrange("p (a b) -> p a b", a=1).to_broadcast([P, 2, T]), ALU.mult), name + x)
                    link(v.tensor_tensor(tt, tt, cosT.rearrange("p (a b) -> p a b", a=1).to_broadcast([P, 2, T]), ALU.mult))
                    v.tensor_tensor(tt, tt, tmp, ALU.add).then_inc(rotated, 1)
                low("sq" + x)
                take("dv0" + x, dv[:, 0, :])
                take("dv1" + x, dv[:, 1, :])
                i0 = 12 + 4 * l

                def diff_logits(h):
                    for j, (p, name) in enumerate(((p1[h % 2], f"ds{h}{x}"), (p2[h % 2], f"de{h}{x}"))):
                        full(dve, name)
                        freed(v.scalar_tensor_tensor(p, b(name)[:, 0:384], 64 ** -0.5, causal, ALU.mult, ALU.add), name)
                        emptied(dve, name)
                        last = maxima(i0 + h, 2 * j, p)
                    last.then_inc(logit_ready, 1)

                def diff_norm(h):
                    i = i0 + h
                    dve.wait_ge(exp_ready, i - 4 + 1)
                    link(v.reciprocal(recs(i, 0, 4), sums(i, 0, 4)))
                    link(v.tensor_scalar(recs(i, 2, 2), recs(i, 2, 2), lam[:, l:l + 1], None, ALU.mult))
                    for j, (at, to) in enumerate(((0, P), (P, 384))):
                        last = v.tensor_scalar(p2[h % 2][:, at:to], p2[h % 2][:, at:to], recs(i, 2 + j), None, ALU.mult)
                    link(last)
                    for j, (at, to) in enumerate(((0, P), (P, 384))):
                        last = v.scalar_tensor_tensor(p1[h % 2][:, at:to], p1[h % 2][:, at:to], recs(i, j), p2[h % 2][:, at:to],
                                                      ALU.mult, ALU.subtract)
                    last.then_inc(prob_ready, 1)

                def take_do(h):
                    full(dve, f"do{h}{x}")
                    freed(v.tensor_copy(od[:, h, :], b(f"do{h}{x}")[:, 0:T]), f"do{h}{x}")

                def diagonals(t):
                    return t.rearrange("p (a c) -> p a c", c=P)[:, 0:3:2, :]

                def sb_logs_of(h):
                    name = f"bz{h}{x}"
                    dve.wait_ge(sb_logs, 8 * l + h + 1)
                    lb, lr = lbeta[h % 2], lrem[h % 2]
                    link(v.tensor_scalar(lb, b(name)[:, 0:384], 64 ** -0.5, 0.0, ALU.mult, ALU.min))
                    link(v.tensor_tensor(lb, lb, stick[h % 4], ALU.subtract))
                    freed(v.scalar_tensor_tensor(lr, b(name)[:, 0:384], -(64 ** -0.5), lb, ALU.mult, ALU.add), name)
                    emptied(dve, name)
                    v.tensor_tensor(diagonals(lr), diagonals(lr), diagonals(strict), ALU.mult).then_inc(sb_rem, 1)

                def sb_add(h):
                    name = f"ba{h}{x}"
                    full(dve, name)
                    freed(v.tensor_tensor(lbeta[h % 2], b(name)[:, 0:384], lbeta[h % 2], ALU.add), name)

                def sb_mask(h):
                    dve.wait_ge(sb_exp, 8 * l + h + 1)
                    v.tensor_tensor(diagonals(stick[h % 4]), diagonals(stick[h % 4]), diagonals(strict), ALU.mult).then_inc(sb_prob, 1)

                diff_logits(0)
                diff_norm(0)
                low("sk" + x)
                diff_logits(1)
                diff_norm(1)
                low("sv" + x)
                take_do(0)
                full(dve, "dt0" + x)
                diff_logits(2)
                diff_norm(2)
                low("ga0" + x)
                take("sv0" + x, bv[:, 0, :])
                take("sv1" + x, bv[:, 1, :])
                take_do(1)
                full(dve, "dt1" + x)
                diff_logits(3)
                diff_norm(3)
                sb_logs_of(0)
                take_do(2)
                low("ga1" + x, [0])
                sb_logs_of(1)
                sb_add(0)
                sb_mask(0)
                low("ga1" + x, [1])
                take_do(3)
                emptied(dve, "do3" + x)
                head_squares(od)
                for h in range(8):
                    if h < 7:
                        sb_add(h + 1)
                        sb_mask(h + 1)
                    if h in (0, 2, 4):
                        sb_logs_of(h + 2)
                        sb_logs_of(h + 3)
                    if h < 2:
                        low("gb0" + x, [h])
                    if h >= 4:
                        last = head_apply(od, ["dn0" + x, "dn1" + x], h - 4, subs)
                    if h == 7:
                        last.then_inc(og_ready, 1)
                    if h in (2, 3):
                        low("gb1" + x, [h - 2])
                    if h % 2 == 1:
                        name = f"bo{h // 2}{x}"
                        full(dve, name)
                        freed(v.tensor_copy(ob[:, h // 2, :], b(name)[:, 0:T]), name)
                merge(x, l + 1)
                hn_low("n_ffn" + x, 3)
                emptied(dve, "n_ffn" + x)
                link(v.reciprocal(ffn_root, ffn_root))
                low("ffn1" + x)
                by_root = over_tiles(ffn_root)
                for j in range(11):
                    take_scaled(f"fg{j}{x}", hid_raw[j % 3], by_root)
                    dve.wait_ge(hid_silu, 11 * l + j + 1)
                    take_scaled(f"fu{j}{x}", hid_raw[j % 3], hid_raw[j % 3])
                    emptied(dve, f"fu{j}{x}")
                    v.tensor_tensor(hid_raw[j % 3], hid_raw[j % 3], by_root, ALU.mult).then_inc(hid_scaled, 1)
                    dve.wait_ge(hid_high, 11 * l + j + 1)
                    v.tensor_tensor(two(hid_parts[1], j), hid_raw[j % 3], two(hid_parts[0], j).bitcast(F32), ALU.subtract).then_inc(hid_split, 1)
                    low(SPLIT[SPLIT.index(f"ffn{j}{x}") + 2])
                for c in range(5 if l + 1 < LAYERS else 3):
                    low(SPLIT[SPLIT.index(f"down{c}{x}") + 2])
            residual([f"fo{j}.{LAYERS - 1}" for j in range(4)])
            for j in range(4):
                emptied(dve, f"fo{j}.{LAYERS - 1}")
            norm_apply("n_last", xres, hn, "norm_final_2")
            for j in range(2, 4):
                take(f"yt{j}", y_out[:, 1, HALF * (j % 2):HALF * (j % 2) + HALF])


_INS = ["x", "mem", "g_mem", "rel_bias", "g_mix", "w_in", "w_alpha_up", "b_alpha", "g_gla_head", "w_proj_gla",
        "w_proj_moba", "w_out", "g_cross", "w_cq", "w_ckv", "w_co", "g_moe", "w_router_group", "b_router_group",
        "w_router_expert", "b_router_expert", "w_exp_gate", "w_exp_up", "w_exp_down", "g_final", "norm_attn_2",
        "w_in_2", "b_gate_2", "diff_lambda_2", "diff_subln_2", "w_o_diff_2", "w_o_sb_2", "w_out_2", "norm_ffn_2",
        "w_ffn_in_2", "w_ffn_out_2", "norm_final_2"]


def kernel(**inputs):
    import concourse.bacc as bacc
    from concourse.bass_utils import run_bass_kernel_spmd

    nc = bacc.Bacc("TRN2", target_bir_lowering=False, num_devices=1)
    arrays, aps = {}, {}
    data = {n: np.ascontiguousarray(inputs[n]) for n in _INS}
    data["gains"] = np.concatenate([data.pop(n).reshape(-1, P) for n in ROWS])
    data["consts"] = constants()
    for n, v in data.items():
        arrays[f"in_{n}"] = v
        aps[n] = nc.dram_tensor(f"in_{n}", v.shape, mybir.dt.from_np(v.dtype), kind="ExternalInput").ap()
    out = nc.dram_tensor("out_0", (1, T, D), F32, kind="ExternalOutput").ap()
    build(nc, aps, out)
    r = run_bass_kernel_spmd(nc, [arrays], core_ids=[0])
    return r.results[0]["out_0"]
```
